# Optimizing a Trainium2 kernel written in Bass

```python
import math
import jax, jax.numpy as jnp
from jax import lax
import numpy as np

D_MODEL = 1024
BATCH = 1
SEQ = 256
DEPTH = 2

BLOCK_Q = 128
N_BRANCHES = 4
BRANCH_WIDTH = 256
A_HEADS = 4
A_DIM = 64
IDX_HEADS = 4
IDX_DIM = 64
TOPK_MAX = 256
MLA_HEADS = 4
MLA_Q_RANK = 256
MLA_KV_RANK = 128
MLA_NOPE = 64
MLA_ROPE = 32
MLA_V = 64
ROPE_THETA = 10000.0
SB_HEADS = 4
SB_DIM = 64
DIFF_HEADS = 4
DIFF_QK = 32
DIFF_V = 2 * DIFF_QK
N_ALIBI_HEADS = A_HEADS + DIFF_HEADS
D_FF = 2816
N_EXPERTS = 8
TOP_K = 2
D_FF_EXPERT = 3584
EPS = 1e-6

IN_SIZES = (
    A_HEADS * A_DIM, A_DIM, A_DIM,
    IDX_HEADS * IDX_DIM, IDX_DIM, IDX_HEADS,
    MLA_Q_RANK, MLA_KV_RANK, MLA_ROPE,
    SB_HEADS * SB_DIM, SB_HEADS * SB_DIM, SB_HEADS * SB_DIM,
    DIFF_HEADS * 2 * DIFF_QK, DIFF_HEADS * 2 * DIFF_QK, DIFF_HEADS * DIFF_V,
    N_BRANCHES * D_MODEL,
)
IN_COLS = sum(IN_SIZES)

kernel_name = 'hybrid_dsa_mla_stickbreak_diff_moe_block'

f32 = jnp.float32

def _rmsnorm(x, g):
    xf = x.astype(f32)
    y = xf * lax.rsqrt(jnp.mean(xf * xf, axis=-1, keepdims=True) + EPS)
    return (y * g.astype(f32)).astype(x.dtype)

def _split_cols(p):
    out, off = [], 0
    for n in IN_SIZES:
        out.append(p[..., off:off + n])
        off += n
    return out

def _qslice(a, i):
    return lax.dynamic_slice_in_dim(a, i * BLOCK_Q, BLOCK_Q, axis=1)

def _blocks(fn, seq):
    ys = lax.map(fn, jnp.arange(seq // BLOCK_Q))
    nb, b, bq = ys.shape[:3]
    return jnp.moveaxis(ys, 0, 1).reshape((b, nb * bq) + ys.shape[3:])

def _alibi_slopes():
    n = N_ALIBI_HEADS
    sl = 2.0 ** (-(8.0 / n) * jnp.arange(1, n + 1, dtype=f32))
    return sl[0::2], sl[1::2]

def _rope_angles(positions):
    half = MLA_ROPE // 2
    inv = ROPE_THETA ** (-jnp.arange(half, dtype=f32) / half)
    ang = positions.astype(f32)[..., None] * inv
    return jnp.cos(ang), jnp.sin(ang)

def _rope(x, cos, sin):
    xf = x.astype(f32)
    half = xf.shape[-1] // 2
    x1, x2 = xf[..., :half], xf[..., half:]
    return jnp.concatenate([x1 * cos - x2 * sin, x1 * sin + x2 * cos], axis=-1).astype(x.dtype)

def _dsa(q, k, v, iq, ik, iw, slopes):
    b, s = q.shape[:2]
    topk = min(TOPK_MAX, s // 4)
    keys = jnp.arange(s)
    w = iw.astype(f32) * (IDX_HEADS ** -0.5)

    def block(i):
        t = i * BLOCK_Q + jnp.arange(BLOCK_Q)
        rel = jax.nn.relu(jnp.einsum('bqhd,bkd->bqhk', _qslice(iq, i), ik, preferred_element_type=f32) * (IDX_DIM ** -0.5))
        score = jnp.einsum('bqhk,bqh->bqk', rel, _qslice(w, i))
        score = jnp.where(keys[None, None, :] <= t[None, :, None], score, -jnp.inf)
        _, sel = lax.top_k(score, topk)
        ksel = jax.vmap(lambda kb, ib: kb[ib])(k, sel)
        vsel = jax.vmap(lambda vb, ib: vb[ib])(v, sel)
        dist = t[None, :, None] - sel
        lg = jnp.einsum('bqhd,bqkd->bqhk', _qslice(q, i), ksel, preferred_element_type=f32) * (A_DIM ** -0.5)
        lg = lg - slopes[None, None, :, None] * dist[:, :, None, :].astype(f32)
        lg = jnp.where((dist >= 0)[:, :, None, :], lg, -jnp.inf)
        p = jax.nn.softmax(lg, axis=-1).astype(v.dtype)
        return jnp.einsum('bqhk,bqkd->bqhd', p, vsel)

    return _blocks(block, s)

def _mla(cq, ckv, kr, q_norm_g, kv_norm_g, w_uq, w_ukv, positions):
    b, s = cq.shape[:2]
    qf = (_rmsnorm(cq, q_norm_g) @ w_uq).reshape(b, s, MLA_HEADS, MLA_NOPE + MLA_ROPE)
    kv = (_rmsnorm(ckv, kv_norm_g) @ w_ukv).reshape(b, s, MLA_HEADS, MLA_NOPE + MLA_V)
    q_nope, k_nope, v = qf[..., :MLA_NOPE], kv[..., :MLA_NOPE], kv[..., MLA_NOPE:]
    cos, sin = _rope_angles(positions)
    q_rope = _rope(qf[..., MLA_NOPE:], cos[:, :, None, :], sin[:, :, None, :])
    k_rope = _rope(kr, cos, sin)
    scale = (MLA_NOPE + MLA_ROPE) ** -0.5
    keys = jnp.arange(s)

    def block(i):
        t = i * BLOCK_Q + jnp.arange(BLOCK_Q)
        lg = (jnp.einsum('bqhd,bkhd->bhqk', _qslice(q_nope, i), k_nope, preferred_element_type=f32)
              + jnp.einsum('bqhd,bkd->bhqk', _qslice(q_rope, i), k_rope, preferred_element_type=f32)) * scale
        lg = jnp.where(keys[None, :] <= t[:, None], lg, -jnp.inf)
        p = jax.nn.softmax(lg, axis=-1).astype(v.dtype)
        return jnp.einsum('bhqk,bkhd->bqhd', p, v)

    return _blocks(block, s)

def _stick_breaking(q, k, v):
    b, s = q.shape[:2]
    keys = jnp.arange(s)

    def block(i):
        t = i * BLOCK_Q + jnp.arange(BLOCK_Q)
        z = jnp.einsum('bqhd,bkhd->bhqk', _qslice(q, i), k, preferred_element_type=f32) * (SB_DIM ** -0.5)
        strict = keys[None, :] < t[:, None]
        log_1m = jnp.where(strict, jax.nn.log_sigmoid(-z), 0.0)
        between = lax.cumsum(log_1m, axis=3, reverse=True) - log_1m
        a = jnp.where(strict, jnp.exp(jax.nn.log_sigmoid(z) + between), 0.0).astype(v.dtype)
        return jnp.einsum('bhqk,bkhd->bqhd', a, v)

    return _blocks(block, s)

def _diff_attn(q, k, v, lq1, lk1, lq2, lk2, norm_g, slopes, lam_init):
    b, s = q.shape[:2]
    lam = (jnp.exp(jnp.sum(lq1.astype(f32) * lk1.astype(f32)))
           - jnp.exp(jnp.sum(lq2.astype(f32) * lk2.astype(f32))) + lam_init)
    keys = jnp.arange(s)

    def block(i):
        t = i * BLOCK_Q + jnp.arange(BLOCK_Q)
        lg = jnp.einsum('bqhmd,bkhmd->bhmqk', _qslice(q, i), k, preferred_element_type=f32) * (DIFF_QK ** -0.5)
        dist = (t[:, None] - keys[None, :]).astype(f32)
        lg = lg - slopes[None, :, None, None, None] * dist
        lg = jnp.where(keys[None, :] <= t[:, None], lg, -jnp.inf)
        p = jax.nn.softmax(lg, axis=-1)
        attn = (p[:, :, 0] - lam * p[:, :, 1]).astype(v.dtype)
        return jnp.einsum('bhqk,bkhd->bqhd', attn, v)

    o = _blocks(block, s)
    return _rmsnorm(o, norm_g) * (1.0 - lam_init)

def _hybrid_mixer(h, positions, w_in, q_norm_g, kv_norm_g, w_uq, w_ukv,
                  lq1, lk1, lq2, lk2, diff_norm_g, w_branch, w_out, lam_init):
    b, s, _ = h.shape
    (aq, ak, av, iq, ik, iw, cq, ckv, kr, sq, sk, sv, dq, dk, dv, gates) = _split_cols(h @ w_in)
    slopes_a, slopes_d = _alibi_slopes()
    ya = _dsa(aq.reshape(b, s, A_HEADS, A_DIM), ak, av,
              iq.reshape(b, s, IDX_HEADS, IDX_DIM), ik, iw, slopes_a)
    yb = _mla(cq, ckv, kr, q_norm_g, kv_norm_g, w_uq, w_ukv, positions)
    yc = _stick_breaking(sq.reshape(b, s, SB_HEADS, SB_DIM), sk.reshape(b, s, SB_HEADS, SB_DIM),
                         sv.reshape(b, s, SB_HEADS, SB_DIM))
    yd = _diff_attn(dq.reshape(b, s, DIFF_HEADS, 2, DIFF_QK), dk.reshape(b, s, DIFF_HEADS, 2, DIFF_QK),
                    dv.reshape(b, s, DIFF_HEADS, DIFF_V), lq1, lk1, lq2, lk2, diff_norm_g, slopes_d, lam_init)
    g = jax.nn.sigmoid(gates.astype(f32)).astype(h.dtype).reshape(b, s, N_BRANCHES, D_MODEL)
    merged = jnp.zeros_like(h)
    for n, y in enumerate((ya, yb, yc, yd)):
        merged = merged + g[:, :, n] * (y.reshape(b, s, BRANCH_WIDTH) @ w_branch[n])
    return merged @ w_out

def _swiglu(h, w1, w3, w2):
    return (jax.nn.silu(h @ w1) * (h @ w3)) @ w2

def _moe(h, router_w, router_b, w1, w3, w2):
    b, s, d = h.shape
    tok = h.reshape(b * s, d)
    logits = (tok @ router_w).astype(f32) + router_b.astype(f32)
    top_val, top_idx = lax.top_k(logits, TOP_K)
    top_w = jax.nn.softmax(top_val, axis=-1)
    combine = jnp.sum(jax.nn.one_hot(top_idx, N_EXPERTS, dtype=f32) * top_w[..., None], axis=1).astype(h.dtype)
    out = jnp.zeros_like(tok)
    for e in range(N_EXPERTS):
        out = out + combine[:, e:e + 1] * _swiglu(tok, w1[e], w3[e], w2[e])
    return out.reshape(b, s, d)

def setup_inputs(seed: int = 0) -> dict:
    key = jax.random.key(seed)
    ks = iter(jax.random.split(key, 32))

    def nrm(shape, scale):
        return jax.random.normal(next(ks), shape, f32) * scale

    def gain(shape):
        return 1.0 + nrm(shape, 0.02)

    L, D = DEPTH, D_MODEL
    nd, nm = (DEPTH + 1) // 2, DEPTH // 2
    return {
        'x': nrm((BATCH, SEQ, D), 1.0),
        'c': nrm((BATCH, D), 1.0),
        'positions': jax.random.randint(next(ks), (BATCH, 1), 0, SEQ, dtype=jnp.int32) + jnp.arange(SEQ, dtype=jnp.int32)[None, :],
        'ada_w': nrm((L, D, 6 * D), 0.5 * D ** -0.5),
        'ada_b': nrm((L, 6 * D), 0.02),
        'norm1_g': gain((L, D)),
        'norm2_g': gain((L, D)),
        'w_in': nrm((L, D, IN_COLS), D ** -0.5),
        'mla_q_norm_g': gain((L, MLA_Q_RANK)),
        'mla_kv_norm_g': gain((L, MLA_KV_RANK)),
        'mla_w_uq': nrm((L, MLA_Q_RANK, MLA_HEADS * (MLA_NOPE + MLA_ROPE)), MLA_Q_RANK ** -0.5),
        'mla_w_ukv': nrm((L, MLA_KV_RANK, MLA_HEADS * (MLA_NOPE + MLA_V)), MLA_KV_RANK ** -0.5),
        'diff_lq1': nrm((L, DIFF_QK), 0.1),
        'diff_lk1': nrm((L, DIFF_QK), 0.1),
        'diff_lq2': nrm((L, DIFF_QK), 0.1),
        'diff_lk2': nrm((L, DIFF_QK), 0.1),
        'diff_norm_g': gain((L, DIFF_V)),
        'w_branch': nrm((L, N_BRANCHES, BRANCH_WIDTH, D), BRANCH_WIDTH ** -0.5),
        'w_out': nrm((L, D, D), D ** -0.5),
        'ffn_w1': nrm((nd, D, D_FF), D ** -0.5),
        'ffn_w3': nrm((nd, D, D_FF), D ** -0.5),
        'ffn_w2': nrm((nd, D_FF, D), D_FF ** -0.5),
        'router_w': nrm((nm, D, N_EXPERTS), D ** -0.5),
        'router_b': nrm((nm, N_EXPERTS), 0.01),
        'moe_w1': nrm((nm, N_EXPERTS, D, D_FF_EXPERT), D ** -0.5),
        'moe_w3': nrm((nm, N_EXPERTS, D, D_FF_EXPERT), D ** -0.5),
        'moe_w2': nrm((nm, N_EXPERTS, D_FF_EXPERT, D), D_FF_EXPERT ** -0.5),
        'final_norm_g': gain((D,)),
    }

def reference(x, c, positions, ada_w, ada_b, norm1_g, norm2_g, w_in, mla_q_norm_g, mla_kv_norm_g,
              mla_w_uq, mla_w_ukv, diff_lq1, diff_lk1, diff_lq2, diff_lk2, diff_norm_g, w_branch, w_out,
              ffn_w1, ffn_w3, ffn_w2, router_w, router_b, moe_w1, moe_w3, moe_w2, final_norm_g):
    cond = jax.nn.silu(c)
    for l in range(DEPTH):
        mod = (cond @ ada_w[l] + ada_b[l])[:, None, :]
        sh1, sc1, g1, sh2, sc2, g2 = jnp.split(mod, 6, axis=-1)
        lam_init = 0.8 - 0.6 * math.exp(-0.3 * l)
        h = _rmsnorm(x, norm1_g[l]) * (1.0 + sc1) + sh1
        x = x + g1 * _hybrid_mixer(h, positions, w_in[l], mla_q_norm_g[l], mla_kv_norm_g[l], mla_w_uq[l],
                                   mla_w_ukv[l], diff_lq1[l], diff_lk1[l], diff_lq2[l], diff_lk2[l],
                                   diff_norm_g[l], w_branch[l], w_out[l], lam_init)
        h = _rmsnorm(x, norm2_g[l]) * (1.0 + sc2) + sh2
        if l % 2 == 0:
            f = _swiglu(h, ffn_w1[l // 2], ffn_w3[l // 2], ffn_w2[l // 2])
        else:
            f = _moe(h, router_w[l // 2], router_b[l // 2], moe_w1[l // 2], moe_w3[l // 2], moe_w2[l // 2])
        x = x + g2 * f
    return _rmsnorm(x, final_norm_g)


_drawn_inputs = setup_inputs


def setup_inputs(seed=0):
    import zlib

    import numpy as np

    out = dict(_drawn_inputs(seed))
    spreads = {}
    factors = {'norm2_g': 3.413,
     'mla_q_norm_g': 8.0,
     'mla_kv_norm_g': 6.727,
     'diff_lq1': 3.845,
     'diff_lk1': 2.756,
     'diff_lq2': 7.334,
     'diff_lk2': 3.299,
     'diff_norm_g': 4.951,
     'router_b': 11.997,
     'final_norm_g': 9.801}
    for name, (base, spread) in spreads.items():
        noise = np.random.default_rng([zlib.crc32(name.encode()), seed]).standard_normal(out[name].shape)
        drawn = base * np.exp(spread * noise) if base else spread * noise
        out[name] = __import__('jax').numpy.asarray(drawn.astype(out[name].dtype))
    for name, factor in factors.items():
        out[name] = (out[name] * factor).astype(out[name].dtype)
    return out
```

```python
import math
from contextlib import ExitStack

import concourse.bass as bass
from concourse import mybir
from concourse.alu_op_type import AluOpType as ALU

P = 128
D = 1024
KB = D // P
SEQ = 256
TB = SEQ // P
L = 2
COLS = 256
HEADS = 4
EXPERTS = 8
TOPK = 64
D_FF = 2816
FFE = 3584
FG = D_FF // COLS
EG = FFE // COLS
EPS = 1e-6
NEG = -1e30
TAKEN = -3e38

NAMES = ("aq", "ak", "av", "iq", "ik", "iw", "cq", "ckv", "kr", "sq", "sk", "sv", "dq", "dk", "dv", "gates")
SIZES = (256, 64, 64, 256, 64, 4, 256, 128, 32, 256, 256, 256, 256, 256, 256, 4096)
COL = {n: sum(SIZES[:i]) for i, n in enumerate(NAMES)}

CONST = {}
_at = 0
for _n, _w in (("ident", 128), ("ntri", 128), ("nones", 128), ("ones", 128), ("blk", 128), ("strict", 128),
               ("iota", 128), ("dist", 256), ("causal", 256), ("rot", 32), ("inv", 1), ("eps", 1),
               ("half_pi", 1)):
    CONST[_n] = (_at, _at + _w)
    _at += _w
NCONST = _at

ROW = {"ada_b": 0, "norm1": 48, "norm2": 56, "qn": 64, "kvn": 66, "c": 67, "final": 75, "diff": 83,
       "lq1": 84, "lk1": 85, "lq2": 86, "lk2": 87, "one_minus_lam": 88, "lam_init": 89}
NROW = 90

ATT = [("C", h) for h in range(4)] + [("B", i) for i in range(3)] + [("D", i) for i in range(6)] \
    + [("A", i) for i in range(3)]
NATT = len(ATT)
NSM = NATT - 4
BRANCH_ORDER = ("C", "B", "D", "A")
BRANCH_N = {"A": 0, "B": 1, "C": 2, "D": 3}


def head_cols(unit):
    b, i = unit
    if b == "D":
        return (0, 128, range(4 * i, 4 * i + 4)) if i < 2 else (128, 256, range(2 * (i - 2), 2 * (i - 2) + 2))
    return (0, 128, (0, 2, 1, 3)) if i == 0 else (128, 256, (i - 1, i + 1))


PRE = ["params", "stats1", "lam", "ada_a", "iq", "ik", "cq", "ckv", "@I0", "sq", "@I1", "sk", "@I2", "mla_stats"]
FILL = {0: ["sv", "uq01"], 1: ["uq23", "uk01", "uk23", "dq"], 2: ["rot01", "rot23", "rotk", "uv", "dk"],
        3: ["dv", "aq"], 4: ["ak", "gate0", "adar0"]}
_g = 1
for _t in range(5, NATT + 2):
    FILL[_t] = [f"gate{_g}"]
    _g += 1
    if _t in (7, 15):
        FILL[_t].append(f"gate{_g}")
        _g += 1
    if _t in (8, 12, 16):
        FILL[_t].append(f"adar{_t // 4 - 1}")
assert _g == 16
FILL[NATT].append("dstats")
POST = [f"wb{n}_{q}" for n in BRANCH_ORDER for q in range(4)] + [f"wo{i}" for i in range(4)] + ["stats2"]
UNITS = [u for u in PRE if u[0] != "@"] + [u for t in sorted(FILL) for u in FILL[t]]
UNITS += POST
assert len(set(UNITS)) == len(UNITS)

ADA_AFTER = {"sq": 8, "sk": 9, "sv": 10, "dk": 11, "gate0": 12, "gate1": 13, "gate2": 14, "gate3": 15,
             "gate5": 16, "gate6": 17, "gate7": 18, "gate8": 19, "gate9": 20, "gate10": 21, "gate11": 22,
             "gate12": 23}
ADA_NEXT = {f"w2_{i}": i for i in range(8)}
ADA_ORDER = list(range(8, 24)) + list(range(8))
ADA_HALVES = 2 * len(ADA_ORDER)


def chunks_of(unit):
    if unit[:2] == "wb":
        return [unit[:3]] if unit[-1] == "0" else []
    plain = ("iq", "ik", "cq", "ckv", "sq", "sk", "sv", "dq", "dk", "dv", "aq", "ak")
    return [unit] if unit in plain or unit[:4] == "gate" or unit[:2] == "wo" else []


MIX_CHUNKS = [c for u in UNITS for c in chunks_of(u)]
FFN_CHUNKS = ["w1_0", "w3_0"]
for _i in range(1, FG):
    FFN_CHUNKS += [f"w1_{_i}", f"w3_{_i}", f"w2_{_i - 1}"]
FFN_CHUNKS.append(f"w2_{FG - 1}")
CHUNKS = MIX_CHUNKS + FFN_CHUNKS
NMIX = len(MIX_CHUNKS)
SPLITS = CHUNKS
RAW = 3
HALVES = 4


def last_of_unit(unit):
    if unit[:2] == "wb":
        return unit[:3] if unit[-1] == "3" else None
    c = chunks_of(unit)
    return c[-1] if c else None


SIGNALLED = [u for u in UNITS if last_of_unit(u) is None]
SC_UNITS = ["I0", "I1", "I2"] + [f"{b}{i}" for b, i in ATT]


def n_of(items, ring, at):
    return len(range(at, items, ring))


def trunk(nc, a, out):
    f32, f32r, i32, u32 = mybir.dt.float32, mybir.dt.float32r, mybir.dt.int32, mybir.dt.uint32
    ACT = mybir.ActivationFunctionType
    AX = mybir.AxisListType

    ctx = ExitStack()
    mix = ExitStack()
    with ctx:
        def sem(name):
            return ctx.enter_context(nc.semaphore(name))

        def sb(name, shape, dt=f32, at=ctx):
            return at.enter_context(nc.sbuf_tensor(name, shape, dt))

        const = sb("const", [P, NCONST])
        C = {n: const[:, lo:hi] for n, (lo, hi) in CONST.items()}
        xT = sb("xT", [P, KB, SEQ])
        htmp = sb("htmp", [P, KB, SEQ])
        hh = sb("hh", [P, KB, SEQ], f32r)
        hl = sb("hl", [P, KB, SEQ], f32r)
        raw = sb("raw", [P, RAW, 2048])
        rows = sb("rows", [P, P])
        pv = sb("pv", [P, NROW])
        adav = sb("adav", [P, 48])
        cond = sb("cond", [P, KB])
        hscale = sb("hscale", [P, KB])
        rstd = sb("rstd", [P, SEQ])
        router_w = sb("router_w", [P, KB, EXPERTS])
        router_b = sb("router_b", [1, EXPERTS])
        npass_i = sb("npass_i", [1, 1], i32)

        def mx(name, shape, dt=f32):
            return sb(name, shape, dt, mix)

        shi = mx("shi", [P, HALVES, 1024], f32r)
        slo = mx("slo", [P, HALVES, 1024], f32r)
        gates = mx("gates", [P, 32, SEQ])
        iqT = mx("iqT", [P, 2, SEQ])
        ikT = mx("ikT", [P, SEQ])
        iw = mx("iw", [P, TB, HEADS])
        aqT = mx("aqT", [P, 2, SEQ])
        akT = mx("akT", [P, SEQ])
        avt = mx("avt", [P, TB, 64])
        cqT = mx("cqT", [P, 2, SEQ])
        ckvT = mx("ckvT", [P, SEQ])
        krT = mx("krT", [P, SEQ])
        krr = mx("krr", [P, SEQ])
        sqT = mx("sqT", [P, 2, SEQ])
        skT = mx("skT", [P, 2, SEQ])
        svt = mx("svt", [P, TB, 256])
        dvt = mx("dvt", [P, TB, 256])
        mqT = mx("mqT", [96, HEADS, SEQ])
        mkT = mx("mkT", [96, HEADS, SEQ])
        mvt = mx("mvt", [P, TB, 256])
        uq = mx("uq", [P, 2, 384])
        ukv = mx("ukv", [P, 512])
        ada_raw = mx("ada_raw", [P, 2, 4, COLS])
        ada_sum = htmp[:, 0:4, :]
        ada_first = gates[:, 0:8, :]
        yh = mx("yh", [P, 4, 512], f32r)
        yl = mx("yl", [P, 4, 512], f32r)
        prob = mx("prob", [P, 2, 512])
        diag = mx("diag", [P, 2, 512])
        pT = mx("pT", [P, 2, 512])
        score = mx("score", [P, 384])
        work = mx("work", [P, 384])
        cosT = mx("cosT", [P, SEQ])
        sinT = mx("sinT", [P, SEQ])
        tmpA = mx("tmpA", [P, 512])
        small = mx("small", [P, 64])
        dqT, dkT = iqT, cqT
        gh, gl = yh, yl

        ps = [ctx.enter_context(nc.psum_tensor(f"ps{i}", [P, 512], f32)) for i in range(8)]
        SCB, TPB, YB = 2, 4, 6

        start_loaded = sem("start_loaded")
        rows_cleared = sem("rows_cleared")
        rows_loaded = sem("rows_loaded")
        small_w_loaded = sem("small_w_loaded")
        x_turned = sem("x_turned")
        x_kept = sem("x_kept")
        rope_arg = sem("rope_arg")
        rope_ready = sem("rope_ready")
        raw_full = [sem(f"raw_full{i}") for i in range(RAW)]
        first_full = [sem(f"first_full{i}") for i in range(RAW)]
        first_summed = sem("first_summed")
        ada_full = [sem(f"ada_full{i}") for i in range(2)]
        ada_summed = sem("ada_summed")
        hi_done = sem("hi_done")
        split_full = [sem(f"split_full{i}") for i in range(HALVES)]
        split_used = [sem(f"split_used{i}") for i in range(HALVES)]
        acc_full = sem("acc_full")
        acc_free = [sem(f"acc_free{i}") for i in range(2)]
        sc_full = sem("sc_full")
        sc_free = [sem(f"sc_free{i}") for i in range(2)]
        squares = sem("squares")
        params_ready = sem("params_ready")
        cond_ready = sem("cond_ready")
        lamprod_ready = sem("lamprod_ready")
        h_ready = sem("h_ready")
        h_high = sem("h_high")
        h_split = sem("h_split")
        q_roped = sem("q_roped")
        k_roped = sem("k_roped")
        lat_squares = sem("lat_squares")
        lat_normed = sem("lat_normed")
        relu_used = sem("relu_used")
        z_log = sem("z_log")
        z_soft = sem("z_soft")
        z_masked = sem("z_masked")
        z_summed = sem("z_summed")
        w_masked = sem("w_masked")
        max_ready = sem("max_ready")
        exp_ready = sem("exp_ready")
        diag_ready = sem("diag_ready")
        turned = sem("turned")
        turned_kept = sem("turned_kept")
        values_done = sem("values_done")
        y_squared = sem("y_squared")
        y_float = sem("y_float")
        y_high = sem("y_high")
        y_split = sem("y_split")
        gates_ready = sem("gates_ready")
        part_used = sem("part_used")
        merged = sem("merged")
        m_high = sem("m_high")
        m_split = sem("m_split")
        up_free = [sem(f"up_free{i}") for i in range(4)]
        glu_high = sem("glu_high")
        glu_split = sem("glu_split")
        x_fed = sem("x_fed")
        vec_order = sem("vec_order")
        first_order = sem("first_order")
        pe_order = sem("pe_order")
        act_order = sem("act_order")
        pool_order = sem("pool_order")
        mixer_over = sem("mixer_over")

        passed = sem("passed")

        def carry(eng):
            eng.sem_inc(passed, 1)

        def dmas(c):
            return {"ak": 2, "ik": 2}.get(c, 1)

        def raw_place(c):
            i = CHUNKS.index(c)
            mine = [x for x in CHUNKS[i % RAW::RAW]]
            return i % RAW, 16 * sum(dmas(x) for x in mine[:i // RAW + 1]), 16 * sum(dmas(x) for x in mine)

        def half_place(c, half):
            h = 2 * SPLITS.index(c) + half
            return h % HALVES, h // HALVES, n_of(2 * len(SPLITS), HALVES, h % HALVES)

        def width(c):
            return {"ik": 132, "ak": 192, "ckv": 192}.get(c, COLS)

        def wait_unit(eng, unit, l):
            c = last_of_unit(unit)
            if c is None:
                eng.wait_ge(acc_full, l * len(SIGNALLED) + SIGNALLED.index(unit) + 1)
            else:
                u, before, total = half_place(c, 1)
                eng.wait_ge(split_used[u], l * total + before + 1)

        def bank_of(unit):
            i = UNITS.index(unit)
            return i % 2, i // 2, n_of(len(UNITS), 2, i % 2)

        def wait_acc_free(eng, unit, l):
            b, before, total = bank_of(unit)
            eng.wait_ge(acc_free[b], l * total + before)
            return ps[b]

        def wait_drained(eng, unit, l):
            b, before, total = bank_of(unit)
            eng.wait_ge(acc_free[b], l * total + before + 1)

        def wait_all_drained(eng, units, l):
            for bank in range(2):
                mine = [u for u in units if bank_of(u)[0] == bank]
                if mine:
                    wait_drained(eng, max(mine, key=UNITS.index), l)

        def sc_place(name):
            i = SC_UNITS.index(name)
            return i % 2, i // 2, n_of(len(SC_UNITS), 2, i % 2)

        def wait_scores(eng, name, l):
            eng.wait_ge(sc_full, l * len(SC_UNITS) + SC_UNITS.index(name) + 1)

        def wait_sc_drained(eng, name, l):
            b, before, total = sc_place(name)
            eng.wait_ge(sc_free[b], l * total + before + 1)

        def scores_read(ins, name):
            ins.then_inc(sc_free[sc_place(name)[0]], 1)

        def read_out(ins, unit):
            ins.then_inc(acc_free[bank_of(unit)[0]], 1)

        def split_high(act, c, l):
            slot, arrived, total = raw_place(c)
            n = 4 * width(c)
            for half in range(2):
                u, before, used = half_place(c, half)
                if half == 0:
                    act.wait_ge(raw_full[slot], l * total + arrived)
                act.wait_ge(split_used[u], l * used + before)
                act.copy(shi[:, u, 0:n], raw[:, slot, half * n:(half + 1) * n]).then_inc(hi_done, 1)

        def split_low(dve, c, l):
            slot, _, _ = raw_place(c)
            n = 4 * width(c)
            for half in range(2):
                u, _, _ = half_place(c, half)
                h = 2 * SPLITS.index(c) + half
                dve.wait_ge(hi_done, l * 2 * len(SPLITS) + h + 1)
                dve.tensor_tensor(slo[:, u, 0:n], raw[:, slot, half * n:(half + 1) * n],
                                  shi[:, u, 0:n].bitcast(f32), ALU.subtract).then_inc(split_full[u], 1)

        w_in = a["w_in"].rearrange("l (k p) n -> l p k n", p=P)
        ada_w = a["ada_w"].rearrange("l (k p) n -> l p k n", p=P)
        w_out = a["w_out"].rearrange("l (k p) n -> l p k n", p=P)
        w_branch = a["w_branch"].rearrange("l b (k p) n -> l b p k n", p=P)
        f1 = a["ffn_w1"].rearrange("l (k p) n -> l p k n", p=P)
        f3 = a["ffn_w3"].rearrange("l (k p) n -> l p k n", p=P)
        f2 = a["ffn_w2"].rearrange("l (g k p) n -> l g p k n", p=P, k=2)
        m1 = a["moe_w1"].rearrange("l e (k p) n -> (l e) p k n", p=P)
        m3 = a["moe_w3"].rearrange("l e (k p) n -> (l e) p k n", p=P)
        m2 = a["moe_w2"].rearrange("l e (g k p) n -> (l e) g p k n", p=P, k=2)

        def sources(c, l):
            if c[:4] == "gate":
                i = COL["gates"] + int(c[4:]) * COLS
                return [(0, w_in[l, :, :, i:i + COLS])]
            if c[:2] == "wo":
                i = int(c[2:]) * COLS
                return [(0, w_out[l, :, :, i:i + COLS])]
            if c in ("ak", "ik"):
                i = COL[c]
                return [(0, w_in[l, :, :, i:i + 64]), (64, w_in[l, :, :, i:i + width(c) - 64])]
            return [(0, w_in[l, :, :, COL[c]:COL[c] + width(c)])]

        def load_chunk(sp, c, l):
            slot, _, _ = raw_place(c)
            i = CHUNKS.index(c)
            if i >= RAW:
                u, before, total = half_place(CHUNKS[i - RAW], 1)
                sp.wait_ge(split_full[u], l * total + before + 1)
                carry(sp)
            else:
                sp.wait_ge(first_summed, max(range(i, 8, RAW)) + 1)
                carry(sp)
            if c[:2] == "wb":
                sp.dma_start(raw[:, slot, :].rearrange("p (k n) -> p k n", k=2),
                             w_branch[l, BRANCH_N[c[2]]]).then_inc(raw_full[slot], 16)
            elif c[:2] == "w2":
                sp.dma_start(raw[:, slot, :].rearrange("p (k n) -> p k n", k=2),
                             f2[0, int(c[3:])]).then_inc(raw_full[slot], 16)
            elif c[:2] in ("w1", "w3"):
                i = int(c[3:]) * COLS
                src = (f1 if c[:2] == "w1" else f3)[0, :, :, i:i + COLS]
                sp.dma_start(raw[:, slot, :].rearrange("p (k n) -> p k n", k=KB), src).then_inc(raw_full[slot], 16)
            else:
                dst = raw[:, slot, 0:KB * width(c)].rearrange("p (k n) -> p k n", k=KB)
                for at, src in sources(c, l):
                    sp.dma_start(dst[:, :, at:at + src.shape[2]], src).then_inc(raw_full[slot], 16)

        def ada_place(i, half):
            return 2 * ADA_ORDER.index(i) + half

        def load_ada(sp, i, l, of_layer):
            for half in range(2):
                h = ada_place(i, half)
                sp.wait_ge(ada_summed, l * ADA_HALVES + h - 1 if h >= 2 else l * ADA_HALVES)
                carry(sp)
                sp.dma_start(ada_raw[:, h % 2], ada_w[of_layer, :, 4 * half:4 * half + 4, i * COLS:(i + 1) * COLS]) \
                    .then_inc(ada_full[h % 2], 16)

        mix.close()
        moe = ctx
        raw_more = sb("raw_more", [P, 6, 2048], f32, moe)
        ehi = sb("ehi", [P, 3, 2048], f32r, moe)
        elo = sb("elo", [P, 3, 2048], f32r, moe)
        sel = sb("sel", [P, TB, EXPERTS + 1, P], f32, moe)
        selT = sb("selT", [P, EXPERTS, SEQ], f32, moe)
        htok = sb("htok", [P, TB, D], f32, moe)
        gth = sb("gth", [P, 2, 256], f32r, moe)
        gtl = sb("gtl", [P, 2, 256], f32r, moe)
        sil = sb("sil", [P, 2, 256], f32, moe)
        glu = sb("glu", [P, 2, 256], f32, moe)
        ysb = sb("ysb", [P, D], f32, moe)
        rt = sb("rt", [P, 160], f32, moe)
        xgh = hh[:].rearrange("p k s -> p (k s)")[:, 0:1024]
        xgl = hl[:].rearrange("p k s -> p (k s)")[:, 0:1024]
        rtu = sb("rtu", [P, TB, 8], u32, moe)
        htok_turned = sem("htok_turned")
        htok_ready = sem("htok_ready")
        logits_done = sem("logits_done")
        gap_ready = sem("gap_ready")
        gapexp_ready = sem("gapexp_ready")
        mask_ready = sem("mask_ready")
        rank_done = sem("rank_done")
        npass_ready = sem("npass_ready")
        sel_ready = sem("sel_ready")
        selw_ready = sem("selw_ready")
        selw_turned = sem("selw_turned")
        selT_ready = sem("selT_ready")
        pair_full = [sem(f"pair_full{i}") for i in range(3)]
        e2_full = [sem(f"e2_full{i}") for i in range(3)]
        e_hi = sem("e_hi")
        e_full = [sem(f"e_full{i}") for i in range(3)]
        e_used = [sem(f"e_used{i}") for i in range(3)]
        gathered = sem("gathered")
        xg_high = sem("xg_high")
        xg_ready = sem("xg_ready")
        e_silu = sem("e_silu")
        e_glu = sem("e_glu")
        e_turned = sem("e_turned")
        e_gth = sem("e_gth")
        e_gtl = sem("e_gtl")
        y_kept = sem("y_kept")
        scattered = sem("scattered")
        x_added = sem("x_added")
        f_std = sem("f_std")
        f_scaled = sem("f_scaled")
        f_turned = sem("f_turned")
        f_kept = sem("f_kept")
        out_stored = sem("out_stored")

        EUNITS = [(0, 0), (0, 1)]
        for g in range(1, EG):
            EUNITS += [(g, 0), (g, 1), (g - 1, 2)]
        EUNITS.append((EG - 1, 2))
        NEU = len(EUNITS)

        def pair_at(i):
            return raw[:, 0:2, :] if i == 0 else raw_more[:, 2 * i - 2:2 * i, :]

        def w2_at(i):
            return raw[:, 2, :] if i == 0 else raw_more[:, 3 + i, :]

        def e_unit(g, part):
            j = EUNITS.index((g, part))
            return j % 3, j // 3

        GPS = [n_of(EG, 3, i) for i in range(3)]

        def load_expert(sp, e, it, very_first=False):
            for j, (g, part) in enumerate(EUNITS):
                r = g % 3
                if part == 0:
                    if g >= 3:
                        u, before = e_unit(g - 3, 1)
                        sp.wait_ge(e_full[u], it * (NEU // 3) + before + 1)
                    elif not very_first:
                        u, before = e_unit(max(range(r, EG, 3)), 1)
                        sp.wait_ge(e_full[u], (it - 1) * (NEU // 3) + before + 1)
                    elif g == 1:
                        sp.wait_ge(mixer_over, 3)
                    for n, w in enumerate((m1, m3)):
                        sp.dma_start(pair_at(r)[:, n, :].rearrange("p (k n) -> p k n", k=KB),
                                     w[e, :, :, g * COLS:(g + 1) * COLS]).then_inc(pair_full[r], 16)
                elif part == 2:
                    if g >= 3:
                        u, before = e_unit(g - 3, 2)
                        sp.wait_ge(e_full[u], it * (NEU // 3) + before + 1)
                    elif not very_first:
                        u, before = e_unit(max(range(r, EG, 3)), 2)
                        sp.wait_ge(e_full[u], (it - 1) * (NEU // 3) + before + 1)
                    sp.dma_start(w2_at(r).rearrange("p (k n) -> p k n", k=2), m2[e, g]).then_inc(e2_full[r], 16)

        block = ctx.enter_context(nc.Block())

        @block.sync
        def _(sp):
            sp.dma_start(const[:], a["consts"]).then_inc(start_loaded, 16)
            sp.dma_start(htmp[:].rearrange("p k s -> p (k s)").rearrange("p (t d) -> p t d", t=TB),
                         a["x"].rearrange("b (t p) d -> p (b t) d", p=P)).then_inc(start_loaded, 16)
            sp.dma_start(cosT[64:96, :].bitcast(i32),
                         a["positions"].broadcast_to([32, SEQ])).then_inc(start_loaded, 16)
            sp.wait_ge(rows_cleared, 1)
            with sp.Fori(0, L) as l:
                sp.wait_ge(params_ready, l)
                carry(sp)

                def row(name, n, src):
                    sp.dma_start(rows[ROW[name]:ROW[name] + n, 0:src.shape[1]], src).then_inc(rows_loaded, 16)

                row("c", 8, a["c"].rearrange("b (n p) -> (b n) p", p=P))
                row("norm1", 8, a["norm1_g"][l].rearrange("(n p) -> n p", p=P))
                row("ada_b", 48, a["ada_b"][l].rearrange("(n p) -> n p", p=P))
                row("norm2", 8, a["norm2_g"][l].rearrange("(n p) -> n p", p=P))
                row("qn", 2, a["mla_q_norm_g"][l].rearrange("(n p) -> n p", p=P))
                row("kvn", 1, a["mla_kv_norm_g"][l].rearrange("(n p) -> n p", p=P))
                row("final", 8, a["final_norm_g"].rearrange("(n p) -> n p", p=P))
                row("lq1", 1, a["diff_lq1"][l].rearrange("(n p) -> n p", n=1))
                row("lk1", 1, a["diff_lk1"][l].rearrange("(n p) -> n p", n=1))
                row("lq2", 1, a["diff_lq2"][l].rearrange("(n p) -> n p", n=1))
                row("lk2", 1, a["diff_lk2"][l].rearrange("(n p) -> n p", n=1))
                row("one_minus_lam", 2, a["lam_rows"][l])
                for half in range(2):
                    r = ROW["diff"]
                    sp.dma_start(rows[r:r + 1, 64 * half:64 * half + 64],
                                 a["diff_norm_g"][l].rearrange("(n p) -> n p", n=1)).then_inc(rows_loaded, 16)
                with sp.If(l < 1):
                    for i in range(8):
                        if i >= RAW:
                            sp.wait_ge(first_summed, i - RAW + 1)
                        sp.dma_start(raw[:, i % RAW, :].rearrange("p (k n) -> p k n", k=KB),
                                     ada_w[0, :, :, i * COLS:(i + 1) * COLS]).then_inc(first_full[i % RAW], 16)
                for u in range(HALVES):
                    sp.wait_ge(split_full[u], l * n_of(2 * len(SPLITS), HALVES, u))
                    carry(sp)
                for c in MIX_CHUNKS:
                    if c == "cq":
                        sp.wait_ge(values_done, l * NATT)
                        carry(sp)
                        sp.dma_start(uq[:], a["mla_w_uq"][l].rearrange("(k p) n -> p k n", p=P)) \
                            .then_inc(small_w_loaded, 16)
                        sp.dma_start(ukv[:], a["mla_w_ukv"][l]).then_inc(small_w_loaded, 16)
                    load_chunk(sp, c, l)
                    if c in ADA_AFTER:
                        load_ada(sp, ADA_AFTER[c], l, l)
                with sp.If(l < 1):
                    for c in FFN_CHUNKS:
                        load_chunk(sp, c, 0)
                        if c in ADA_NEXT:
                            load_ada(sp, ADA_NEXT[c], 0, 1)
            sp.dma_start(router_w[:], a["router_w"].rearrange("l (k p) n -> p (l k) n", p=P)) \
                .then_inc(small_w_loaded, 16)
            sp.dma_start(router_b[:], a["router_b"]).then_inc(small_w_loaded, 16)
            for u in range(HALVES):
                sp.wait_ge(split_full[u], n_of(2 * len(SPLITS), HALVES, u) + n_of(2 * NMIX, HALVES, u))
            load_expert(sp, 0, 0, True)
            with sp.Fori(1, EXPERTS) as e:
                load_expert(sp, e, e)
            sp.wait_ge(npass_ready, 1)
            npass = sp.value_load(npass_i[0:1, 0:1], min_val=1, max_val=2)
            with sp.If(npass > 1):
                with sp.Fori(0, EXPERTS) as e2:
                    load_expert(sp, e2, e2 + EXPERTS)
            for t in range(TB):
                sp.wait_ge(f_kept, 2 * t + 2)
                sp.dma_start(out.rearrange("b (t p) d -> p (b t) d", p=P)[:, t, :], htok[:, t, :]).then_inc(out_stored, 16)
            sp.wait_ge(out_stored, 16 * TB)

        @block.tensor
        def _(pe):
            mm = pe.matmul

            def three(outp, w_hi, w_lo, x_hi, x_lo, first, last, weights_still=True):
                for n, (w, x) in enumerate(((w_hi, x_hi), (w_hi, x_lo), (w_lo, x_hi)) if weights_still else
                                           ((w_hi, x_hi), (w_lo, x_hi), (w_hi, x_lo))):
                    lhs, rhs = (w, x) if weights_still else (x, w)
                    ins = mm(outp, lhs, rhs, start=first and n == 0, stop=last and n == 2, skip_group_check=True)
                return ins

            pe.wait_ge(start_loaded, 48)
            xtok = htmp[:].rearrange("p k s -> p (k s)").rearrange("p (t d) -> p t d", t=TB)
            for b in range(4):
                for j in range(2):
                    for t in range(TB):
                        k = 2 * b + j
                        ins = pe.transpose(ps[b][:, j * 256 + t * 128:j * 256 + (t + 1) * 128],
                                           xtok[:, t, k * 128:(k + 1) * 128], C["ident"])
                ins.then_inc(x_turned, 1)
            pe.wait_ge(x_kept, 4)

            with pe.Fori(0, L) as l:
                def chunk_product(unit, c, parts):
                    acc = wait_acc_free(pe, unit, l)
                    w = width(c)
                    first = True
                    for half in range(2):
                        u, before, total = half_place(c, half)
                        pe.wait_ge(split_full[u], l * total + before + 1)
                        for (o0, o1), kind, (c0, c1), t in parts:
                            for kk in range(4):
                                k = 4 * half + kk
                                whi = shi[:, u, kk * w + c0:kk * w + c1]
                                wlo = slo[:, u, kk * w + c0:kk * w + c1]
                                if kind == "feat":
                                    ins = three(acc[:, o0:o1], whi, wlo, hh[:, k, :], hl[:, k, :],
                                                first, k == KB - 1)
                                else:
                                    ts = slice(t * 128, (t + 1) * 128)
                                    ins = three(acc[:, o0:o1], whi, wlo, hh[:, k, ts], hl[:, k, ts],
                                                first, k == KB - 1, False)
                                first = False
                        ins.then_inc(split_used[u], 1)

                two = [((0, 256), "feat", (0, 128), 0), ((256, 512), "feat", (128, 256), 0)]
                PARTS = {
                    "ik": [((0, 256), "feat", (0, 128), 0), ((256, 260), "tok", (128, 132), 0),
                           ((260, 264), "tok", (128, 132), 1)],
                    "ak": [((0, 256), "feat", (0, 128), 0), ((256, 320), "tok", (128, 192), 0),
                           ((320, 384), "tok", (128, 192), 1)],
                    "ckv": [((0, 256), "feat", (0, 128), 0), ((256, 512), "feat", (64, 192), 0)],
                    "sv": [((0, 256), "tok", (0, 256), 0), ((256, 512), "tok", (0, 256), 1)],
                }
                PARTS["dv"] = PARTS["sv"]

                def ada(acc, sums):
                    for n, chunk in enumerate(sums):
                        for j in range(2):
                            ins = mm(acc[:, 2 * n + j:2 * n + j + 1], chunk[:, j * 128:(j + 1) * 128],
                                     C["ones"][:, 0:1], start=True, stop=True)
                    ins.then_inc(acc_full, 1)

                def stats(unit, norm):
                    acc = wait_acc_free(pe, unit, l)
                    for k in range(KB):
                        if k % 4 == 0:
                            pe.wait_ge(squares, l * 4 + 2 * norm + k // 4 + 1)
                        ins = mm(acc[:, 0:256], C["ones"], htmp[:, k, :], start=k == 0, stop=k == KB - 1)
                    ins.then_inc(acc_full, 1)

                def unit(name):
                    if name == "params":
                        acc = wait_acc_free(pe, name, l)
                        pe.wait_ge(rows_loaded, (l + 1) * 14 * 16)
                        pe.transpose(acc[:, 0:P], rows[:], C["ident"]).then_inc(acc_full, 1)
                    elif name in ("stats1", "stats2"):
                        stats(name, int(name[-1]) - 1)
                    elif name == "ada_a":
                        acc = wait_acc_free(pe, name, l)
                        carry(pe)
                        pe.wait_ge(first_summed, 8)
                        carry(pe)
                        pe.wait_ge(ada_summed, l * ADA_HALVES)
                        ada(acc, [ada_first[:, n, :] for n in range(8)])
                    elif name[:4] == "adar":
                        acc = wait_acc_free(pe, name, l)
                        pe.wait_ge(ada_summed, l * ADA_HALVES + 8 * (int(name[4:]) + 1))
                        ada(acc, [ada_sum[:, n, :] for n in range(4)])
                    elif name == "lam":
                        acc = wait_acc_free(pe, name, l)
                        pe.wait_ge(lamprod_ready, l + 1)
                        mm(acc[:, 0:2], C["ones"][0:32, :], small[0:32, 0:2], start=True, stop=True).then_inc(acc_full, 1)
                    elif name == "mla_stats":
                        acc = wait_acc_free(pe, name, l)
                        pe.wait_ge(lat_squares, l + 1)
                        mm(acc[:, 0:256], C["ones"], tmpA[:, 0:256], start=True, stop=False)
                        mm(acc[:, 0:256], C["ones"], tmpA[:, 256:512], start=False, stop=True)
                        mm(acc[:, 256:512], C["ones"], krT[:, :], start=True, stop=True).then_inc(acc_full, 1)
                    elif name[:2] == "uq":
                        acc = wait_acc_free(pe, name, l)
                        if name == "uq01":
                            pe.wait_ge(small_w_loaded, 32 * (l + 1))
                            pe.wait_ge(lat_normed, l + 1)
                        for j in range(2):
                            h = int(name[2 + j])
                            for k in range(2):
                                ins = mm(acc[0:96, j * 256:(j + 1) * 256], uq[:, k, h * 96:(h + 1) * 96],
                                         cqT[:, k, :], start=k == 0, stop=k == 1)
                        ins.then_inc(acc_full, 1)
                    elif name in ("uk01", "uk23"):
                        acc = wait_acc_free(pe, name, l)
                        for j in range(2):
                            h = int(name[2 + j])
                            ins = mm(acc[0:64, j * 256:(j + 1) * 256], ukv[:, h * 128:h * 128 + 64], ckvT[:],
                                     start=True, stop=True)
                        ins.then_inc(acc_full, 1)
                    elif name == "uv":
                        acc = wait_acc_free(pe, name, l)
                        v = ukv[:].rearrange("p (h two d) -> p h two d", h=HEADS, two=2)[:, :, 1, :]
                        for t in range(TB):
                            ins = mm(acc[:, t * 256:(t + 1) * 256], ckvT[:, t * 128:(t + 1) * 128], v,
                                     start=True, stop=True)
                        ins.then_inc(acc_full, 1)
                    elif name in ("rot01", "rot23"):
                        acc = wait_acc_free(pe, name, l)
                        carry(pe)
                        wait_drained(pe, "uq" + name[3:], l)
                        carry(pe)
                        h = int(name[3])
                        mm(acc[64:96, :], C["rot"][64:96, :], mqT[64:96, h:h + 2, :], start=True, stop=True) \
                            .then_inc(acc_full, 1)
                    elif name == "rotk":
                        acc = wait_acc_free(pe, name, l)
                        carry(pe)
                        wait_drained(pe, "ckv", l)
                        carry(pe)
                        mm(acc[64:96, 0:256], C["rot"][64:96, :], krr[64:96, :], start=True, stop=True) \
                            .then_inc(acc_full, 1)
                    elif name == "dstats":
                        acc = wait_acc_free(pe, name, l)
                        pe.wait_ge(y_squared, l + 1)
                        mm(acc[:], C["blk"], tmpA[:], start=True, stop=True).then_inc(acc_full, 1)
                    elif name[:2] == "wb":
                        b, q = name[2], int(name[4])
                        acc = wait_acc_free(pe, name, l)
                        n = BRANCH_ORDER.index(b)
                        if q == 0:
                            pe.wait_ge(y_split, 4 * l + n + 1)
                        for k in range(2):
                            u, before, total = half_place(name[:3], k)
                            if q == 0:
                                pe.wait_ge(split_full[u], l * total + before + 1)
                            for j in range(2):
                                m = 2 * q + j
                                ins = three(acc[:, j * 256:(j + 1) * 256], shi[:, u, m * 128:(m + 1) * 128],
                                            slo[:, u, m * 128:(m + 1) * 128], yh[:, n, k * 256:(k + 1) * 256],
                                            yl[:, n, k * 256:(k + 1) * 256], k == 0 and j == 0, k == 1)
                            if q == 3:
                                ins.then_inc(split_used[u], 1)
                        if q < 3:
                            ins.then_inc(acc_full, 1)
                    else:
                        if name == "iq":
                            pe.wait_ge(h_split, 4 * l + 2)
                        if name == "wo0":
                            pe.wait_ge(m_split, 4 * (l + 1))
                        chunk_product(name, name, PARTS.get(name, two))

                def other_rows(ins):
                    rows_no[0] += 1
                    ins.then_inc(pe_order, 1)
                    pe.wait_ge(pe_order, rows_no[0])

                rows_no = [0]

                def index_scores(i):
                    b, before, total = sc_place(f"I{i}")
                    pe.wait_ge(sc_free[b], l * total + before)
                    if i == 0:
                        wait_drained(pe, "iq", l)
                        wait_drained(pe, "ik", l)
                    qb, keys, heads = (0, 128, (0, 2, 1, 3)) if i == 0 else (1, 256, (i - 1, i + 1))
                    for n, h in enumerate(heads):
                        if n and h % 2 != heads[n - 1] % 2:
                            other_rows(ins)
                        r = slice(64 * (h % 2), 64 * (h % 2) + 64)
                        ins = mm(ps[SCB + b][:, n * keys:(n + 1) * keys], iqT[r, h // 2, qb * 128:qb * 128 + 128],
                                 ikT[r, 0:keys], start=True, stop=True)
                    ins.then_inc(sc_full, 1)

                def scores(t):
                    br, i = ATT[t]
                    b, before, total = sc_place(f"{br}{i}")
                    sc = ps[SCB + b]
                    pe.wait_ge(sc_free[b], l * total + before)
                    if br == "C":
                        if i == 0:
                            wait_drained(pe, "sq", l)
                            wait_drained(pe, "sk", l)
                        r = slice(64 * (i % 2), 64 * (i % 2) + 64)
                        mm(sc[:, 0:256], skT[r, i // 2, 0:128], sqT[r, i // 2, :], start=True, stop=False,
                           skip_group_check=True)
                        mm(sc[:, 256:384], skT[r, i // 2, 128:256], sqT[r, i // 2, 128:256], start=False, stop=False,
                           skip_group_check=True).then_inc(sc_full, 1)
                        return
                    q0, keys, maps = head_cols(ATT[t])
                    if i == 0:
                        wait_all_drained(pe, {"B": ("uk01", "uk23"), "D": ("dq", "dk"), "A": ("aq", "ak")}[br], l)
                        if br == "B":
                            pe.wait_ge(q_roped, 2 * (l + 1))
                            pe.wait_ge(k_roped, l + 1)
                    for n, m in enumerate(maps):
                        if n and (br == "D" or br == "A" and m % 2 != maps[n - 1] % 2):
                            other_rows(ins)
                        if br == "B":
                            q, k = mqT[:, m, q0:q0 + 128], mkT[:, m, 0:keys]
                        elif br == "D":
                            r = slice(32 * (m % 4), 32 * (m % 4) + 32)
                            q, k = dqT[r, m // 4, q0:q0 + 128], dkT[r, m // 4, 0:keys]
                        else:
                            r = slice(64 * (m % 2), 64 * (m % 2) + 64)
                            q, k = aqT[r, m // 2, q0:q0 + 128], akT[r, 0:keys]
                        ins = mm(sc[:, n * keys:(n + 1) * keys], q, k, start=True, stop=True)
                    ins.then_inc(sc_full, 1)

                def second(t):
                    br, i = ATT[t]
                    if br == "C":
                        b, _, _ = sc_place(f"C{i}")
                        sc, sp_ = ps[SCB + b], prob[:, t % 2, :]
                        pe.wait_ge(z_masked, 4 * l + i + 1)
                        mm(sc[:, 0:256], C["ntri"], sp_[:, 0:256], start=False, stop=False, skip_group_check=True)
                        mm(sc[:, 128:256], C["nones"], sp_[:, 256:384], start=False, stop=False, skip_group_check=True)
                        mm(sc[:, 256:384], C["ntri"], sp_[:, 256:384], start=False, stop=True,
                           skip_group_check=True).then_inc(z_summed, 1)
                        return
                    v = t - 4
                    pe.wait_ge(exp_ready, l * NSM + v + 1)
                    pe.wait_ge(diag_ready, l * NSM + v + 1)
                    if v >= 2:
                        pe.wait_ge(turned_kept, l * NSM + v - 1)
                    q0, keys, maps = head_cols(ATT[t])
                    tp = ps[TPB + v % 2]
                    kb = keys // 128
                    per = 2 if br == "D" else 1
                    for n, m in enumerate(maps):
                        for j in range(kb):
                            o = (n // per) * keys + j * 128
                            ins = mm(tp[:, o:o + 128], prob[:, t % 2, n * keys + j * 128:n * keys + (j + 1) * 128],
                                     diag[:, t % 2, n * 128:(n + 1) * 128], start=(n == 0 and j == 0),
                                     stop=(n % per == per - 1), skip_group_check=True)
                    ins.then_inc(turned, 1)

                def values(t):
                    br, i = ATT[t]
                    y = ps[YB + BRANCH_ORDER.index(br) % 2]
                    if i == 0 and BRANCH_ORDER.index(br) >= 2:
                        pe.wait_ge(y_split, 4 * l + BRANCH_ORDER.index(br) - 1)
                    p_ = pT[:, t % 2, :]
                    if br == "C":
                        if i == 0:
                            wait_drained(pe, "sv", l)
                        pe.wait_ge(w_masked, 4 * l + i + 1)
                        yo = y[64 * (i % 2):64 * (i % 2) + 64, (i // 2) * 256:(i // 2) * 256 + 256]
                        mm(yo, svt[:, 0, i * 64:(i + 1) * 64], p_[:, 0:256], start=True, stop=True,
                           skip_group_check=True)
                        mm(yo[:, 128:256], svt[:, 1, i * 64:(i + 1) * 64], p_[:, 256:384], start=False, stop=True,
                           skip_group_check=True).then_inc(values_done, 1)
                        return
                    q0, keys, maps = head_cols(ATT[t])
                    pe.wait_ge(turned_kept, l * NSM + t - 4 + 1)
                    if i == 0:
                        wait_drained(pe, {"B": "uv", "D": "dv", "A": "ak"}[br], l)
                    heads = [m // 2 for m in maps if m % 2 == 0] if br == "D" else list(maps)
                    for n, h in enumerate(heads):
                        yo = y[64 * (h % 2):64 * (h % 2) + 64, (h // 2) * 256 + q0:(h // 2) * 256 + q0 + 128]
                        for j in range(keys // 128):
                            v = {"B": mvt, "D": dvt}[br][:, j, h * 64:(h + 1) * 64] if br != "A" else avt[:, j, :]
                            ins = mm(yo, v, p_[:, n * keys + j * 128:n * keys + (j + 1) * 128], start=j == 0,
                                     stop=j == keys // 128 - 1, skip_group_check=True)
                    ins.then_inc(values_done, 1)

                for name in PRE:
                    if name[0] == "@":
                        index_scores(int(name[2]))
                    else:
                        unit(name)
                for t in range(NATT + 2):
                    if t < NATT:
                        scores(t)
                    for name in FILL[t]:
                        unit(name)
                    if 1 <= t <= NATT:
                        second(t - 1)
                    if t >= 2:
                        values(t - 2)
                for name in POST:
                    unit(name)

                with pe.If(l < 1):
                    pe.wait_ge(h_split, 4)
                    for g in range(FG + 1):
                        if g < FG:
                            for n in range(2):
                                c = f"w{1 + 2 * n}_{g}"
                                b = (2 * g + n) % 4
                                if g >= 2:
                                    pe.wait_ge(up_free[b], g // 2)
                                for half in range(2):
                                    u, before, _ = half_place(c, half)
                                    pe.wait_ge(split_full[u], before + 1)
                                    for j in range(2):
                                        for kk in range(4):
                                            k = 4 * half + kk
                                            o = kk * COLS + j * 128
                                            ins = three(ps[b][:, j * 256:(j + 1) * 256], shi[:, u, o:o + 128],
                                                        slo[:, u, o:o + 128], hh[:, k, :], hl[:, k, :],
                                                        k == 0 and j == 0, k == KB - 1)
                                    ins.then_inc(split_used[u], 1)
                        if g >= 1:
                            pe.wait_ge(glu_split, g)
                            for j in range(2):
                                u, before, _ = half_place(f"w2_{g - 1}", j)
                                pe.wait_ge(split_full[u], before + 1)
                                for m in range(KB):
                                    ins = three(ps[4 + m // 2][:, (m % 2) * 256:(m % 2) * 256 + 256],
                                                shi[:, u, m * 128:(m + 1) * 128], slo[:, u, m * 128:(m + 1) * 128],
                                                gh[:, (g - 1) % 2, j * 256:(j + 1) * 256],
                                                gl[:, (g - 1) % 2, j * 256:(j + 1) * 256],
                                                g == 1 and j == 0 and m % 2 == 0, g == FG and j == 1)
                                ins.then_inc(split_used[u], 1)

                pe.sem_clear(pe_order)

            pe.wait_ge(h_split, 8)
            pe.wait_ge(mixer_over, 3)
            for t in range(TB):
                for b in range(2):
                    for j in range(4):
                        k = 4 * b + j
                        ins = pe.transpose(ps[2 * t + b][:, j * 128:(j + 1) * 128],
                                           htmp[:, k, t * 128:(t + 1) * 128], C["ident"])
                    ins.then_inc(htok_turned, 1)
            pe.wait_ge(small_w_loaded, 96)
            for t in range(TB):
                for k in range(KB):
                    mm(ps[4][:, t * 8:t * 8 + 8], htmp[:, k, t * 128:(t + 1) * 128], router_w[:, k, :],
                       start=k == 0, stop=False)
                ins = mm(ps[4][:, t * 8:t * 8 + 8], C["ones"][0:1, :], router_b[:], start=False, stop=True)
            ins.then_inc(logits_done, 1)
            pe.wait_ge(mask_ready, 1)
            mask = rt[:, 0:16].rearrange("p (t e) -> p t e", t=TB)
            mm(ps[5][:, 0:8], C["strict"], mask[:, 0, :], start=True, stop=True)
            mm(ps[5][:, 8:16], C["strict"], mask[:, 1, :], start=True, stop=False)
            mm(ps[5][:, 8:16], C["ones"], mask[:, 0, :], start=False, stop=True)
            mm(ps[5][:, 16:24], C["ones"], mask[:, 0, :], start=True, stop=False)
            mm(ps[5][:, 16:24], C["ones"], mask[:, 1, :], start=False, stop=True).then_inc(rank_done, 1)
            pe.wait_ge(npass_ready, 1)
            npass = pe.value_load(npass_i[0:1, 0:1], min_val=1, max_val=2)
            with pe.Fori(0, npass) as p:
                def gather(nth, e):
                    for b in range(2):
                        if b == 0:
                            pe.wait_ge(x_added, nth * 4)
                        for j in range(4):
                            k = 4 * b + j
                            for t in range(TB):
                                ins = mm(ps[6 + b][:, j * 128:(j + 1) * 128], htok[:, t, k * 128:(k + 1) * 128],
                                         sel[:, t, e, :], start=t == 0, stop=t == TB - 1)
                        ins.then_inc(gathered, 1)

                pe.wait_ge(selw_ready, p + 1)
                pe.wait_ge(htok_ready, 4)
                for b in range(4):
                    for j in range(4):
                        e_, t_ = 2 * b + j // 2, j % 2
                        ins = pe.transpose(ps[b][:, j * 128:(j + 1) * 128],
                                           htmp[:].rearrange("p k s -> p (k s)")
                                           [:, (t_ * 8 + e_) * 128:(t_ * 8 + e_ + 1) * 128], C["ident"])
                    ins.then_inc(selw_turned, 1)
                gather(p * 8, 0)
                with pe.Fori(0, EXPERTS) as e:
                    it = p * EXPERTS + e
                    N3 = NEU // 3

                    def up(g, part):
                        u, before = e_unit(g, part)
                        if part == 0:
                            if g == 0:
                                pe.wait_ge(xg_ready, 2 * (it + p + 1))
                            pe.wait_ge(e_glu, it * EG + g - 1 if g >= 2 else it * EG)
                        pe.wait_ge(e_full[u], it * N3 + before + 1)
                        wh = ehi[:, u, :].rearrange("p (w k n) -> p w k n", w=2, k=4)
                        wl = elo[:, u, :].rearrange("p (w k n) -> p w k n", w=2, k=4)
                        for kk in range(4):
                            k = 4 * part + kk
                            ks = slice(k * 128, (k + 1) * 128)
                            ins = three(ps[g % 2][:], wh[:, :, kk, :], wl[:, :, kk, :], xgh[:, ks], xgl[:, ks],
                                        k == 0, k == KB - 1, False)
                        ins.then_inc(e_used[u], 1)

                    def turn(g):
                        pe.wait_ge(e_glu, it * EG + g + 1)
                        pe.wait_ge(e_gtl, it * EG + g - 1 if g >= 2 else it * EG)
                        for j in range(2):
                            ins = pe.transpose(ps[2 + g % 2][:, j * 128:(j + 1) * 128],
                                               glu[:, g % 2, j * 128:(j + 1) * 128], C["ident"])
                        ins.then_inc(e_turned, 1)

                    def down(g):
                        u, before = e_unit(g, 2)
                        pe.wait_ge(e_gtl, it * EG + g + 1)
                        pe.wait_ge(e_full[u], it * N3 + before + 1)
                        if g == 0:
                            pe.wait_ge(y_kept, 2 * it)
                        for j in range(2):
                            js = slice(j * 128, (j + 1) * 128)
                            for n in range(2):
                                o = j * 1024 + n * 512
                                ins = three(ps[4 + n][:], ehi[:, u, o:o + 512], elo[:, u, o:o + 512],
                                            gth[:, g % 2, js], gtl[:, g % 2, js], g == 0 and j == 0,
                                            g == EG - 1 and j == 1, False)
                        ins.then_inc(e_used[u], 1)

                    for g in range(EG):
                        up(g, 0)
                        if g >= 1:
                            turn(g - 1)
                        up(g, 1)
                        if g == EG - 1:
                            gather(it, e + 1)
                        if g >= 1:
                            down(g - 1)
                    turn(EG - 1)
                    down(EG - 1)
                    pe.wait_ge(y_kept, 2 * it + 2)
                    pe.wait_ge(selT_ready, 4 * (p + 1))
                    pe.wait_ge(xg_ready, 2 * (it + p + 2))
                    for q in range(4):
                        if q >= 2:
                            pe.wait_ge(x_added, it * 4 + q - 1)
                        for j in range(2):
                            m = 2 * q + j
                            ins = mm(ps[6 + q % 2][:, j * 256:(j + 1) * 256], ysb[:, m * 128:(m + 1) * 128],
                                     selT[:, e, :], start=True, stop=True)
                        ins.then_inc(scattered, 1)

            for k in range(KB):
                if k % 4 == 0:
                    pe.wait_ge(squares, 4 * L + k // 4 + 1)
                ins = mm(ps[0][:, 0:256], C["ones"], htmp[:, k, :], start=k == 0, stop=k == KB - 1)
            ins.then_inc(acc_full, 1)
            pe.wait_ge(f_scaled, 1)
            for t in range(TB):
                for b in range(2):
                    for j in range(4):
                        k = 4 * b + j
                        ins = pe.transpose(ps[1 + 2 * t + b][:, j * 128:(j + 1) * 128],
                                           htmp[:, k, t * 128:(t + 1) * 128], C["ident"])
                    ins.then_inc(f_turned, 1)


        @block.scalar
        def _(act):
            A = act.activation
            step_no = [0]

            def step(ins):
                step_no[0] += 1
                ins.then_inc(act_order, 1)
                act.wait_ge(act_order, step_no[0])

            for b in (0, 2):
                act.wait_ge(x_turned, b + 1)
                act.copy(xT[:, 2 * b:2 * b + 2, :].rearrange("p k s -> p (k s)"), ps[b][:]).then_inc(x_kept, 1)
            act.wait_ge(rope_arg, 1)
            A(sinT[64:96, :], sinT[64:96, :], ACT.Sin).then_inc(rope_ready, 1)
            A(cosT[64:96, :], cosT[64:96, :], ACT.Sin, bias=C["half_pi"][64:96, :], scale=-1.0).then_inc(rope_ready, 1)
            act.wait_ge(x_kept, 4)

            with act.Fori(0, L) as l:
                split_to = [0]

                def advance(c):
                    want = min(SPLITS.index(c) + 2, NMIX)
                    while split_to[0] < want:
                        split_high(act, SPLITS[split_to[0]], l)
                        split_to[0] += 1

                def squares_of_x():
                    for half in range(2):
                        ks = slice(4 * half, 4 * half + 4)
                        A(htmp[:, ks, :], xT[:, ks, :], ACT.Square).then_inc(squares, 1)

                def std(unit):
                    wait_unit(act, unit, l)
                    read_out(A(rstd[:], ps[bank_of(unit)[0]][:, 0:256], ACT.Sqrt, bias=C["eps"], scale=1.0 / D), unit)

                def high_of_h(norm):
                    for half in range(2):
                        ks = slice(4 * half, 4 * half + 4)
                        act.wait_ge(h_ready, 4 * l + 2 * norm + half + 1)
                        act.copy(hh[:, ks, :], htmp[:, ks, :]).then_inc(h_high, 1)

                def drain(name):
                    acc = ps[bank_of(name)[0]]
                    wait_unit(act, name, l)
                    if name == "iq":
                        read_out(A(iqT[:].rearrange("p k s -> p (k s)"), acc[:], ACT.Copy, scale=64 ** -0.5), name)
                    elif name == "ik":
                        act.copy(ikT[:], acc[:, 0:256])
                        read_out(A(iw[:].rearrange("p t h -> p (t h)"), acc[:, 256:264], ACT.Copy,
                                   scale=HEADS ** -0.5), name)
                    elif name == "cq":
                        step(act.copy(cqT[:].rearrange("p k s -> p (k s)"), acc[:]))
                        read_out(A(tmpA[:], acc[:], ACT.Square), name)
                    elif name == "ckv":
                        act.copy(ckvT[:], acc[:, 0:256])
                        A(krT[:], acc[:, 0:256], ACT.Square).then_inc(lat_squares, 1)
                        read_out(act.copy(krr[64:96, :], acc[64:96, 256:512]), name)
                    elif name in ("sq", "aq"):
                        read_out(A((sqT if name == "sq" else aqT)[:].rearrange("p k s -> p (k s)"), acc[:],
                                   ACT.Copy, scale=64 ** -0.5), name)
                    elif name == "dq":
                        read_out(A(dqT[:].rearrange("p k s -> p (k s)"), acc[:], ACT.Copy, scale=32 ** -0.5), name)
                    elif name in ("sk", "dk", "sv", "dv", "uv"):
                        dst = {"sk": skT, "dk": dkT, "sv": svt, "dv": dvt, "uv": mvt}[name]
                        read_out(act.copy(dst[:].rearrange("p k s -> p (k s)"), acc[:]), name)
                    elif name == "ak":
                        act.copy(akT[:], acc[:, 0:256])
                        read_out(act.copy(avt[:].rearrange("p t d -> p (t d)"), acc[:, 256:384]), name)
                    elif name == "mla_stats":
                        A(pT[:, 0, 0:256], acc[:, 0:256], ACT.Sqrt, bias=C["eps"], scale=1.0 / 256)
                        read_out(A(pT[:, 0, 256:512], acc[:, 256:512], ACT.Sqrt, bias=C["eps"], scale=1.0 / 128), name)
                    elif name[:2] == "uq":
                        h = int(name[2])
                        read_out(A(mqT[:, h:h + 2, :].rearrange("p h s -> p (h s)"), acc[0:96, :], ACT.Copy,
                                   scale=96 ** -0.5), name)
                    elif name[:2] == "uk":
                        h = int(name[2])
                        read_out(act.copy(mkT[0:64, h:h + 2, :].rearrange("p h s -> p (h s)"), acc[0:64, :]), name)
                    elif name[:4] == "gate":
                        i = int(name[4:])
                        read_out(act.copy(gates[:, 2 * i:2 * i + 2, :].rearrange("p k s -> p (k s)"), acc[:]), name)
                    elif name == "dstats":
                        read_out(A(tmpA[:], acc[:], ACT.Sqrt, bias=C["eps"], scale=1.0 / 64), name)

                ACT_DRAINS = ("iq", "ik", "cq", "ckv", "sq", "sk", "sv", "mla_stats", "uq01", "uq23", "uk01", "uk23",
                              "uv", "dq", "dk", "dv", "aq", "ak", "dstats")

                def unit(name):
                    for c in chunks_of(name):
                        advance(c)
                    if name in ACT_DRAINS or name[:4] == "gate":
                        drain(name)

                def relu(i):
                    n = f"I{i}"
                    b, _, _ = sc_place(n)
                    if i == 2:
                        act.wait_ge(relu_used, 3 * l + 1)
                    wait_scores(act, n, l)
                    scores_read(A(prob[:, i % 2, :], ps[SCB + b][:], ACT.Relu), n)

                def stage1(t):
                    br, i = ATT[t]
                    pr = prob[:, t % 2, :]
                    if br == "C":
                        if i < 2:
                            act.wait_ge(relu_used, 3 * (l + 1))
                        else:
                            act.wait_ge(z_summed, 4 * l + i - 1)
                        wait_scores(act, f"C{i}", l)
                        step(A(pr[:, 0:384], ps[SCB + sc_place(f"C{i}")[0]][:, 0:384], ACT.Abs))
                        step(A(pr[:, 0:384], pr[:, 0:384], ACT.Exp, scale=-1.0))
                        A(pr[:, 0:384], pr[:, 0:384], ACT.Ln, bias=1.0).then_inc(z_log, 1)
                        return
                    v = t - 4
                    _, keys, maps = head_cols(ATT[t])
                    act.wait_ge(max_ready, l * NSM + v + 1)
                    for n in range(len(maps)):
                        ins = A(pr[:, n * keys:(n + 1) * keys], pr[:, n * keys:(n + 1) * keys], ACT.Exp,
                                bias=small[:, 8 + 4 * (t % 2) + n:9 + 4 * (t % 2) + n],
                                accum_out=small[:, 16 + 4 * (t % 2) + n:17 + 4 * (t % 2) + n])
                    ins.then_inc(exp_ready, 1)

                def stage2(t):
                    br, i = ATT[t]
                    act.wait_ge(values_done, l * NATT + t - 1 if t >= 2 else l * NATT)
                    if br == "C":
                        n = f"C{i}"
                        b, _, _ = sc_place(n)
                        if i == 0:
                            act.wait_ge(lat_normed, l + 1)
                        act.wait_ge(z_summed, 4 * l + i + 1)
                        scores_read(A(pT[:, t % 2, 0:384], ps[SCB + b][:, 0:384], ACT.Exp), n)
                        return
                    v = t - 4
                    act.wait_ge(turned, l * NSM + v + 1)
                    _, keys, maps = head_cols(ATT[t])
                    w = 256 if br == "D" else 512
                    act.copy(pT[:, t % 2, 0:w], ps[TPB + v % 2][:, 0:w]).then_inc(turned_kept, 1)

                def branch_out(br):
                    n = BRANCH_ORDER.index(br)
                    y = ps[YB + n % 2]
                    if br == "D":
                        act.wait_ge(y_float, l + 1)
                        act.copy(yh[:, n, :], tmpA[:]).then_inc(y_high, 1)
                    else:
                        last = max(t for t in range(NATT) if ATT[t][0] == br)
                        act.wait_ge(values_done, l * NATT + last + 1)
                        act.copy(yh[:, n, :], y[:]).then_inc(y_high, 1)

                act.wait_ge(x_fed, 8 * l)
                squares_of_x()
                std("stats1")
                act.wait_ge(params_ready, l + 1)
                carry(act)
                with act.If(l < 1):
                    A(cond[:], pv[:, ROW["c"]:ROW["c"] + KB], ACT.Silu).then_inc(cond_ready, 1)
                advance("iq")
                wait_unit(act, "lam", l)
                read_out(A(small[:, 2:4], ps[bank_of("lam")[0]][:, 0:2], ACT.Exp), "lam")
                high_of_h(0)
                for name in PRE[PRE.index("ada_a") + 1:]:
                    if name[0] == "@":
                        relu(int(name[2]))
                    else:
                        unit(name)
                for t in range(NATT + 2):
                    if FILL[t] and chunks_of(FILL[t][0]):
                        advance(FILL[t][0])
                    if t < NATT:
                        stage1(t)
                    for name in FILL[t]:
                        unit(name)
                    if 1 <= t <= NATT:
                        stage2(t - 1)
                    if t >= 3 and ATT[t - 3][0] != (ATT + [("", 0)])[t - 2][0] and ATT[t - 3][0] in "CB":
                        branch_out(ATT[t - 3][0])
                    if t == NATT - 1:
                        act.wait_ge(values_done, l * NATT + t - 2)
                        A(tmpA[:], ps[YB + 0][:], ACT.Square).then_inc(y_squared, 1)
                branch_out("D")
                for b in range(2):
                    wait_drained(act, [u for u in UNITS if u[:4] == "gate" and bank_of(u)[0] == b][-1], l)
                for n, br in enumerate(BRANCH_ORDER):
                    b = BRANCH_N[br]
                    A(gates[:, 8 * b:8 * b + 8, :], gates[:, 8 * b:8 * b + 8, :], ACT.Sigmoid).then_inc(gates_ready, 1)
                    if n == 1:
                        branch_out("A")
                for name in POST:
                    unit(name)
                    if name[:3] == "wbA":
                        q = int(name[4])
                        act.wait_ge(merged, 4 * l + q + 1)
                        act.copy(hh[:, 2 * q:2 * q + 2, :], htmp[:, 2 * q:2 * q + 2, :]).then_inc(m_high, 1)
                    if name == "wo3":
                        wait_drained(act, "wo3", l)
                        squares_of_x()
                std("stats2")
                high_of_h(1)

                with act.If(l < 1):
                    to = [NMIX]

                    def ahead(c):
                        while to[0] < min(SPLITS.index(c) + 2, len(SPLITS)):
                            split_high(act, SPLITS[to[0]], 0)
                            to[0] += 1

                    for g in range(FG + 1):
                        if g < FG:
                            ahead(f"w1_{g}")
                            ahead(f"w3_{g}")
                            u, before, _ = half_place(f"w1_{g}", 1)
                            act.wait_ge(split_used[u], before + 1)
                            b = (2 * g) % 4
                            A(prob[:, g % 2, :], ps[b][:], ACT.Silu).then_inc(up_free[b], 1)
                        if g >= 1:
                            ahead(f"w2_{g - 1}")
                        if g < FG:
                            if g >= 2:
                                u, before, _ = half_place(f"w2_{g - 2}", 1)
                                act.wait_ge(split_used[u], before + 1)
                            act.wait_ge(up_free[b + 1], g // 2 + 1)
                            act.copy(gh[:, g % 2, :], diag[:, g % 2, :]).then_inc(glu_high, 1)
                act.sem_clear(act_order)
                step_no[0] = 0
            act.nop().then_inc(mixer_over, 1)

            for n in range(4):
                act.wait_ge(htok_turned, n + 1)
                act.copy(htok[:, n // 2, (n % 2) * 512:(n % 2) * 512 + 512], ps[n][:]).then_inc(htok_ready, 1)
            act.wait_ge(gap_ready, 1)
            A(rt[:, 96:98], rt[:, 98:100], ACT.Exp).then_inc(gapexp_ready, 1)
            act.wait_ge(npass_ready, 1)
            npass = act.value_load(npass_i[0:1, 0:1], min_val=1, max_val=2)
            with act.Fori(0, npass) as p:
                for b in range(4):
                    act.wait_ge(selw_turned, 4 * p + b + 1)
                    act.copy(selT[:, 2 * b:2 * b + 2, :].rearrange("p e s -> p (e s)"), ps[b][:]).then_inc(selT_ready, 1)

                def high_of_tokens(nth):
                    for b in range(2):
                        act.wait_ge(gathered, 2 * nth + b + 1)
                        act.copy(xgh[:, b * 512:(b + 1) * 512], ps[6 + b][:]).then_inc(xg_high, 1)

                high_of_tokens(p * 9)
                with act.Fori(0, EXPERTS) as e:
                    it = p * EXPERTS + e
                    N3 = NEU // 3

                    def split(j):
                        g, part = EUNITS[j]
                        r = g % 3
                        act.wait_ge(e_used[j % 3], it * N3 + j // 3)
                        if part == 2:
                            act.wait_ge(e2_full[r], 16 * (it * GPS[r] + g // 3 + 1))
                            act.copy(ehi[:, j % 3, :], w2_at(r)).then_inc(e_hi, 1)
                        else:
                            act.wait_ge(pair_full[r], 32 * (it * GPS[r] + g // 3 + 1))
                            act.copy(ehi[:, j % 3, :].rearrange("p (w n) -> p w n", w=2),
                                     pair_at(r)[:, :, part * 1024:(part + 1) * 1024]).then_inc(e_hi, 1)

                    split(0)
                    split(1)
                    for j, (g, part) in enumerate(EUNITS):
                        if j + 2 < NEU:
                            split(j + 2)
                        if part == 1:
                            u, before = e_unit(g, 1)
                            act.wait_ge(e_used[u], it * N3 + before + 1)
                            act.wait_ge(e_glu, it * EG + g - 1 if g >= 2 else it * EG)
                            A(sil[:, g % 2, :], ps[g % 2][:, 0:256], ACT.Silu).then_inc(e_silu, 1)
                        if g >= 1 and part == 0 or j == NEU - 1:
                            h = g - 1 if part == 0 else g
                            act.wait_ge(e_turned, it * EG + h + 1)
                            if h >= 2:
                                u, before = e_unit(h - 2, 2)
                                act.wait_ge(e_used[u], it * N3 + before + 1)
                            act.copy(gth[:, h % 2, :], ps[2 + h % 2][:, 0:256]).then_inc(e_gth, 1)
                        if part == 1 and g == EG - 1:
                            high_of_tokens(it + p + 1)
                    u, before = e_unit(EG - 1, 2)
                    act.wait_ge(e_used[u], it * N3 + before + 1)
                    act.wait_ge(scattered, 4 * it)
                    act.copy(ysb[:, 0:512], ps[4][:]).then_inc(y_kept, 1)

            act.wait_ge(x_added, npass * (4 * EXPERTS))
            for half in range(2):
                ks = slice(4 * half, 4 * half + 4)
                A(htmp[:, ks, :], xT[:, ks, :], ACT.Square).then_inc(squares, 1)
            act.wait_ge(acc_full, L * len(SIGNALLED) + 1)
            A(rstd[:], ps[0][:, 0:256], ACT.Sqrt, bias=C["eps"], scale=1.0 / D).then_inc(f_std, 1)
            for n in range(4):
                act.wait_ge(f_turned, n + 1)
                act.copy(htok[:, n // 2, (n % 2) * 512:(n % 2) * 512 + 512], ps[1 + n][:]).then_inc(f_kept, 1)

        @block.vector
        def _(dve):
            step_no = [0]

            def step(ins):
                step_no[0] += 1
                ins.then_inc(vec_order, 1)
                dve.wait_ge(vec_order, step_no[0])

            TT, TS, STT = dve.tensor_tensor, dve.tensor_scalar, dve.scalar_tensor_tensor
            R = slice(64, 96)
            dve.wait_ge(start_loaded, 48)
            step(dve.tensor_copy(sinT[R, :], cosT[R, :].bitcast(i32)))
            step(TS(sinT[R, :], sinT[R, :], C["inv"][R, :], None, ALU.mult))
            step(TS(tmpA[R, 0:256], sinT[R, :], 1.0 / (2 * math.pi), 12582912.0, ALU.mult, ALU.add))
            step(TS(tmpA[R, 0:256], tmpA[R, 0:256], 12582912.0, None, ALU.subtract))
            c1 = 6.28125
            c2 = math.floor((2 * math.pi - c1) * 2 ** 21) / 2 ** 21
            for c in (c1, c2, 2 * math.pi - c1 - c2):
                step(STT(sinT[R, :], tmpA[R, 0:256], -c, sinT[R, :], ALU.mult, ALU.add))
            step(TS(sinT[R, :], sinT[R, :], -3.1415925, 3.1415925, ALU.max, ALU.min))
            STT(cosT[R, :], sinT[R, :], -1.0, sinT[R, :], ALU.mult, ALU.max).then_inc(rope_arg, 1)
            for b in (1, 3):
                dve.wait_ge(x_turned, b + 1)
                dve.tensor_copy(xT[:, 2 * b:2 * b + 2, :].rearrange("p k s -> p (k s)"), ps[b][:]).then_inc(x_kept, 1)
            dve.wait_ge(x_kept, 4)
            dve.sem_clear(vec_order)
            step_no[0] = 0

            with dve.Fori(0, L) as l:
                split_to = [0]

                def advance(c):
                    want = min(SPLITS.index(c) + 2, NMIX)
                    while split_to[0] < want:
                        split_low(dve, SPLITS[split_to[0]], l)
                        split_to[0] += 1

                def scale_x(unit):
                    wait_drained(dve, unit, l)
                    step(dve.reciprocal(rstd[:], rstd[:]))
                    for half in range(2):
                        ks = slice(4 * half, 4 * half + 4)
                        step(TT(htmp[:, ks, :], xT[:, ks, :], rstd[:].unsqueeze(1).broadcast_to([P, 4, SEQ]), ALU.mult))

                def modulate(norm, shift, scale, gain):
                    step(STT(hscale[:], adav[:, scale:scale + KB], 1.0, pv[:, gain:gain + KB], ALU.add, ALU.mult))
                    for half in range(2):
                        for m in range(4 * half, 4 * half + 4):
                            ins = TS(htmp[:, m, :], htmp[:, m, :], hscale[:, m:m + 1], adav[:, shift + m:shift + m + 1],
                                     ALU.mult, ALU.add)
                        ins.then_inc(h_ready, 1)
                    for half in range(2):
                        ks = slice(4 * half, 4 * half + 4)
                        dve.wait_ge(h_high, 4 * l + 2 * norm + half + 1)
                        TT(hl[:, ks, :], htmp[:, ks, :], hh[:, ks, :].bitcast(f32), ALU.subtract).then_inc(h_split, 1)

                def drain(name):
                    acc = ps[bank_of(name)[0]]
                    if name[:4] == "adar":
                        i = 16 + 8 * int(name[4:])
                        wait_unit(dve, name, l)
                        read_out(TT(adav[:, i:i + 8], acc[:, 0:8], pv[:, i:i + 8], ALU.add), name)
                    elif name in ("rot01", "rot23"):
                        h = int(name[3])
                        q = mqT[R, h:h + 2, :]
                        cosb = cosT[R, :].unsqueeze(1).broadcast_to([32, 2, SEQ])
                        sinb = sinT[R, :].unsqueeze(1).broadcast_to([32, 2, SEQ])
                        wait_unit(dve, name, l)
                        if name == "rot23":
                            dve.wait_ge(q_roped, 2 * l + 1)
                        read_out(TT(tmpA[R, :].rearrange("p (h s) -> p h s", h=2),
                                    acc[R, :].rearrange("p (h s) -> p h s", h=2), sinb, ALU.mult), name)
                        step(TT(q, q, cosb, ALU.mult))
                        wait_drained(dve, name, l)
                        TT(q, q, tmpA[R, :].rearrange("p (h s) -> p h s", h=2), ALU.add).then_inc(q_roped, 1)
                    elif name == "rotk":
                        wait_unit(dve, name, l)
                        dve.wait_ge(q_roped, 2 * (l + 1))
                        read_out(TT(tmpA[R, 0:256], acc[R, 0:256], sinT[R, :], ALU.mult), name)
                        step(TT(krr[R, :], krr[R, :], cosT[R, :], ALU.mult))
                        wait_drained(dve, name, l)
                        TT(mkT[R, :, :], krr[R, :].unsqueeze(1).broadcast_to([32, HEADS, SEQ]),
                           tmpA[R, 0:256].unsqueeze(1).broadcast_to([32, HEADS, SEQ]), ALU.add).then_inc(k_roped, 1)

                def unit(name):
                    for c in chunks_of(name):
                        advance(c)
                    drain(name)

                def index(i):
                    wait_sc_drained(dve, f"I{i}", l)
                    if i == 2:
                        dve.wait_ge(relu_used, 3 * l + 2)
                    t, keys, heads = (0, 128, (0, 2, 1, 3)) if i == 0 else (1, 256, (i - 1, i + 1))
                    dst = score[:, 0:128] if i == 0 else score[:, 128:384]
                    for n, h in enumerate(heads):
                        before = C["causal"][:, 256 - keys:256] if h == 0 else dst
                        ins = STT(dst, prob[:, i % 2, n * keys:(n + 1) * keys], iw[:, t, h:h + 1], before,
                                  ALU.mult, ALU.add)
                        if n < len(heads) - 1:
                            step(ins)
                    ins.then_inc(relu_used, 1)

                def topk_round(r):
                    if r == 0:
                        dve.wait_ge(relu_used, 3 * (l + 1))
                        carry(dve)
                    for t, cols in enumerate((slice(0, 128), slice(128, 384))):
                        src = (score if r == 0 else work)[:, cols]
                        step(dve.max(small[:, 32 + 8 * t:40 + 8 * t], src))
                        step(dve.match_replace(work[:, cols], small[:, 32 + 8 * t:40 + 8 * t], src, TAKEN))
                    if r == TOPK // 8 - 1:
                        step(TS(work[:], work[:], TAKEN / 2, NEG, ALU.is_gt, ALU.mult))

                def stage1a(t):
                    br, i = ATT[t]
                    if br == "C":
                        return
                    name = f"{br}{i}"
                    sc = ps[SCB + sc_place(name)[0]]
                    pr = prob[:, t % 2, :]
                    wait_scores(dve, name, l)
                    if t >= 2:
                        if ATT[t - 2][0] == "C":
                            dve.wait_ge(z_summed, 4 * l + t - 1)
                        else:
                            dve.wait_ge(turned, l * NSM + t - 2 - 4 + 1)
                    _, keys, maps = head_cols(ATT[t])
                    n = len(maps)
                    p3 = pr.rearrange("p (n k) -> p n k", n=n)
                    s3 = sc[:].rearrange("p (n k) -> p n k", n=n)
                    if br == "B":
                        ins = TT(p3, s3, C["causal"][:, 256 - keys:256].unsqueeze(1).broadcast_to([P, n, keys]), ALU.add)
                    else:
                        dist = C["dist"][:, 256 - keys:256]
                        per = 2 if br == "D" else 1
                        for j in range(0, n, per):
                            head = maps[j] // per
                            slope = 2.0 ** -(2 * head + (2 if br == "D" else 1))
                            ins = STT(p3[:, j:j + per, :], dist.unsqueeze(1).broadcast_to([P, per, keys]), slope,
                                      s3[:, j:j + per, :], ALU.mult, ALU.add)
                    scores_read(ins, name)
                    wait_sc_drained(dve, name, l)
                    if br == "A":
                        bias = work[:, 0:128] if keys == 128 else work[:, 128:384]
                        step(TT(p3, p3, bias.unsqueeze(1).broadcast_to([P, n, keys]), ALU.add))
                    dve.tensor_reduce(small[:, 8 + 4 * (t % 2):8 + 4 * (t % 2) + n], p3, AX.X, ALU.max, negate=True) \
                        .then_inc(max_ready, 1)

                def stage1b(t):
                    br, i = ATT[t]
                    pr = prob[:, t % 2, :]
                    if br == "C":
                        sc = ps[SCB + sc_place(f"C{i}")[0]]
                        dve.wait_ge(z_log, 4 * l + i + 1)
                        STT(pr[:, 0:384], sc[:, 0:384], 0.0, pr[:, 0:384], ALU.max, ALU.add).then_inc(z_soft, 1)
                        return
                    v = t - 4
                    n = len(head_cols(ATT[t])[2])
                    dve.wait_ge(exp_ready, l * NSM + v + 1)
                    rec = small[:, 24 + 4 * (t % 2):24 + 4 * (t % 2) + n]
                    step(dve.reciprocal(rec, small[:, 16 + 4 * (t % 2):16 + 4 * (t % 2) + n]))
                    if br == "D":
                        odd = rec.rearrange("p (a two) -> p a two", two=2)[:, :, 1]
                        step(TS(odd, odd, small[:, 5:6], None, ALU.mult))
                    TT(diag[:, t % 2, 0:n * 128].rearrange("p (n k) -> p n k", n=n),
                       C["ident"].unsqueeze(1).broadcast_to([P, n, 128]), rec.unsqueeze(2).broadcast_to([P, n, 128]),
                       ALU.mult).then_inc(diag_ready, 1)

                def low_of_branch(br):
                    n = BRANCH_ORDER.index(br)
                    dve.wait_ge(y_high, 4 * l + n + 1)
                    y = tmpA[:] if br == "D" else ps[YB + n % 2][:]
                    TT(yl[:, n, :], y, yh[:, n, :].bitcast(f32), ALU.subtract).then_inc(y_split, 1)

                wait_unit(dve, "params", l)
                read_out(dve.tensor_copy(pv[:], ps[bank_of("params")[0]][:, 0:NROW]), "params")
                wait_drained(dve, "params", l)
                TT(small[0:32, 0:2], pv[0:32, ROW["lq1"]:ROW["lq1"] + 4:2], pv[0:32, ROW["lk1"]:ROW["lk1"] + 4:2],
                   ALU.mult).then_inc(lamprod_ready, 1)
                TT(small[:, 6:7], pv[:, ROW["diff"]:ROW["diff"] + 1],
                   pv[:, ROW["one_minus_lam"]:ROW["one_minus_lam"] + 1], ALU.mult).then_inc(params_ready, 1)
                scale_x("stats1")
                with dve.If(l < 1):
                    dve.wait_ge(cond_ready, 1)
                    added = 0
                    for i in range(8):
                        dve.wait_ge(first_full[i % RAW], 16 * (i // RAW + 1))
                        w = raw[:, i % RAW, :].rearrange("p (k n) -> p k n", k=KB)
                        for k in range(KB):
                            if k == 0:
                                ins = TS(ada_first[:, i, :], w[:, 0, :], cond[:, 0:1], None, ALU.mult)
                            else:
                                dve.wait_ge(first_order, added)
                                ins = STT(ada_first[:, i, :], w[:, k, :], cond[:, k:k + 1], ada_first[:, i, :],
                                          ALU.mult, ALU.add)
                            if k < KB - 1:
                                ins.then_inc(first_order, 1)
                                added += 1
                        ins.then_inc(first_summed, 1)
                wait_unit(dve, "ada_a", l)
                read_out(TT(adav[:, 0:16], ps[bank_of("ada_a")[0]][:, 0:16], pv[:, 0:16], ALU.add), "ada_a")
                wait_drained(dve, "ada_a", l)
                modulate(0, 0, 8, ROW["norm1"])
                wait_drained(dve, "lam", l)
                step(TT(small[:, 4:5], small[:, 3:4], small[:, 2:3], ALU.subtract))
                step(TT(small[:, 5:6], small[:, 4:5], pv[:, ROW["lam_init"]:ROW["lam_init"] + 1], ALU.subtract))
                advance("iq")
                for name in PRE[PRE.index("ada_a") + 1:]:
                    if name[0] == "@":
                        index(int(name[2]))
                    elif name == "mla_stats":
                        wait_drained(dve, name, l)
                        step(dve.reciprocal(pT[:, 0, :], pT[:, 0, :]))
                        for k in range(2):
                            step(STT(cqT[:, k, :], cqT[:, k, :], pv[:, ROW["qn"] + k:ROW["qn"] + k + 1], pT[:, 0, 0:256],
                                     ALU.mult, ALU.mult))
                        STT(ckvT[:], ckvT[:], pv[:, ROW["kvn"]:ROW["kvn"] + 1], pT[:, 0, 256:512],
                            ALU.mult, ALU.mult).then_inc(lat_normed, 1)
                    else:
                        unit(name)
                for t in range(NATT + 2):
                    if t < NATT:
                        stage1a(t)
                    if FILL[t] and chunks_of(FILL[t][0]):
                        advance(FILL[t][0])
                    if t < NATT:
                        stage1b(t)
                    for name in FILL[t]:
                        unit(name)
                    if 2 <= t < 2 + TOPK // 8:
                        topk_round(t - 2)
                    if t >= 3 and ATT[t - 3][0] != (ATT + [("", 0)])[t - 2][0] and ATT[t - 3][0] in "CB":
                        low_of_branch(ATT[t - 3][0])
                wait_drained(dve, "dstats", l)
                step(dve.reciprocal(tmpA[:], tmpA[:]))
                STT(tmpA[:], ps[YB][:], small[:, 6:7], tmpA[:], ALU.mult, ALU.mult).then_inc(y_float, 1)
                low_of_branch("D")
                low_of_branch("A")
                parts = 0
                for name in POST:
                    unit(name)
                    if name[:2] == "wb":
                        q, n = int(name[4]), BRANCH_ORDER.index(name[2])
                        g = gates[:, 8 * BRANCH_N[name[2]] + 2 * q:8 * BRANCH_N[name[2]] + 2 * q + 2, :]
                        acc = ps[bank_of(name)[0]][:].rearrange("p (m s) -> p m s", m=2)
                        if q == 0:
                            dve.wait_ge(gates_ready, 4 * l + n + 1)
                        wait_unit(dve, name, l)
                        if n == 0:
                            read_out(TT(htmp[:, 2 * q:2 * q + 2, :], acc, g, ALU.mult), name)
                        else:
                            if parts >= 10:
                                dve.wait_ge(merged, 4 * l + parts - 9)
                            elif parts >= 2:
                                dve.wait_ge(part_used, 8 * l + parts - 1)
                            read_out(TT(prob[:, parts % 2, :].rearrange("p (m s) -> p m s", m=2), acc, g, ALU.mult), name)
                            parts += 1
                    if name[:3] == "wbA":
                        q = int(name[4])
                        dve.wait_ge(m_high, 4 * l + q + 1)
                        TT(hl[:, 2 * q:2 * q + 2, :], htmp[:, 2 * q:2 * q + 2, :],
                           hh[:, 2 * q:2 * q + 2, :].bitcast(f32), ALU.subtract).then_inc(m_split, 1)
                    if name[:2] == "wo":
                        acc = ps[bank_of(name)[0]]
                        i = int(name[2])
                        wait_unit(dve, name, l)
                        for j in range(2):
                            m = 2 * i + j
                            ins = STT(xT[:, m, :], acc[:, j * 256:(j + 1) * 256], adav[:, 16 + m:17 + m], xT[:, m, :],
                                      ALU.mult, ALU.add)
                        read_out(ins, name)
                scale_x("stats2")
                modulate(1, 24, 32, ROW["norm2"])

                with dve.If(l < 1):
                    to = [NMIX]

                    def ahead(c):
                        while to[0] < min(SPLITS.index(c) + 2, len(SPLITS)):
                            split_low(dve, SPLITS[to[0]], 0)
                            to[0] += 1

                    for g in range(FG + 1):
                        if g < FG:
                            ahead(f"w1_{g}")
                            ahead(f"w3_{g}")
                            b = (2 * g) % 4
                            dve.wait_ge(up_free[b], g // 2 + 1)
                            u, before, _ = half_place(f"w3_{g}", 1)
                            dve.wait_ge(split_used[u], before + 1)
                            TT(diag[:, g % 2, :], prob[:, g % 2, :], ps[b + 1][:], ALU.mult).then_inc(up_free[b + 1], 1)
                        if g >= 1:
                            ahead(f"w2_{g - 1}")
                        if g < FG:
                            dve.wait_ge(glu_high, g + 1)
                            TT(gl[:, g % 2, :], diag[:, g % 2, :], gh[:, g % 2, :].bitcast(f32), ALU.subtract) \
                                .then_inc(glu_split, 1)
                    u, before, _ = half_place(f"w2_{FG - 1}", 1)
                    dve.wait_ge(split_used[u], before + 1)
                    for m in range(KB):
                        STT(xT[:, m, :], ps[4 + m // 2][:, (m % 2) * 256:(m % 2) * 256 + 256], adav[:, 40 + m:41 + m],
                            xT[:, m, :], ALU.mult, ALU.add).then_inc(x_fed, 1)
                dve.sem_clear(vec_order)
                step_no[0] = 0
            dve.nop().then_inc(mixer_over, 1)

            lg = rt[:, 16:32].rearrange("p (t e) -> p t e", t=TB)
            top = rt[:, 32:48].rearrange("p (t e) -> p t e", t=TB)
            idx = rt[:, 48:64].rearrange("p (t e) -> p t e", t=TB)
            mask = rt[:, 0:16].rearrange("p (t e) -> p t e", t=TB)
            comb = rt[:, 64:80].rearrange("p (t e) -> p t e", t=TB)
            second = rt[:, 80:96].rearrange("p (t e) -> p t e", t=TB)
            gapexp, gap, w1, w2 = (rt[:, c:c + 2] for c in (96, 98, 100, 102))
            slot = rt[:, 104:104 + 18].rearrange("p (t e) -> p t e", t=TB)
            dve.wait_ge(mixer_over, 3)
            dve.wait_ge(logits_done, 1)
            step(dve.tensor_copy(rt[:, 16:32], ps[4][:, 0:16]))
            for t in range(TB):
                step(dve.max(top[:, t, :], lg[:, t, :]))
                step(dve.max_index(rtu[:, t, :], top[:, t, :], lg[:, t, :]))
            step(dve.tensor_copy(rt[:, 48:64], rtu[:].rearrange("p t e -> p (t e)")))
            TT(gap, top[:, :, 1], top[:, :, 0], ALU.subtract).then_inc(gap_ready, 1)
            dve.wait_ge(gapexp_ready, 1)
            step(TS(w1, gapexp, 1.0, None, ALU.add))
            step(dve.reciprocal(w1, w1))
            step(TT(w2, w1, gapexp, ALU.mult))
            for t in range(TB):
                step(TS(mask[:, t, :], C["iota"][:, 0:8], idx[:, t, 0:1], None, ALU.is_equal))
                step(TS(second[:, t, :], C["iota"][:, 0:8], idx[:, t, 1:2], None, ALU.is_equal))
                step(TS(comb[:, t, :], second[:, t, :], w2[:, t:t + 1], None, ALU.mult))
                step(STT(comb[:, t, :], mask[:, t, :], w1[:, t:t + 1], comb[:, t, :], ALU.mult, ALU.add))
            TT(mask, mask, second, ALU.add).then_inc(mask_ready, 1)
            dve.wait_ge(rank_done, 1)
            step(dve.memset(rt[:, 104:122], -1.0))
            step(STT(slot[:, :, 0:8], ps[5][:, 0:16].rearrange("p (t e) -> p t e", t=TB), 1.0, mask, ALU.add, ALU.mult))
            step(TS(slot[:, :, 0:8], slot[:, :, 0:8], 1.0, None, ALU.subtract))
            step(dve.tensor_reduce(rt[:, 124:125], ps[5][:, 16:24], AX.X, ALU.max))
            step(TS(rt[:, 125:126], rt[:, 124:125], 128.5, 1.0, ALU.is_gt, ALU.add))
            dve.tensor_copy(npass_i[:], rt[0:1, 125:126]).then_inc(npass_ready, 1)
            dve.wait_ge(npass_ready, 1)
            npass = dve.value_load(npass_i[0:1, 0:1], min_val=1, max_val=2)
            dve.sem_clear(vec_order)
            step_no[0] = 0
            with dve.Fori(0, npass) as p:
                for t in range(TB):
                    step(TT(sel[:, t, :, :], C["iota"].unsqueeze(1).broadcast_to([P, EXPERTS + 1, P]),
                            slot[:, t, :].unsqueeze(2).broadcast_to([P, EXPERTS + 1, P]), ALU.is_equal))
                flat = htmp[:].rearrange("p k s -> p (k s)").rearrange("p (t e c) -> p t e c", t=TB, e=EXPERTS)
                for t in range(TB):
                    ins = TT(flat[:, t, :, :], sel[:, t, 0:EXPERTS, :],
                             comb[:, t, :].unsqueeze(2).broadcast_to([P, EXPERTS, P]), ALU.mult)
                    if t == 0:
                        step(ins)
                ins.then_inc(selw_ready, 1)
                step(TS(rt[:, 104:122], rt[:, 104:122], 128.0, None, ALU.subtract))

                def low_of_tokens(nth):
                    for b in range(2):
                        dve.wait_ge(xg_high, 2 * nth + b + 1)
                        TT(xgl[:, b * 512:(b + 1) * 512], ps[6 + b][:],
                           xgh[:, b * 512:(b + 1) * 512].bitcast(f32), ALU.subtract).then_inc(xg_ready, 1)

                low_of_tokens(p * 9)
                with dve.Fori(0, EXPERTS) as e:
                    it = p * EXPERTS + e
                    N3 = NEU // 3

                    def split(j):
                        g, part = EUNITS[j]
                        r = g % 3
                        dve.wait_ge(e_hi, it * NEU + j + 1)
                        if part == 2:
                            o, i = elo[:, j % 3, :], w2_at(r)
                            h = ehi[:, j % 3, :].bitcast(f32)
                        else:
                            o = elo[:, j % 3, :].rearrange("p (w n) -> p w n", w=2)
                            h = ehi[:, j % 3, :].bitcast(f32).rearrange("p (w n) -> p w n", w=2)
                            i = pair_at(r)[:, :, part * 1024:(part + 1) * 1024]
                        TT(o, i, h, ALU.subtract).then_inc(e_full[j % 3], 1)

                    split(0)
                    split(1)
                    for j, (g, part) in enumerate(EUNITS):
                        if j + 2 < NEU:
                            split(j + 2)
                        if part == 1:
                            dve.wait_ge(e_silu, it * EG + g + 1)
                            dve.wait_ge(e_turned, it * EG + g - 1 if g >= 2 else it * EG)
                            TT(glu[:, g % 2, :], sil[:, g % 2, :], ps[g % 2][:, 256:512], ALU.mult).then_inc(e_glu, 1)
                        if g >= 1 and part == 0 or j == NEU - 1:
                            h = g - 1 if part == 0 else g
                            dve.wait_ge(e_gth, it * EG + h + 1)
                            TT(gtl[:, h % 2, :], ps[2 + h % 2][:, 0:256], gth[:, h % 2, :].bitcast(f32),
                               ALU.subtract).then_inc(e_gtl, 1)
                        if part == 1 and g == EG - 1:
                            low_of_tokens(it + p + 1)
                    u, before = e_unit(EG - 1, 2)
                    dve.wait_ge(e_used[u], it * N3 + before + 1)
                    dve.wait_ge(scattered, 4 * it)
                    dve.tensor_copy(ysb[:, 512:1024], ps[5][:]).then_inc(y_kept, 1)
                    for q in range(4):
                        dve.wait_ge(scattered, 4 * it + q + 1)
                        for j in range(2):
                            m = 2 * q + j
                            ins = STT(xT[:, m, :], ps[6 + q % 2][:, j * 256:(j + 1) * 256], adav[:, 40 + m:41 + m],
                                      xT[:, m, :], ALU.mult, ALU.add)
                        ins.then_inc(x_added, 1)
                dve.sem_clear(vec_order)
                step_no[0] = 0

            dve.wait_ge(f_std, 1)
            step(dve.reciprocal(rstd[:], rstd[:]))
            for m in range(KB):
                ins = STT(htmp[:, m, :], xT[:, m, :], pv[:, ROW["final"] + m:ROW["final"] + m + 1], rstd[:],
                          ALU.mult, ALU.mult)
            ins.then_inc(f_scaled, 1)

        @block.gpsimd
        def _(pool):
            step_no = [0]
            pool.memset(rows[:], 0.0).then_inc(rows_cleared, 1)
            with pool.Fori(0, L) as l:
                def strictly_causal(buf):
                    for o in (0, 256):
                        ins = pool.affine_select(out=buf[:, o:o + 128], in_=buf[:, o:o + 128], pattern=[[1, 128]],
                                                 compare_op=ALU.is_gt, fill=0.0, base=0, channel_multiplier=-1)
                    return ins

                def step(ins):
                    step_no[0] += 1
                    ins.then_inc(pool_order, 1)
                    pool.wait_ge(pool_order, step_no[0])

                def sum_ada(i, half, acc, base):
                    h = ada_place(i, half)
                    w = ada_raw[:, h % 2]
                    pool.wait_ge(ada_full[h % 2], 16 * (base * (ADA_HALVES // 2) + h // 2 + 1))
                    carry(pool)
                    step(pool.tensor_tensor(w, w, cond[:, 4 * half:4 * half + 4].unsqueeze(2)
                                            .broadcast_to([P, 4, COLS]), ALU.mult))
                    step(pool.tensor_tensor(w[:, 0:2, :], w[:, 0:2, :], w[:, 2:4, :], ALU.add))
                    if half == 0:
                        ins = pool.tensor_tensor(acc, w[:, 0, :], w[:, 1, :], ALU.add)
                    else:
                        step(pool.tensor_tensor(w[:, 0, :], w[:, 0, :], w[:, 1, :], ALU.add))
                        pool.wait_ge(ada_summed, base * ADA_HALVES + h)
                        carry(pool)
                        ins = pool.tensor_tensor(acc, acc, w[:, 0, :], ALU.add)
                    ins.then_inc(ada_summed, 1)

                def mixer_ada(i):
                    if i in (8, 12, 16, 20):
                        if i == 8:
                            pool.wait_ge(h_split, 4 * l + 2)
                        else:
                            wait_unit(pool, f"adar{i // 4 - 3}", l)
                        carry(pool)
                    for half in range(2):
                        sum_ada(i, half, ada_sum[:, i % 4, :], l)

                pool.wait_ge(cond_ready, 1)
                carry(pool)
                mixer_ada(8)
                mixer_ada(9)
                for i in range(4):
                    pool.wait_ge(z_soft, 4 * l + i + 1)
                    carry(pool)
                    strictly_causal(prob[:, i % 2, :]).then_inc(z_masked, 1)
                    wait_sc_drained(pool, f"C{i}", l)
                    carry(pool)
                    strictly_causal(pT[:, i % 2, :]).then_inc(w_masked, 1)
                    if i < 2:
                        mixer_ada(10 + i)
                for i in range(12, 24):
                    mixer_ada(i)
                parts = 0
                for n in range(1, 4):
                    for q in range(4):
                        wait_drained(pool, f"wb{BRANCH_ORDER[n]}_{q}", l)
                        m = htmp[:, 2 * q:2 * q + 2, :]
                        pool.tensor_tensor(m, m, prob[:, parts % 2, :].rearrange("p (m s) -> p m s", m=2), ALU.add) \
                            .then_inc(merged if n == 3 else part_used, 1)
                        parts += 1
                with pool.If(l < 1):
                    for i in range(8):
                        for half in range(2):
                            sum_ada(i, half, ada_first[:, i, :], 0)
                pool.sem_clear(pool_order)
                step_no[0] = 0
            pool.nop().then_inc(mixer_over, 1)


def table():
    import numpy as np

    t = np.zeros((P, NCONST), np.float32)
    i, j = np.arange(P)[:, None], np.arange(P)[None, :]

    def put(name, v):
        lo, hi = CONST[name]
        t[:, lo:hi] = v

    put("ident", i == j)
    put("ntri", -1.0 * (i >= j))
    put("nones", -1.0)
    put("ones", 1.0)
    put("blk", i // 64 == j // 64)
    put("strict", i < j)
    put("iota", j)
    put("dist", np.concatenate([-(128.0 + i - j), np.where(j <= i, -(i - j), NEG)], 1))
    put("causal", np.concatenate([np.zeros((P, P)), np.where(j <= i, 0.0, NEG)], 1))
    rot = np.zeros((P, 32), np.float32)
    for d in range(16):
        rot[64 + 16 + d, d] = -1.0
        rot[64 + d, 16 + d] = 1.0
    put("rot", rot)
    inv = np.zeros((P, 1), np.float32)
    inv[64:96, 0] = 10000.0 ** (-(np.arange(32) % 16) / 16.0)
    put("inv", inv)
    put("eps", EPS)
    put("half_pi", math.pi / 2)
    lam = [0.8 - 0.6 * math.exp(-0.3 * l) for l in range(L)]
    rows = np.array([[[1.0 - v] * P, [v] * P] for v in lam], np.float32)
    return t, rows


_INS = ["x", "c", "positions", "ada_w", "ada_b", "norm1_g", "norm2_g", "w_in", "mla_q_norm_g", "mla_kv_norm_g",
        "mla_w_uq", "mla_w_ukv", "diff_lq1", "diff_lk1", "diff_lq2", "diff_lk2", "diff_norm_g", "w_branch", "w_out",
        "ffn_w1", "ffn_w3", "ffn_w2", "router_w", "router_b", "moe_w1", "moe_w3", "moe_w2", "final_norm_g"]


def kernel(**inputs):
    import numpy as np
    import concourse.bacc as bacc
    from concourse.bass_utils import run_bass_kernel_spmd

    nc = bacc.Bacc("TRN2", target_bir_lowering=False, num_devices=1)
    arrays = {n: np.ascontiguousarray(inputs[n]) for n in _INS}
    arrays["consts"], arrays["lam_rows"] = table()
    args = {}
    for n, v in arrays.items():
        args[n] = nc.dram_tensor(f"in_{n}", v.shape, mybir.dt.from_np(v.dtype), kind="ExternalInput").ap()
    out = nc.dram_tensor("out_x", (1, SEQ, D), mybir.dt.float32, kind="ExternalOutput").ap()
    trunk(nc, args, out)
    r = run_bass_kernel_spmd(nc, [{f"in_{n}": v for n, v in arrays.items()}], core_ids=[0])
    return r.results[0]["out_x"]
```

```python
import math
from contextlib import ExitStack

import concourse.bass as bass
from concourse import mybir
from concourse.alu_op_type import AluOpType as ALU

P = 128
D = 1024
KB = D // P
SEQ = 256
TB = SEQ // P
L = 2
COLS = 256
HEADS = 4
EXPERTS = 8
TOPK = 64
D_FF = 2816
FFE = 3584
FG = D_FF // COLS
EG = FFE // COLS
EPS = 1e-6
NEG = -1e30
TAKEN = -3e38

NAMES = ("aq", "ak", "av", "iq", "ik", "iw", "cq", "ckv", "kr", "sq", "sk", "sv", "dq", "dk", "dv", "gates")
SIZES = (256, 64, 64, 256, 64, 4, 256, 128, 32, 256, 256, 256, 256, 256, 256, 4096)
COL = {n: sum(SIZES[:i]) for i, n in enumerate(NAMES)}

CONST = {}
_at = 0
for _n, _w in (("ident", 128), ("ntri", 128), ("nones", 128), ("ones", 128), ("blk", 128), ("strict", 128),
               ("iota", 128), ("dist", 256), ("causal", 256), ("rot", 32), ("inv", 1), ("eps", 1),
               ("half_pi", 1)):
    CONST[_n] = (_at, _at + _w)
    _at += _w
NCONST = _at

ROW = {"ada_b": 0, "norm1": 48, "norm2": 56, "qn": 64, "kvn": 66, "c": 67, "final": 75, "diff": 83,
       "lq1": 84, "lk1": 85, "lq2": 86, "lk2": 87, "one_minus_lam": 88, "lam_init": 89}
NROW = 90

ATT = [("C", h) for h in range(4)] + [("B", i) for i in range(3)] + [("D", i) for i in range(6)] \
    + [("A", i) for i in range(3)]
NATT = len(ATT)
NSM = NATT - 4
BRANCH_ORDER = ("C", "B", "D", "A")
BRANCH_N = {"A": 0, "B": 1, "C": 2, "D": 3}


def head_cols(unit):
    b, i = unit
    if b == "D":
        return (0, 128, range(4 * i, 4 * i + 4)) if i < 2 else (128, 256, range(2 * (i - 2), 2 * (i - 2) + 2))
    return (0, 128, (0, 2, 1, 3)) if i == 0 else (128, 256, (i - 1, i + 1))


PRE = ["params", "stats1", "lam", "ada_a", "iq", "ik", "cq", "ckv", "@I0", "sq", "@I1", "sk", "@I2", "mla_stats"]
FILL = {0: ["sv", "uq01", "uk01", "dq"], 1: ["uq23", "dk", "uk23"], 2: ["aq", "rot01", "rot23"],
        3: ["dv", "rotk", "uv"], 4: ["ak"]}
GATES = [f"gate{4 * BRANCH_N[b] + i}" for b in BRANCH_ORDER for i in range(4)]
_g = 0
for _t in range(4, NATT + 2):
    FILL.setdefault(_t, []).append(GATES[_g])
    _g += 1
    if _t in (7, 13):
        FILL[_t].append(GATES[_g])
        _g += 1
assert _g == 16
for _i, _t in enumerate((5, 8, 11, 15)):
    FILL[_t].append(f"adar{_i}")
FILL[16] += ["dstats", "wbC_0", "wbC_1", "wbC_2", "wbC_3"]
FILL[17] += ["wbB_0", "wbB_1", "wbB_2", "wbB_3"]
POST = [f"wb{n}_{q}" for n in "DA" for q in range(4)] + [f"wo{i}" for i in range(4)] + ["stats2"]
UNITS = [u for u in PRE if u[0] != "@"] + [u for t in sorted(FILL) for u in FILL[t]]
UNITS += POST
assert len(set(UNITS)) == len(UNITS)

FIRST_PE = (1, 4, 6)
FIRST_DVE = tuple(i for i in range(8) if i not in FIRST_PE)
ADA_ORDER = list(range(8, 24)) + list(range(8))
ADA_HALVES = 2 * len(ADA_ORDER)


def chunks_of(unit):
    if unit[:2] == "wb":
        return [unit[:3]] if unit[-1] == "0" else []
    plain = ("iq", "ik", "cq", "ckv", "sq", "sk", "sv", "dq", "dk", "dv", "aq", "ak")
    return [unit] if unit in plain or unit[:4] == "gate" or unit[:2] == "wo" else []


MIX_CHUNKS = [c for u in UNITS for c in chunks_of(u)]
FFN_CHUNKS = ["w1_0", "w3_0"]
for _i in range(1, FG):
    FFN_CHUNKS += [f"w1_{_i}", f"w3_{_i}", f"w2_{_i - 1}"]
FFN_CHUNKS.append(f"w2_{FG - 1}")
CHUNKS = MIX_CHUNKS + FFN_CHUNKS
NMIX = len(MIX_CHUNKS)
SPLITS = CHUNKS
RAW = 3
HALVES = 4


def last_of_unit(unit):
    if unit[:2] == "wb":
        return unit[:3] if unit[-1] == "3" else None
    c = chunks_of(unit)
    return c[-1] if c else None


SIGNALLED = [u for u in UNITS if last_of_unit(u) is None]
SC_UNITS = ["I0", "I1", "I2"] + [f"{b}{i}" for b, i in ATT]


def n_of(items, ring, at):
    return len(range(at, items, ring))


def trunk(nc, a, out):
    f32, f32r, i32, u32 = mybir.dt.float32, mybir.dt.float32r, mybir.dt.int32, mybir.dt.uint32
    ACT = mybir.ActivationFunctionType
    AX = mybir.AxisListType

    ctx = ExitStack()
    mix = ExitStack()
    with ctx:
        def sem(name):
            return ctx.enter_context(nc.semaphore(name))

        def sb(name, shape, dt=f32, at=ctx):
            return at.enter_context(nc.sbuf_tensor(name, shape, dt))

        const = sb("const", [P, NCONST])
        C = {n: const[:, lo:hi] for n, (lo, hi) in CONST.items()}
        xT = sb("xT", [P, KB, SEQ])
        htmp = sb("htmp", [P, KB, SEQ])
        hh = sb("hh", [P, KB, SEQ], f32r)
        hl = sb("hl", [P, KB, SEQ], f32r)
        raw = sb("raw", [P, RAW, 2048])
        rows = sb("rows", [P, P])
        pv = sb("pv", [P, NROW])
        adav = sb("adav", [P, 48])
        cond = sb("cond", [P, KB])
        hscale = sb("hscale", [P, KB])
        rstd = sb("rstd", [P, SEQ])
        router_w = sb("router_w", [P, KB, EXPERTS])
        router_b = sb("router_b", [1, EXPERTS])
        npass_i = sb("npass_i", [1, 1], i32)

        def mx(name, shape, dt=f32):
            return sb(name, shape, dt, mix)

        shi = mx("shi", [P, HALVES, 1024], f32r)
        slo = mx("slo", [P, HALVES, 1024], f32r)
        gates = mx("gates", [P, 32, SEQ])
        iqT = mx("iqT", [P, 2, SEQ])
        ikT = mx("ikT", [P, SEQ])
        iw = mx("iw", [P, TB, HEADS])
        aqT = mx("aqT", [P, 2, SEQ])
        akT = mx("akT", [P, SEQ])
        avt = mx("avt", [P, TB, 64])
        cqT = mx("cqT", [P, 2, SEQ])
        ckvT = mx("ckvT", [P, SEQ])
        part0 = mx("part0", [P, 2, SEQ])
        part1 = mx("part1", [P, 2, SEQ])
        krT = part1[:, 0, :]
        krr = part1[:, 1, :]
        sqT = mx("sqT", [P, 2, SEQ])
        skT = mx("skT", [P, 2, SEQ])
        svt = mx("svt", [P, TB, 256])
        dvt = mx("dvt", [P, TB, 256])
        mqT = mx("mqT", [96, HEADS, SEQ])
        mkT = mx("mkT", [96, HEADS, SEQ])
        mvt = mx("mvt", [P, TB, 256])
        uq = mx("uq", [P, 2, 384])
        ukv = mx("ukv", [P, 512])
        ada_raw = mx("ada_raw", [P, 2, 4, COLS])
        ada_sum = htmp
        ada_first = gates[:, 0:8, :]
        yh = mx("yh", [P, 4, 512], f32r)
        yl = mx("yl", [P, 4, 512], f32r)
        pd = mx("pd", [P, 4, 512])
        prob = pd[:, 0:2, :]
        diag = pd[:, 2:4, :]
        pT = mx("pT", [P, 2, 512])
        score = mx("score", [P, 384])
        work = mx("work", [P, 384])
        cosT = mx("cosT", [P, SEQ])
        sinT = mx("sinT", [P, SEQ])
        tmpA = mx("tmpA", [P, 512])
        small = mx("small", [P, 48])
        dqT, dkT = iqT, cqT
        gh, gl = yh, yl

        ps = [ctx.enter_context(nc.psum_tensor(f"ps{i}", [P, 512], f32)) for i in range(8)]
        SCB, TPB, YB = 2, 4, 6

        start_loaded = sem("start_loaded")
        rows_cleared = sem("rows_cleared")
        rows_loaded = sem("rows_loaded")
        small_w_loaded = sem("small_w_loaded")
        x_turned = sem("x_turned")
        x_kept = sem("x_kept")
        rope_arg = sem("rope_arg")
        rope_ready = sem("rope_ready")
        raw_full = [sem(f"raw_full{i}") for i in range(RAW)]
        first_full = [sem(f"first_full{i}") for i in range(8)]
        first_summed = sem("first_summed")
        first_taken = sem("first_taken")
        ada_full = [sem(f"ada_full{i}") for i in range(2)]
        ada_summed = sem("ada_summed")
        hi_done = sem("hi_done")
        split_full = [sem(f"split_full{i}") for i in range(HALVES)]
        split_used = [sem(f"split_used{i}") for i in range(HALVES)]
        acc_full = sem("acc_full")
        acc_free = [sem(f"acc_free{i}") for i in range(2)]
        sc_full = sem("sc_full")
        sc_free = [sem(f"sc_free{i}") for i in range(2)]
        squares = sem("squares")
        params_ready = sem("params_ready")
        cond_ready = sem("cond_ready")
        lamprod_ready = sem("lamprod_ready")
        h_ready = sem("h_ready")
        h_high = sem("h_high")
        h_split = sem("h_split")
        q_roped = sem("q_roped")
        k_roped = sem("k_roped")
        lat_squares = sem("lat_squares")
        lat_normed = sem("lat_normed")
        relu_used = sem("relu_used")
        z_log = sem("z_log")
        z_masked = sem("z_masked")
        z_summed = sem("z_summed")
        w_masked = sem("w_masked")
        max_ready = sem("max_ready")
        exp_ready = sem("exp_ready")
        diag_ready = sem("diag_ready")
        turned = sem("turned")
        turned_kept = sem("turned_kept")
        values_done = sem("values_done")
        y_squared = sem("y_squared")
        y_float = sem("y_float")
        y_high = sem("y_high")
        y_split = sem("y_split")
        part_used = sem("part_used")
        merged = sem("merged")
        m_high = sem("m_high")
        m_split = sem("m_split")
        down_done = sem("down_done")
        up_free = [sem(f"up_free{i}") for i in range(4)]
        glu_high = sem("glu_high")
        glu_split = sem("glu_split")
        x_fed = sem("x_fed")
        vec_order = sem("vec_order")
        first_order = sem("first_order")
        pe_order = sem("pe_order")
        act_order = sem("act_order")
        pool_order = sem("pool_order")
        mixer_over = sem("mixer_over")

        passed = sem("passed")

        def carry(eng):
            eng.sem_inc(passed, 1)

        BEGUN = 4

        def dmas(c):
            return {"ak": 2, "ik": 2}.get(c, 1)

        def raw_place(c):
            i = CHUNKS.index(c)
            mine = [x for x in CHUNKS[i % RAW::RAW]]
            return i % RAW, 16 * sum(dmas(x) for x in mine[:i // RAW + 1]), 16 * sum(dmas(x) for x in mine)

        def half_place(c, half):
            h = 2 * SPLITS.index(c) + half
            return h % HALVES, h // HALVES, n_of(2 * len(SPLITS), HALVES, h % HALVES)

        def width(c):
            return {"ik": 132, "ak": 192, "ckv": 192}.get(c, COLS)

        def wait_unit(eng, unit, l):
            c = last_of_unit(unit)
            if c is None:
                eng.wait_ge(acc_full, l * len(SIGNALLED) + SIGNALLED.index(unit) + 1)
            else:
                u, before, total = half_place(c, 1)
                eng.wait_ge(split_used[u], l * total + before + 1 + BEGUN)

        def bank_of(unit):
            i = UNITS.index(unit)
            return i % 2, i // 2, n_of(len(UNITS), 2, i % 2)

        def wait_acc_free(eng, unit, l):
            b, before, total = bank_of(unit)
            eng.wait_ge(acc_free[b], l * total + before + BEGUN)
            return ps[b]

        def wait_drained(eng, unit, l):
            b, before, total = bank_of(unit)
            eng.wait_ge(acc_free[b], l * total + before + 1 + BEGUN)

        def wait_all_drained(eng, units, l):
            for bank in range(2):
                mine = [u for u in units if bank_of(u)[0] == bank]
                if mine:
                    wait_drained(eng, max(mine, key=UNITS.index), l)

        def sc_place(name):
            i = SC_UNITS.index(name)
            return i % 2, i // 2, n_of(len(SC_UNITS), 2, i % 2)

        def wait_scores(eng, name, l):
            eng.wait_ge(sc_full, l * len(SC_UNITS) + SC_UNITS.index(name) + 1)

        def wait_sc_drained(eng, name, l):
            b, before, total = sc_place(name)
            eng.wait_ge(sc_free[b], l * total + before + 1 + BEGUN)

        def scores_read(ins, name):
            ins.then_inc(sc_free[sc_place(name)[0]], 1)

        def read_out(ins, unit):
            ins.then_inc(acc_free[bank_of(unit)[0]], 1)

        def split_high(act, c, l):
            slot, arrived, total = raw_place(c)
            n = 4 * width(c)
            for half in range(2):
                u, before, used = half_place(c, half)
                if half == 0:
                    act.wait_ge(raw_full[slot], l * total + arrived)
                act.wait_ge(split_used[u], l * used + before + BEGUN)
                act.copy(shi[:, u, 0:n], raw[:, slot, half * n:(half + 1) * n]).then_inc(hi_done, 1)

        def split_low(dve, c, l):
            slot, _, _ = raw_place(c)
            n = 4 * width(c)
            for half in range(2):
                u, _, _ = half_place(c, half)
                h = 2 * SPLITS.index(c) + half
                dve.wait_ge(hi_done, l * 2 * len(SPLITS) + h + 1)
                dve.tensor_tensor(slo[:, u, 0:n], raw[:, slot, half * n:(half + 1) * n],
                                  shi[:, u, 0:n].bitcast(f32), ALU.subtract).then_inc(split_full[u], 1)

        w_in = a["w_in"].rearrange("l (k p) n -> l p k n", p=P)
        ada_w = a["ada_w"].rearrange("l (k p) n -> l p k n", p=P)
        w_out = a["w_out"].rearrange("l (k p) n -> l p k n", p=P)
        w_branch = a["w_branch"].rearrange("l b (k p) n -> l b p k n", p=P)
        f1 = a["ffn_w1"].rearrange("l (k p) n -> l p k n", p=P)
        f3 = a["ffn_w3"].rearrange("l (k p) n -> l p k n", p=P)
        f2 = a["ffn_w2"].rearrange("l (g k p) n -> l g p k n", p=P, k=2)
        m1 = a["moe_w1"].rearrange("l e (k p) n -> (l e) p k n", p=P)
        m3 = a["moe_w3"].rearrange("l e (k p) n -> (l e) p k n", p=P)
        m2 = a["moe_w2"].rearrange("l e (g k p) n -> (l e) g p k n", p=P, k=2)

        def sources(c, l):
            if c[:4] == "gate":
                i = COL["gates"] + int(c[4:]) * COLS
                return [(0, w_in[l, :, :, i:i + COLS])]
            if c[:2] == "wo":
                i = int(c[2:]) * COLS
                return [(0, w_out[l, :, :, i:i + COLS])]
            if c in ("ak", "ik"):
                i = COL[c]
                return [(0, w_in[l, :, :, i:i + 64]), (64, w_in[l, :, :, i:i + width(c) - 64])]
            return [(0, w_in[l, :, :, COL[c]:COL[c] + width(c)])]

        def first_at(i):
            if i < 3 or i == 7:
                place = raw[:, min(i, 2), :]
            elif i < 6:
                place = gates[:, 8 * i - 16:8 * i - 8, :].rearrange("p k s -> p (k s)")
            else:
                place = pd[:].rearrange("p n s -> p (n s)")
            return place.rearrange("p (k n) -> p k n", k=KB)

        def wait_first_used(eng, i):
            if i in FIRST_PE:
                eng.wait_ge(first_taken, FIRST_PE.index(i) + 1)
            else:
                eng.wait_ge(first_summed, FIRST_DVE.index(i) + 1)

        def load_chunk(sp, c, l):
            slot, _, _ = raw_place(c)
            i = CHUNKS.index(c)
            if i >= RAW:
                u, before, total = half_place(CHUNKS[i - RAW], 1)
                sp.wait_ge(split_full[u], l * total + before + 1)
                carry(sp)
            else:
                wait_first_used(sp, (0, 1, 7)[i])
                carry(sp)
            if c[:2] == "wb":
                sp.dma_start(raw[:, slot, :].rearrange("p (k n) -> p k n", k=2),
                             w_branch[l, BRANCH_N[c[2]]]).then_inc(raw_full[slot], 16)
            elif c[:2] == "w2":
                sp.dma_start(raw[:, slot, :].rearrange("p (k n) -> p k n", k=2),
                             f2[0, int(c[3:])]).then_inc(raw_full[slot], 16)
            elif c[:2] in ("w1", "w3"):
                i = int(c[3:]) * COLS
                src = (f1 if c[:2] == "w1" else f3)[0, :, :, i:i + COLS]
                sp.dma_start(raw[:, slot, :].rearrange("p (k n) -> p k n", k=KB), src).then_inc(raw_full[slot], 16)
            else:
                dst = raw[:, slot, 0:KB * width(c)].rearrange("p (k n) -> p k n", k=KB)
                for at, src in sources(c, l):
                    sp.dma_start(dst[:, :, at:at + src.shape[2]], src).then_inc(raw_full[slot], 16)

        def ada_place(i, half):
            return 2 * ADA_ORDER.index(i) + half

        mix.close()
        moe = ctx
        ehi = sb("ehi", [P, 3, 2048], f32r, moe)
        elo = sb("elo", [P, 3, 2048], f32r, moe)
        raw_more = sb("raw_more", [P, 6, 2048], f32, moe)
        sel = sb("sel", [P, TB, EXPERTS + 1, P], f32, moe)
        selT = sb("selT", [P, EXPERTS + 1, SEQ], f32, moe)
        htok = sb("htok", [P, TB, D], f32, moe)
        gth = sb("gth", [P, 2, 256], f32r, moe)
        gtl = sb("gtl", [P, 2, 256], f32r, moe)
        sil = sb("sil", [P, 2, 256], f32, moe)
        glu = sb("glu", [P, 2, 256], f32, moe)
        ysb = sb("ysb", [P, D], f32, moe)
        rt = sb("rt", [P, 160], f32, moe)
        xgh = hh[:].rearrange("p k s -> p (k s)")[:, 0:1024]
        xgl = hl[:].rearrange("p k s -> p (k s)")[:, 0:1024]
        rtu = sb("rtu", [P, TB, 8], u32, moe)
        htok_turned = sem("htok_turned")
        htok_ready = sem("htok_ready")
        logits_done = sem("logits_done")
        gap_ready = sem("gap_ready")
        gapexp_ready = sem("gapexp_ready")
        mask_ready = sem("mask_ready")
        rank_done = sem("rank_done")
        npass_ready = sem("npass_ready")
        sel_ready = sem("sel_ready")
        selw_ready = sem("selw_ready")
        selw_turned = sem("selw_turned")
        selT_ready = sem("selT_ready")
        pair_full = [sem(f"pair_full{i}") for i in range(3)]
        e2_full = [sem(f"e2_full{i}") for i in range(3)]
        e_hi = sem("e_hi")
        e_full = [sem(f"e_full{i}") for i in range(3)]
        e_used = [sem(f"e_used{i}") for i in range(3)]
        gathered = sem("gathered")
        xg_high = sem("xg_high")
        xg_ready = sem("xg_ready")
        e_silu = sem("e_silu")
        e_glu = sem("e_glu")
        e_turned = sem("e_turned")
        e_gth = sem("e_gth")
        e_gtl = sem("e_gtl")
        y_kept = sem("y_kept")
        scattered = sem("scattered")
        x_added = sem("x_added")
        f_std = sem("f_std")
        f_scaled = sem("f_scaled")
        f_turned = sem("f_turned")
        f_kept = [sem(f"f_kept{t}") for t in range(TB)]
        out_stored = sem("out_stored")

        EUNITS = [(0, 0), (0, 1)]
        for g in range(1, EG):
            EUNITS += [(g, 0), (g, 1), (g - 1, 2)]
        EUNITS.append((EG - 1, 2))
        NEU = len(EUNITS)

        def pair_at(i):
            return raw[:, 0:2, :] if i == 0 else raw_more[:, 2 * i - 2:2 * i, :]

        def w2_at(i):
            return raw[:, 2, :] if i == 0 else raw_more[:, 3 + i, :]

        def e_unit(g, part):
            j = EUNITS.index((g, part))
            return j % 3, j // 3

        GPS = [n_of(EG, 3, i) for i in range(3)]

        def load_expert(sp, e, it, very_first=False):
            for j, (g, part) in enumerate(EUNITS):
                r = g % 3
                if part == 0:
                    if g >= 3:
                        u, before = e_unit(g - 3, 1)
                        sp.wait_ge(e_full[u], it * (NEU // 3) + before + 1)
                    elif not very_first:
                        u, before = e_unit(max(range(r, EG, 3)), 1)
                        sp.wait_ge(e_full[u], (it - 1) * (NEU // 3) + before + 1)
                    elif g == 1:
                        sp.wait_ge(m_split, 4 * L)
                    for n, w in enumerate((m1, m3)):
                        sp.dma_start(pair_at(r)[:, n, :].rearrange("p (k n) -> p k n", k=KB),
                                     w[e, :, :, g * COLS:(g + 1) * COLS]).then_inc(pair_full[r], 16)
                elif part == 2:
                    if g >= 3:
                        u, before = e_unit(g - 3, 2)
                        sp.wait_ge(e_full[u], it * (NEU // 3) + before + 1)
                    elif not very_first:
                        u, before = e_unit(max(range(r, EG, 3)), 2)
                        sp.wait_ge(e_full[u], (it - 1) * (NEU // 3) + before + 1)
                    sp.dma_start(w2_at(r).rearrange("p (k n) -> p k n", k=2), m2[e, g]).then_inc(e2_full[r], 16)

        block = ctx.enter_context(nc.Block())

        @block.sync
        def _(sp):
            sp.dma_start(const[:], a["consts"]).then_inc(start_loaded, 16)
            sp.dma_start(htmp[:].rearrange("p k s -> p (k s)").rearrange("p (t d) -> p t d", t=TB),
                         a["x"].rearrange("b (t p) d -> p (b t) d", p=P)).then_inc(start_loaded, 16)
            sp.dma_start(cosT[64:96, :].bitcast(i32),
                         a["positions"].broadcast_to([32, SEQ])).then_inc(start_loaded, 16)
            sp.wait_ge(rows_cleared, 1)
            with sp.Fori(0, L) as l:
                with sp.If(l > 0):
                    sp.wait_ge(params_ready, 1)

                def row(name, n, src):
                    sp.dma_start(rows[ROW[name]:ROW[name] + n, 0:src.shape[1]], src).then_inc(rows_loaded, 16)

                row("c", 8, a["c"].rearrange("b (n p) -> (b n) p", p=P))
                row("norm1", 8, a["norm1_g"][l].rearrange("(n p) -> n p", p=P))
                row("ada_b", 48, a["ada_b"][l].rearrange("(n p) -> n p", p=P))
                row("norm2", 8, a["norm2_g"][l].rearrange("(n p) -> n p", p=P))
                row("qn", 2, a["mla_q_norm_g"][l].rearrange("(n p) -> n p", p=P))
                row("kvn", 1, a["mla_kv_norm_g"][l].rearrange("(n p) -> n p", p=P))
                row("final", 8, a["final_norm_g"].rearrange("(n p) -> n p", p=P))
                row("lq1", 1, a["diff_lq1"][l].rearrange("(n p) -> n p", n=1))
                row("lk1", 1, a["diff_lk1"][l].rearrange("(n p) -> n p", n=1))
                row("lq2", 1, a["diff_lq2"][l].rearrange("(n p) -> n p", n=1))
                row("lk2", 1, a["diff_lk2"][l].rearrange("(n p) -> n p", n=1))
                row("one_minus_lam", 2, a["lam_rows"][l])
                for half in range(2):
                    r = ROW["diff"]
                    sp.dma_start(rows[r:r + 1, 64 * half:64 * half + 64],
                                 a["diff_norm_g"][l].rearrange("(n p) -> n p", n=1)).then_inc(rows_loaded, 16)
                with sp.If(l < 1):
                    for i in range(8):
                        if i == 7:
                            wait_first_used(sp, 2)
                        sp.dma_start(first_at(i), ada_w[0, :, :, i * COLS:(i + 1) * COLS]).then_inc(first_full[i], 16)
                with sp.If(l > 0):
                    for u in range(HALVES):
                        sp.wait_ge(split_full[u], n_of(2 * len(SPLITS), HALVES, u))
                for c in MIX_CHUNKS:
                    if c == "cq":
                        with sp.If(l > 0):
                            sp.wait_ge(values_done, NATT)
                        sp.dma_start(uq[:], a["mla_w_uq"][l].rearrange("(k p) n -> p k n", p=P)) \
                            .then_inc(small_w_loaded, 16)
                        sp.dma_start(ukv[:], a["mla_w_ukv"][l]).then_inc(small_w_loaded, 16)
                    load_chunk(sp, c, l)
                with sp.If(l < 1):
                    for c in FFN_CHUNKS:
                        load_chunk(sp, c, 0)
            sp.dma_start(router_w[:], a["router_w"].rearrange("l (k p) n -> p (l k) n", p=P)) \
                .then_inc(small_w_loaded, 16)
            sp.dma_start(router_b[:], a["router_b"]).then_inc(small_w_loaded, 16)
            for u in range(HALVES):
                sp.wait_ge(split_full[u], n_of(2 * len(SPLITS), HALVES, u) + n_of(2 * NMIX, HALVES, u))
            load_expert(sp, 0, 0, True)
            with sp.Fori(1, EXPERTS) as e:
                load_expert(sp, e, e)
            sp.wait_ge(npass_ready, 1)
            npass = sp.value_load(npass_i[0:1, 0:1], min_val=1, max_val=2)
            with sp.If(npass > 1):
                with sp.Fori(0, EXPERTS) as e2:
                    load_expert(sp, e2, e2 + EXPERTS)
            for b in range(2):
                for t in range(TB):
                    sp.wait_ge(f_kept[t], b + 1)
                sp.dma_start(out.rearrange("b (t p) d -> p (b t) d", p=P)[:, :, b * 512:b * 512 + 512],
                             htok[:, :, b * 512:b * 512 + 512]).then_inc(out_stored, 16)
            sp.wait_ge(out_stored, 32)

        @block.tensor
        def _(pe):
            mm = pe.matmul

            def three(outp, w_hi, w_lo, x_hi, x_lo, first, last, weights_still=True):
                for n, (w, x) in enumerate(((w_hi, x_hi), (w_hi, x_lo), (w_lo, x_hi)) if weights_still else
                                           ((w_hi, x_hi), (w_lo, x_hi), (w_hi, x_lo))):
                    lhs, rhs = (w, x) if weights_still else (x, w)
                    ins = mm(outp, lhs, rhs, start=first and n == 0, stop=last and n == 2, skip_group_check=True)
                return ins

            pe.wait_ge(start_loaded, 48)
            xtok = htmp[:].rearrange("p k s -> p (k s)").rearrange("p (t d) -> p t d", t=TB)
            for b in range(4):
                for j in range(2):
                    for t in range(TB):
                        k = 2 * b + j
                        ins = pe.transpose(ps[b][:, j * 256 + t * 128:j * 256 + (t + 1) * 128],
                                           xtok[:, t, k * 128:(k + 1) * 128], C["ident"])
                ins.then_inc(x_turned, 1)
            pe.wait_ge(x_kept, 4)

            with pe.Fori(0, L) as l:
                def chunk_product(unit, c, parts):
                    acc = wait_acc_free(pe, unit, l)
                    w = width(c)
                    first = True
                    for half in range(2):
                        u, before, total = half_place(c, half)
                        pe.wait_ge(split_full[u], l * total + before + 1)
                        for n, ((o0, o1), kind, (c0, c1), t) in enumerate(parts):
                            for kk in range(4):
                                k = 4 * half + kk
                                if n == 0 and k % 2 == 0:
                                    if c == "iq":
                                        pe.wait_ge(h_split, 8 * l + k // 2 + 1)
                                    if c == "wo0":
                                        pe.wait_ge(m_split, 4 * l + k // 2 + 1)
                                whi = shi[:, u, kk * w + c0:kk * w + c1]
                                wlo = slo[:, u, kk * w + c0:kk * w + c1]
                                if kind == "feat":
                                    ins = three(acc[:, o0:o1], whi, wlo, hh[:, k, :], hl[:, k, :],
                                                first, k == KB - 1)
                                else:
                                    ts = slice(t * 128, (t + 1) * 128)
                                    ins = three(acc[:, o0:o1], whi, wlo, hh[:, k, ts], hl[:, k, ts],
                                                first, k == KB - 1, False)
                                first = False
                        ins.then_inc(split_used[u], 1)

                two = [((0, 256), "feat", (0, 128), 0), ((256, 512), "feat", (128, 256), 0)]
                PARTS = {
                    "ik": [((0, 256), "feat", (0, 128), 0), ((256, 260), "tok", (128, 132), 0),
                           ((260, 264), "tok", (128, 132), 1)],
                    "ak": [((0, 256), "feat", (0, 128), 0), ((256, 320), "tok", (128, 192), 0),
                           ((320, 384), "tok", (128, 192), 1)],
                    "ckv": [((0, 256), "feat", (0, 128), 0), ((256, 512), "feat", (64, 192), 0)],
                    "sv": [((0, 256), "tok", (0, 256), 0), ((256, 512), "tok", (0, 256), 1)],
                }
                PARTS["dv"] = PARTS["sv"]

                def ada(acc, sums):
                    for n, chunk in sums:
                        for j in range(2):
                            ins = mm(acc[:, 2 * n + j:2 * n + j + 1], chunk[:, j * 128:(j + 1) * 128],
                                     C["ones"][:, 0:1], start=True, stop=True)
                    ins.then_inc(acc_full, 1)

                def ada_whole(acc, n):
                    pe.wait_ge(first_full[n], 16)
                    w = first_at(n)
                    for j in range(2):
                        for k in range(KB):
                            ins = mm(acc[:, 2 * n + j:2 * n + j + 1], w[:, k, j * 128:(j + 1) * 128],
                                     cond[:, k:k + 1], start=k == 0, stop=k == KB - 1)
                    ins.then_inc(first_taken, 1)

                def stats(acc, norm, i):
                    pe.wait_ge(squares, 8 * l + 4 * norm + i + 1)
                    for k in (2 * i, 2 * i + 1):
                        ins = mm(acc[:, 0:256], C["ones"], htmp[:, k, :], start=k == 0, stop=k == KB - 1)
                    if i == 3:
                        ins.then_inc(acc_full, 1)

                def unit(name):
                    if name == "params":
                        acc = wait_acc_free(pe, name, l)
                        pe.wait_ge(rows_loaded, (l + 1) * 14 * 16)
                        pe.transpose(acc[:, 0:P], rows[:], C["ident"]).then_inc(acc_full, 1)
                    elif name == "stats1":
                        acc = wait_acc_free(pe, name, l)
                        for i in range(4):
                            stats(acc, 0, i)
                    elif name == "stats2":
                        stats(ps[YB], 1, 3)
                    elif name == "ada_a":
                        acc = wait_acc_free(pe, name, l)
                        carry(pe)
                        with pe.If(l < 1):
                            pe.wait_ge(cond_ready, 1)
                            for n in FIRST_PE:
                                ada_whole(acc, n)
                            pe.wait_ge(first_summed, len(FIRST_DVE))
                            ada(acc, [(n, ada_first[:, n, :]) for n in FIRST_DVE])
                        with pe.If(l > 0):
                            pe.wait_ge(ada_summed, ADA_HALVES)
                            ada(acc, [(n, ada_first[:, n, :]) for n in range(8)])
                    elif name[:4] == "adar":
                        acc = wait_acc_free(pe, name, l)
                        pe.wait_ge(ada_summed, l * ADA_HALVES + 8 * (int(name[4:]) + 1))
                        ada(acc, [(n, ada_sum[:, 4 * (int(name[4:]) % 2) + n, :]) for n in range(4)])
                    elif name == "lam":
                        acc = wait_acc_free(pe, name, l)
                        pe.wait_ge(lamprod_ready, l + 1)
                        mm(acc[:, 0:2], C["ones"][0:32, :], small[0:32, 0:2], start=True, stop=True).then_inc(acc_full, 1)
                    elif name == "mla_stats":
                        acc = wait_acc_free(pe, name, l)
                        pe.wait_ge(lat_squares, l + 1)
                        mm(acc[:, 0:256], C["ones"], tmpA[:, 0:256], start=True, stop=False)
                        mm(acc[:, 0:256], C["ones"], tmpA[:, 256:512], start=False, stop=True)
                        mm(acc[:, 256:512], C["ones"], krT, start=True, stop=True).then_inc(acc_full, 1)
                    elif name[:2] == "uq":
                        acc = wait_acc_free(pe, name, l)
                        if name == "uq01":
                            pe.wait_ge(small_w_loaded, 32 * (l + 1))
                            pe.wait_ge(lat_normed, l + 1)
                        for j in range(2):
                            h = int(name[2 + j])
                            for k in range(2):
                                ins = mm(acc[0:96, j * 256:(j + 1) * 256], uq[:, k, h * 96:(h + 1) * 96],
                                         cqT[:, k, :], start=k == 0, stop=k == 1)
                        ins.then_inc(acc_full, 1)
                    elif name in ("uk01", "uk23"):
                        acc = wait_acc_free(pe, name, l)
                        for j in range(2):
                            h = int(name[2 + j])
                            ins = mm(acc[0:64, j * 256:(j + 1) * 256], ukv[:, h * 128:h * 128 + 64], ckvT[:],
                                     start=True, stop=True)
                        ins.then_inc(acc_full, 1)
                    elif name == "uv":
                        acc = wait_acc_free(pe, name, l)
                        v = ukv[:].rearrange("p (h two d) -> p h two d", h=HEADS, two=2)[:, :, 1, :]
                        for t in range(TB):
                            ins = mm(acc[:, t * 256:(t + 1) * 256], ckvT[:, t * 128:(t + 1) * 128], v,
                                     start=True, stop=True)
                        ins.then_inc(acc_full, 1)
                    elif name in ("rot01", "rot23"):
                        acc = wait_acc_free(pe, name, l)
                        carry(pe)
                        wait_drained(pe, "uq" + name[3:], l)
                        carry(pe)
                        h = int(name[3])
                        mm(acc[64:96, :], C["rot"][64:96, :], mqT[64:96, h:h + 2, :], start=True, stop=True) \
                            .then_inc(acc_full, 1)
                    elif name == "rotk":
                        acc = wait_acc_free(pe, name, l)
                        carry(pe)
                        wait_drained(pe, "ckv", l)
                        carry(pe)
                        mm(acc[64:96, 0:256], C["rot"][64:96, :], krr[64:96, :], start=True, stop=True) \
                            .then_inc(acc_full, 1)
                    elif name == "dstats":
                        acc = wait_acc_free(pe, name, l)
                        pe.wait_ge(y_squared, l + 1)
                        mm(acc[:], C["blk"], tmpA[:], start=True, stop=True).then_inc(acc_full, 1)
                    elif name[:2] == "wb":
                        b, q = name[2], int(name[4])
                        acc = wait_acc_free(pe, name, l)
                        n = BRANCH_ORDER.index(b)
                        if q == 0:
                            pe.wait_ge(y_split, 4 * l + n + 1)
                        for k in range(2):
                            u, before, total = half_place(name[:3], k)
                            if q == 0:
                                pe.wait_ge(split_full[u], l * total + before + 1)
                            for j in range(2):
                                m = 2 * q + j
                                ins = three(acc[:, j * 256:(j + 1) * 256], shi[:, u, m * 128:(m + 1) * 128],
                                            slo[:, u, m * 128:(m + 1) * 128], yh[:, n, k * 256:(k + 1) * 256],
                                            yl[:, n, k * 256:(k + 1) * 256], k == 0 and j == 0, k == 1)
                            if q == 3:
                                ins.then_inc(split_used[u], 1)
                        if q < 3:
                            ins.then_inc(acc_full, 1)
                    else:
                        chunk_product(name, name, PARTS.get(name, two))

                def other_rows(ins):
                    rows_no[0] += 1
                    ins.then_inc(pe_order, 1)
                    pe.wait_ge(pe_order, rows_no[0])

                rows_no = [0]

                def index_scores(i):
                    b, before, total = sc_place(f"I{i}")
                    pe.wait_ge(sc_free[b], l * total + before + BEGUN)
                    if i == 0:
                        wait_drained(pe, "iq", l)
                        wait_drained(pe, "ik", l)
                    qb, keys, heads = (0, 128, (0, 2, 1, 3)) if i == 0 else (1, 256, (i - 1, i + 1))
                    for n, h in enumerate(heads):
                        if n and h % 2 != heads[n - 1] % 2:
                            other_rows(ins)
                        r = slice(64 * (h % 2), 64 * (h % 2) + 64)
                        ins = mm(ps[SCB + b][:, n * keys:(n + 1) * keys], iqT[r, h // 2, qb * 128:qb * 128 + 128],
                                 ikT[r, 0:keys], start=True, stop=True)
                    ins.then_inc(sc_full, 1)

                def scores(t):
                    br, i = ATT[t]
                    b, before, total = sc_place(f"{br}{i}")
                    sc = ps[SCB + b]
                    pe.wait_ge(sc_free[b], l * total + before + BEGUN)
                    if br == "C":
                        if i == 0:
                            wait_drained(pe, "sq", l)
                            wait_drained(pe, "sk", l)
                        r = slice(64 * (i % 2), 64 * (i % 2) + 64)
                        mm(sc[:, 0:256], skT[r, i // 2, 0:128], sqT[r, i // 2, :], start=True, stop=False,
                           skip_group_check=True)
                        mm(sc[:, 256:384], skT[r, i // 2, 128:256], sqT[r, i // 2, 128:256], start=False, stop=False,
                           skip_group_check=True).then_inc(sc_full, 1)
                        return
                    q0, keys, maps = head_cols(ATT[t])
                    if i == 0:
                        wait_all_drained(pe, {"B": ("uk01", "uk23"), "D": ("dq", "dk"), "A": ("aq", "ak")}[br], l)
                        if br == "B":
                            pe.wait_ge(q_roped, 2 * (l + 1))
                            pe.wait_ge(k_roped, l + 1)
                    for n, m in enumerate(maps):
                        if n and (br == "D" or br == "A" and m % 2 != maps[n - 1] % 2):
                            other_rows(ins)
                        if br == "B":
                            q, k = mqT[:, m, q0:q0 + 128], mkT[:, m, 0:keys]
                        elif br == "D":
                            r = slice(32 * (m % 4), 32 * (m % 4) + 32)
                            q, k = dqT[r, m // 4, q0:q0 + 128], dkT[r, m // 4, 0:keys]
                        else:
                            r = slice(64 * (m % 2), 64 * (m % 2) + 64)
                            q, k = aqT[r, m // 2, q0:q0 + 128], akT[r, 0:keys]
                        ins = mm(sc[:, n * keys:(n + 1) * keys], q, k, start=True, stop=True)
                    ins.then_inc(sc_full, 1)

                def second(t):
                    br, i = ATT[t]
                    if br == "C":
                        b, _, _ = sc_place(f"C{i}")
                        sc, sp_ = ps[SCB + b], prob[:, t % 2, :]
                        pe.wait_ge(z_masked, 4 * l + i + 1)
                        mm(sc[:, 0:256], C["ntri"], sp_[:, 0:256], start=False, stop=False, skip_group_check=True)
                        mm(sc[:, 128:256], C["nones"], sp_[:, 256:384], start=False, stop=False, skip_group_check=True)
                        mm(sc[:, 256:384], C["ntri"], sp_[:, 256:384], start=False, stop=True,
                           skip_group_check=True).then_inc(z_summed, 1)
                        return
                    v = t - 4
                    pe.wait_ge(exp_ready, l * NSM + v + 1)
                    pe.wait_ge(diag_ready, l * NSM + v + 1)
                    if v >= 2:
                        pe.wait_ge(turned_kept, l * NSM + v - 1)
                    q0, keys, maps = head_cols(ATT[t])
                    tp = ps[TPB + v % 2]
                    kb = keys // 128
                    per = 2 if br == "D" else 1
                    for n, m in enumerate(maps):
                        for j in range(kb):
                            o = (n // per) * keys + j * 128
                            ins = mm(tp[:, o:o + 128], prob[:, t % 2, n * keys + j * 128:n * keys + (j + 1) * 128],
                                     diag[:, t % 2, n * 128:(n + 1) * 128], start=(n == 0 and j == 0),
                                     stop=(n % per == per - 1), skip_group_check=True)
                    ins.then_inc(turned, 1)

                def values(t):
                    br, i = ATT[t]
                    y = ps[YB + BRANCH_ORDER.index(br) % 2]
                    if i == 0 and BRANCH_ORDER.index(br) >= 2:
                        pe.wait_ge(y_split, 4 * l + BRANCH_ORDER.index(br) - 1)
                    p_ = pT[:, t % 2, :]
                    if br == "C":
                        if i == 0:
                            wait_drained(pe, "sv", l)
                        pe.wait_ge(w_masked, 4 * l + i + 1)
                        yo = y[64 * (i % 2):64 * (i % 2) + 64, (i // 2) * 256:(i // 2) * 256 + 256]
                        mm(yo, svt[:, 0, i * 64:(i + 1) * 64], p_[:, 0:256], start=True, stop=True,
                           skip_group_check=True)
                        mm(yo[:, 128:256], svt[:, 1, i * 64:(i + 1) * 64], p_[:, 256:384], start=False, stop=True,
                           skip_group_check=True).then_inc(values_done, 1)
                        return
                    q0, keys, maps = head_cols(ATT[t])
                    pe.wait_ge(turned_kept, l * NSM + t - 4 + 1)
                    if i == 0:
                        wait_drained(pe, {"B": "uv", "D": "dv", "A": "ak"}[br], l)
                    heads = [m // 2 for m in maps if m % 2 == 0] if br == "D" else list(maps)
                    for n, h in enumerate(heads):
                        yo = y[64 * (h % 2):64 * (h % 2) + 64, (h // 2) * 256 + q0:(h // 2) * 256 + q0 + 128]
                        for j in range(keys // 128):
                            v = {"B": mvt, "D": dvt}[br][:, j, h * 64:(h + 1) * 64] if br != "A" else avt[:, j, :]
                            ins = mm(yo, v, p_[:, n * keys + j * 128:n * keys + (j + 1) * 128], start=j == 0,
                                     stop=j == keys // 128 - 1, skip_group_check=True)
                    ins.then_inc(values_done, 1)

                for name in PRE:
                    if name[0] == "@":
                        index_scores(int(name[2]))
                    else:
                        unit(name)
                for t in range(NATT + 2):
                    if t < NATT:
                        scores(t)
                    for name in FILL[t]:
                        unit(name)
                    if 1 <= t <= NATT:
                        second(t - 1)
                    if t >= 2:
                        values(t - 2)
                for name in POST:
                    unit(name)
                    if name[:2] == "wo" and name != "wo0":
                        stats(ps[YB], 1, int(name[2]) - 1)

                with pe.If(l < 1):
                    for g in range(FG + 1):
                        if g < FG:
                            for n in range(2):
                                c = f"w{1 + 2 * n}_{g}"
                                b = (2 * g + n) % 4
                                if g >= 2:
                                    pe.wait_ge(up_free[b], g // 2)
                                for half in range(2):
                                    u, before, _ = half_place(c, half)
                                    pe.wait_ge(split_full[u], before + 1)
                                    for j in range(2):
                                        for kk in range(4):
                                            k = 4 * half + kk
                                            if g == 0 and n == 0 and j == 0 and k % 2 == 0:
                                                pe.wait_ge(h_split, 4 + k // 2 + 1)
                                            o = kk * COLS + j * 128
                                            ins = three(ps[b][:, j * 256:(j + 1) * 256], shi[:, u, o:o + 128],
                                                        slo[:, u, o:o + 128], hh[:, k, :], hl[:, k, :],
                                                        k == 0 and j == 0, k == KB - 1)
                                    ins.then_inc(split_used[u], 1)
                        if g >= 1:
                            pe.wait_ge(glu_split, g)
                            for j in range(2):
                                u, before, _ = half_place(f"w2_{g - 1}", j)
                                pe.wait_ge(split_full[u], before + 1)
                                for m in range(KB):
                                    ins = three(ps[4 + m // 2][:, (m % 2) * 256:(m % 2) * 256 + 256],
                                                shi[:, u, m * 128:(m + 1) * 128], slo[:, u, m * 128:(m + 1) * 128],
                                                gh[:, (g - 1) % 2, j * 256:(j + 1) * 256],
                                                gl[:, (g - 1) % 2, j * 256:(j + 1) * 256],
                                                g == 1 and j == 0 and m % 2 == 0, g == FG and j == 1)
                                    if g == FG and j == 1 and m in (1, 3, 5):
                                        ins.then_inc(down_done, 1)
                                ins.then_inc(split_used[u], 1)

                pe.sem_clear(pe_order)

            pe.wait_ge(small_w_loaded, 96)
            for k in range(KB):
                if k % 2 == 0:
                    pe.wait_ge(h_ready, 8 * L - 4 + k // 2 + 1)
                for t in range(TB):
                    mm(ps[4 + t][:, 0:8], htmp[:, k, t * 128:(t + 1) * 128], router_w[:, k, :],
                       start=k == 0, stop=False)
            for t in range(TB):
                ins = mm(ps[4 + t][:, 0:8], C["ones"][0:1, :], router_b[:], start=False, stop=True)
            ins.then_inc(logits_done, 1)
            pe.wait_ge(mixer_over, 3)
            for t in range(TB):
                for b in range(2):
                    for j in range(4):
                        k = 4 * b + j
                        ins = pe.transpose(ps[2 * t + b][:, j * 128:(j + 1) * 128],
                                           htmp[:, k, t * 128:(t + 1) * 128], C["ident"])
                    ins.then_inc(htok_turned, 1)
            pe.wait_ge(mask_ready, 1)
            mask = rt[:, 0:16].rearrange("p (t e) -> p t e", t=TB)
            mm(ps[7][:, 0:8], C["strict"], mask[:, 0, :], start=True, stop=True)
            mm(ps[7][:, 8:16], C["strict"], mask[:, 1, :], start=True, stop=False)
            mm(ps[7][:, 8:16], C["ones"], mask[:, 0, :], start=False, stop=True)
            mm(ps[7][:, 16:24], C["ones"], mask[:, 0, :], start=True, stop=False)
            mm(ps[7][:, 16:24], C["ones"], mask[:, 1, :], start=False, stop=True).then_inc(rank_done, 1)
            pe.wait_ge(npass_ready, 1)
            npass = pe.value_load(npass_i[0:1, 0:1], min_val=1, max_val=2)
            with pe.Fori(0, npass) as p:
                def gather(nth, e):
                    for b in range(2):
                        if b == 0:
                            pe.wait_ge(x_added, nth * 4 + BEGUN)
                        for j in range(4):
                            k = 4 * b + j
                            for t in range(TB):
                                ins = mm(ps[6 + b][:, j * 128:(j + 1) * 128], htok[:, t, k * 128:(k + 1) * 128],
                                         sel[:, t, e, :], start=t == 0, stop=t == TB - 1)
                        ins.then_inc(gathered, 1)

                def scatter(nth, after):
                    pe.wait_ge(y_kept, 2 * nth + 2 + BEGUN)
                    pe.wait_ge(selT_ready, 4 * (p + 1))
                    pe.wait_ge(xg_ready, 2 * (nth + p + 2))
                    for q in range(4):
                        if q >= 2:
                            pe.wait_ge(x_added, nth * 4 + q - 1 + BEGUN)
                        for j in range(2):
                            m = 2 * q + j
                            ins = mm(ps[6 + q % 2][:, j * 256:(j + 1) * 256], ysb[:, m * 128:(m + 1) * 128],
                                     selT[:, after, :], start=True, stop=True)
                        ins.then_inc(scattered, 1)

                pe.wait_ge(htok_ready, 4)
                pe.wait_ge(sel_ready, p + 1)
                gather(p * 8, 0)
                pe.wait_ge(selw_ready, p + 1)
                for b in range(4):
                    for j in range(4):
                        e_, t_ = 2 * b + j // 2, j % 2
                        ins = pe.transpose(ps[b][:, j * 128:(j + 1) * 128],
                                           htmp[:].rearrange("p k s -> p (k s)")
                                           [:, (t_ * 8 + e_) * 128:(t_ * 8 + e_ + 1) * 128], C["ident"])
                    ins.then_inc(selw_turned, 1)
                pe.wait_ge(selT_ready, 4 * (p + 1))
                carry(pe)
                with pe.Fori(0, EXPERTS) as e:
                    it = p * EXPERTS + e
                    N3 = NEU // 3

                    def up(g, part):
                        u, before = e_unit(g, part)
                        if part == 0:
                            if g == 0:
                                pe.wait_ge(xg_ready, 2 * (it + p + 1))
                            pe.wait_ge(e_glu, (it * EG + g - 1 if g >= 2 else it * EG) + BEGUN)
                        pe.wait_ge(e_full[u], it * N3 + before + 1)
                        wh = ehi[:, u, :].rearrange("p (w k n) -> p w k n", w=2, k=4)
                        wl = elo[:, u, :].rearrange("p (w k n) -> p w k n", w=2, k=4)
                        for kk in range(4):
                            k = 4 * part + kk
                            ks = slice(k * 128, (k + 1) * 128)
                            ins = three(ps[g % 2][:], wh[:, :, kk, :], wl[:, :, kk, :], xgh[:, ks], xgl[:, ks],
                                        k == 0, k == KB - 1, False)
                        ins.then_inc(e_used[u], 1)

                    def turn(g):
                        pe.wait_ge(e_glu, it * EG + g + 1 + BEGUN)
                        pe.wait_ge(e_gtl, (it * EG + g - 1 if g >= 2 else it * EG) + BEGUN)
                        for j in range(2):
                            ins = pe.transpose(ps[2 + g % 2][:, j * 128:(j + 1) * 128],
                                               glu[:, g % 2, j * 128:(j + 1) * 128], C["ident"])
                        ins.then_inc(e_turned, 1)

                    def down(g):
                        u, before = e_unit(g, 2)
                        pe.wait_ge(e_gtl, it * EG + g + 1 + BEGUN)
                        pe.wait_ge(e_full[u], it * N3 + before + 1)
                        if g == 0:
                            pe.wait_ge(y_kept, 2 * it + BEGUN)
                        for j in range(2):
                            js = slice(j * 128, (j + 1) * 128)
                            for n in range(2):
                                o = j * 1024 + n * 512
                                ins = three(ps[4 + n][:], ehi[:, u, o:o + 512], elo[:, u, o:o + 512],
                                            gth[:, g % 2, js], gtl[:, g % 2, js], g == 0 and j == 0,
                                            g == EG - 1 and j == 1, False)
                        ins.then_inc(e_used[u], 1)

                    for g in range(EG):
                        up(g, 0)
                        if g >= 1:
                            turn(g - 1)
                        up(g, 1)
                        if g == 0:
                            with pe.If(e > 0):
                                scatter(it - 1, e)
                        if g == EG - 1:
                            gather(it, e + 1)
                        if g >= 1:
                            down(g - 1)
                    turn(EG - 1)
                    down(EG - 1)
                scatter(p * EXPERTS + EXPERTS - 1, EXPERTS)

            for k in range(KB):
                if k % 2 == 0:
                    pe.wait_ge(squares, 8 * L + k // 2 + 1)
                ins = mm(ps[0][:, 0:256], C["ones"], htmp[:, k, :], start=k == 0, stop=k == KB - 1)
            ins.then_inc(acc_full, 1)
            for b in range(2):
                for j in range(4):
                    k = 4 * b + j
                    pe.wait_ge(f_scaled, k + 1)
                    for t in range(TB):
                        ins = pe.transpose(ps[1 + 2 * b + t][:, j * 128:(j + 1) * 128],
                                           htmp[:, k, t * 128:(t + 1) * 128], C["ident"])
                ins.then_inc(f_turned, 1)

        @block.scalar
        def _(act):
            A = act.activation
            step_no = [0]

            def step(ins):
                step_no[0] += 1
                ins.then_inc(act_order, 1)
                act.wait_ge(act_order, step_no[0])

            for b in (0, 2):
                act.wait_ge(x_turned, b + 1)
                act.copy(xT[:, 2 * b:2 * b + 2, :].rearrange("p k s -> p (k s)"), ps[b][:]).then_inc(x_kept, 1)
            act.wait_ge(rope_arg, 1)
            A(sinT[64:96, :], sinT[64:96, :], ACT.Sin).then_inc(rope_ready, 1)
            A(cosT[64:96, :], cosT[64:96, :], ACT.Sin, bias=C["half_pi"][64:96, :], scale=-1.0).then_inc(rope_ready, 1)
            act.wait_ge(x_kept, 4)

            with act.Fori(0, L) as l:
                split_to = [0]

                def advance(c):
                    want = min(SPLITS.index(c) + 2, NMIX)
                    while split_to[0] < want:
                        split_high(act, SPLITS[split_to[0]], l)
                        split_to[0] += 1

                def squares_of_x(i):
                    A(htmp[:, 2 * i:2 * i + 2, :], xT[:, 2 * i:2 * i + 2, :], ACT.Square).then_inc(squares, 1)

                def std(unit):
                    wait_unit(act, unit, l)
                    acc = ps[YB] if unit == "stats2" else ps[bank_of(unit)[0]]
                    read_out(A(rstd[:], acc[:, 0:256], ACT.Sqrt, bias=C["eps"], scale=1.0 / D), unit)

                def high_of_h(norm):
                    for i in range(4):
                        ks = slice(2 * i, 2 * i + 2)
                        act.wait_ge(h_ready, 8 * l + 4 * norm + i + 1)
                        act.copy(hh[:, ks, :], htmp[:, ks, :]).then_inc(h_high, 1)

                def drain(name):
                    acc = ps[bank_of(name)[0]]
                    wait_unit(act, name, l)
                    if name == "iq":
                        read_out(A(iqT[:].rearrange("p k s -> p (k s)"), acc[:], ACT.Copy, scale=64 ** -0.5), name)
                    elif name == "ik":
                        act.copy(ikT[:], acc[:, 0:256])
                        read_out(A(iw[:].rearrange("p t h -> p (t h)"), acc[:, 256:264], ACT.Copy,
                                   scale=HEADS ** -0.5), name)
                    elif name == "cq":
                        step(act.copy(cqT[:].rearrange("p k s -> p (k s)"), acc[:]))
                        read_out(A(tmpA[:], acc[:], ACT.Square), name)
                    elif name == "ckv":
                        act.copy(ckvT[:], acc[:, 0:256])
                        A(krT, acc[:, 0:256], ACT.Square).then_inc(lat_squares, 1)
                        read_out(act.copy(krr[64:96, :], acc[64:96, 256:512]), name)
                    elif name in ("sq", "aq"):
                        read_out(A((sqT if name == "sq" else aqT)[:].rearrange("p k s -> p (k s)"), acc[:],
                                   ACT.Copy, scale=64 ** -0.5), name)
                    elif name == "dq":
                        read_out(A(dqT[:].rearrange("p k s -> p (k s)"), acc[:], ACT.Copy, scale=32 ** -0.5), name)
                    elif name in ("sk", "dk", "sv", "dv", "uv"):
                        dst = {"sk": skT, "dk": dkT, "sv": svt, "dv": dvt, "uv": mvt}[name]
                        read_out(act.copy(dst[:].rearrange("p k s -> p (k s)"), acc[:]), name)
                    elif name == "ak":
                        act.copy(akT[:], acc[:, 0:256])
                        read_out(act.copy(avt[:].rearrange("p t d -> p (t d)"), acc[:, 256:384]), name)
                    elif name == "mla_stats":
                        A(pT[:, 0, 0:256], acc[:, 0:256], ACT.Sqrt, bias=C["eps"], scale=1.0 / 256)
                        read_out(A(pT[:, 0, 256:512], acc[:, 256:512], ACT.Sqrt, bias=C["eps"], scale=1.0 / 128), name)
                    elif name[:2] == "uq":
                        h = int(name[2])
                        read_out(A(mqT[:, h:h + 2, :].rearrange("p h s -> p (h s)"), acc[0:96, :], ACT.Copy,
                                   scale=96 ** -0.5), name)
                    elif name[:2] == "uk":
                        h = int(name[2])
                        read_out(act.copy(mkT[0:64, h:h + 2, :].rearrange("p h s -> p (h s)"), acc[0:64, :]), name)
                    elif name[:4] == "gate":
                        i = int(name[4:])
                        read_out(A(gates[:, 2 * i:2 * i + 2, :].rearrange("p k s -> p (k s)"), acc[:], ACT.Tanh,
                                   scale=0.5), name)
                    elif name == "dstats":
                        read_out(A(tmpA[:], acc[:], ACT.Sqrt, bias=C["eps"], scale=1.0 / 64), name)

                ACT_DRAINS = ("iq", "ik", "cq", "ckv", "sq", "sk", "sv", "mla_stats", "uq01", "uq23", "uk01", "uk23",
                              "uv", "dq", "dk", "dv", "aq", "ak", "dstats")

                def unit(name):
                    for c in chunks_of(name):
                        advance(c)
                    if name in ACT_DRAINS or name[:4] == "gate":
                        drain(name)

                def relu(i):
                    n = f"I{i}"
                    b, _, _ = sc_place(n)
                    if i == 2:
                        act.wait_ge(relu_used, 3 * l + 1)
                    wait_scores(act, n, l)
                    scores_read(A(prob[:, i % 2, :], ps[SCB + b][:], ACT.Relu), n)

                def stage1(t):
                    br, i = ATT[t]
                    pr = prob[:, t % 2, :]
                    if br == "C":
                        if i < 2:
                            act.wait_ge(relu_used, 3 * (l + 1))
                        else:
                            act.wait_ge(z_summed, 4 * l + i - 1)
                        wait_scores(act, f"C{i}", l)
                        step(A(pr[:, 0:384], ps[SCB + sc_place(f"C{i}")[0]][:, 0:384], ACT.Abs))
                        step(A(pr[:, 0:384], pr[:, 0:384], ACT.Exp, scale=-1.0))
                        A(pr[:, 0:384], pr[:, 0:384], ACT.Ln, bias=1.0).then_inc(z_log, 1)
                        return
                    v = t - 4
                    _, keys, maps = head_cols(ATT[t])
                    act.wait_ge(max_ready, l * NSM + v + 1)
                    for n in range(len(maps)):
                        ins = A(pr[:, n * keys:(n + 1) * keys], pr[:, n * keys:(n + 1) * keys], ACT.Exp,
                                bias=small[:, 8 + 4 * (t % 2) + n:9 + 4 * (t % 2) + n],
                                accum_out=small[:, 16 + 4 * (t % 2) + n:17 + 4 * (t % 2) + n])
                    ins.then_inc(exp_ready, 1)

                def stage2(t):
                    br, i = ATT[t]
                    if t >= 2:
                        act.wait_ge(values_done, l * NATT + t - 1)
                    if br == "C":
                        n = f"C{i}"
                        b, _, _ = sc_place(n)
                        if i == 0:
                            act.wait_ge(lat_normed, l + 1)
                        act.wait_ge(z_summed, 4 * l + i + 1)
                        scores_read(A(pT[:, t % 2, 0:384], ps[SCB + b][:, 0:384], ACT.Exp), n)
                        return
                    v = t - 4
                    act.wait_ge(turned, l * NSM + v + 1)
                    _, keys, maps = head_cols(ATT[t])
                    w = 256 if br == "D" else 512
                    act.copy(pT[:, t % 2, 0:w], ps[TPB + v % 2][:, 0:w]).then_inc(turned_kept, 1)

                def branch_out(br):
                    n = BRANCH_ORDER.index(br)
                    y = ps[YB + n % 2]
                    if br == "D":
                        act.wait_ge(y_float, l + 1)
                        act.copy(yh[:, n, :], tmpA[:]).then_inc(y_high, 1)
                    else:
                        last = max(t for t in range(NATT) if ATT[t][0] == br)
                        act.wait_ge(values_done, l * NATT + last + 1)
                        act.copy(yh[:, n, :], y[:]).then_inc(y_high, 1)

                with act.If(l < 1):
                    act.wait_ge(params_ready, 1)
                    A(cond[:], pv[:, ROW["c"]:ROW["c"] + KB], ACT.Silu).then_inc(cond_ready, 1)
                for i in range(4):
                    act.wait_ge(x_fed, 4 * l + i + 1)
                    squares_of_x(i)
                std("stats1")
                split_high(act, SPLITS[0], l)
                split_to[0] = 1
                wait_unit(act, "lam", l)
                read_out(A(small[:, 2:4], ps[bank_of("lam")[0]][:, 0:2], ACT.Exp), "lam")
                high_of_h(0)
                for name in PRE[PRE.index("ada_a") + 1:]:
                    if name[0] == "@":
                        relu(int(name[2]))
                    else:
                        unit(name)
                for t in range(NATT + 2):
                    if t == NATT + 1:
                        branch_out("D")
                    if FILL[t] and chunks_of(FILL[t][0]):
                        advance(FILL[t][0])
                    if t < NATT:
                        stage1(t)
                    for name in FILL[t]:
                        unit(name)
                    if 1 <= t <= NATT:
                        stage2(t - 1)
                    if t >= 3 and ATT[t - 3][0] != (ATT + [("", 0)])[t - 2][0] and ATT[t - 3][0] in "CB":
                        branch_out(ATT[t - 3][0])
                    if t == NATT - 1:
                        act.wait_ge(values_done, l * NATT + t - 2)
                        A(tmpA[:], ps[YB + 0][:], ACT.Square).then_inc(y_squared, 1)
                branch_out("A")
                for name in POST:
                    unit(name)
                    if name[:3] == "wbA":
                        q = int(name[4])
                        act.wait_ge(merged, 4 * l + q + 1)
                        act.copy(hh[:, 2 * q:2 * q + 2, :], htmp[:, 2 * q:2 * q + 2, :]).then_inc(m_high, 1)
                    if name[:2] == "wo":
                        if name == "wo3":
                            with act.If(l < 1):
                                split_high(act, SPLITS[NMIX], 0)
                            A(small[:, 7:8], C["eps"], ACT.Sqrt)
                        wait_drained(act, name, l)
                        squares_of_x(int(name[2]))
                std("stats2")
                with act.If(l < 1):
                    high_of_h(1)
                    to = [NMIX + 1]

                    def ahead(c):
                        while to[0] < min(SPLITS.index(c) + 2, len(SPLITS)):
                            split_high(act, SPLITS[to[0]], 0)
                            to[0] += 1

                    for g in range(FG + 1):
                        if g < FG:
                            ahead(f"w1_{g}")
                            ahead(f"w3_{g}")
                            u, before, _ = half_place(f"w1_{g}", 1)
                            act.wait_ge(split_used[u], before + 1 + BEGUN)
                            b = (2 * g) % 4
                            A(prob[:, g % 2, :], ps[b][:], ACT.Silu).then_inc(up_free[b], 1)
                        if g >= 1:
                            ahead(f"w2_{g - 1}")
                        if g < FG:
                            if g >= 2:
                                u, before, _ = half_place(f"w2_{g - 2}", 1)
                                act.wait_ge(split_used[u], before + 1 + BEGUN)
                            act.wait_ge(up_free[b + 1], g // 2 + 1)
                            act.copy(gh[:, g % 2, :], diag[:, g % 2, :]).then_inc(glu_high, 1)
                act.sem_clear(act_order)
                step_no[0] = 0
            act.nop().then_inc(mixer_over, 1)

            N3 = NEU // 3

            def split(it, j):
                g, part = EUNITS[j]
                r = g % 3
                act.wait_ge(e_used[j % 3], it * N3 + j // 3 + BEGUN)
                if part == 2:
                    act.wait_ge(e2_full[r], 16 * (it * GPS[r] + g // 3 + 1))
                    act.copy(ehi[:, j % 3, :], w2_at(r)).then_inc(e_hi, 1)
                else:
                    act.wait_ge(pair_full[r], 32 * (it * GPS[r] + g // 3 + 1))
                    act.copy(ehi[:, j % 3, :].rearrange("p (w n) -> p w n", w=2),
                             pair_at(r)[:, :, part * 1024:(part + 1) * 1024]).then_inc(e_hi, 1)

            act.wait_ge(mixer_over, 3)
            split(0, 0)
            split(0, 1)
            for n in range(4):
                act.wait_ge(htok_turned, n + 1)
                act.copy(htok[:, n // 2, (n % 2) * 512:(n % 2) * 512 + 512], ps[n][:]).then_inc(htok_ready, 1)
            act.wait_ge(gap_ready, 1)
            A(rt[:, 96:98], rt[:, 98:100], ACT.Exp).then_inc(gapexp_ready, 1)
            act.wait_ge(npass_ready, 1)
            npass = act.value_load(npass_i[0:1, 0:1], min_val=1, max_val=2)
            with act.Fori(0, npass) as p:
                def high_of_tokens(nth):
                    for b in range(2):
                        act.wait_ge(gathered, 2 * nth + b + 1)
                        act.copy(xgh[:, b * 512:(b + 1) * 512], ps[6 + b][:]).then_inc(xg_high, 1)

                high_of_tokens(p * 9)
                for b in range(4):
                    act.wait_ge(selw_turned, 4 * p + b + 1)
                    act.copy(selT[:, 2 * b + 1:2 * b + 3, :].rearrange("p e s -> p (e s)"), ps[b][:]).then_inc(selT_ready, 1)
                with act.If(p > 0):
                    split(p * EXPERTS, 0)
                    split(p * EXPERTS, 1)
                with act.Fori(0, EXPERTS) as e:
                    it = p * EXPERTS + e
                    for j, (g, part) in enumerate(EUNITS):
                        if j + 2 < NEU:
                            split(it, j + 2)
                        if part == 1:
                            u, before = e_unit(g, 1)
                            act.wait_ge(e_used[u], it * N3 + before + 1 + BEGUN)
                            act.wait_ge(e_glu, (it * EG + g - 1 if g >= 2 else it * EG) + BEGUN)
                            A(sil[:, g % 2, :], ps[g % 2][:, 0:256], ACT.Silu).then_inc(e_silu, 1)
                        if g >= 1 and part == 0 or j == NEU - 1:
                            h = g - 1 if part == 0 else g
                            act.wait_ge(e_turned, it * EG + h + 1 + BEGUN)
                            if h >= 2:
                                u, before = e_unit(h - 2, 2)
                                act.wait_ge(e_used[u], it * N3 + before + 1 + BEGUN)
                            act.copy(gth[:, h % 2, :], ps[2 + h % 2][:, 0:256]).then_inc(e_gth, 1)
                        if part == 1 and g == EG - 1:
                            high_of_tokens(it + p + 1)
                    with act.If(e < EXPERTS - 1):
                        split(it + 1, 0)
                        split(it + 1, 1)
                    u, before = e_unit(EG - 1, 2)
                    act.wait_ge(e_used[u], it * N3 + before + 1 + BEGUN)
                    act.wait_ge(scattered, 4 * it + BEGUN)
                    act.copy(ysb[:, 0:512], ps[4][:]).then_inc(y_kept, 1)

            A(rt[:, 98:99], C["eps"], ACT.Sqrt)
            for i in range(4):
                act.wait_ge(x_added, npass * (4 * EXPERTS) - 3 + i + BEGUN)
                ks = slice(2 * i, 2 * i + 2)
                A(htmp[:, ks, :], xT[:, ks, :], ACT.Square).then_inc(squares, 1)
            act.wait_ge(acc_full, L * len(SIGNALLED) + 1)
            A(rstd[:], ps[0][:, 0:256], ACT.Sqrt, bias=C["eps"], scale=1.0 / D).then_inc(f_std, 1)
            for b in range(2):
                act.wait_ge(f_turned, b + 1)
                act.copy(htok[:, 0, b * 512:b * 512 + 512], ps[1 + 2 * b][:]).then_inc(f_kept[0], 1)

        @block.vector
        def _(dve):
            step_no = [0]

            def step(ins):
                step_no[0] += 1
                ins.then_inc(vec_order, 1)
                dve.wait_ge(vec_order, step_no[0])

            TT, TS, STT = dve.tensor_tensor, dve.tensor_scalar, dve.scalar_tensor_tensor
            R = slice(64, 96)
            dve.wait_ge(start_loaded, 48)
            step(dve.tensor_copy(sinT[R, :], cosT[R, :].bitcast(i32)))
            step(TS(sinT[R, :], sinT[R, :], C["inv"][R, :], None, ALU.mult))
            step(TS(tmpA[R, 0:256], sinT[R, :], 1.0 / (2 * math.pi), 12582912.0, ALU.mult, ALU.add))
            step(TS(tmpA[R, 0:256], tmpA[R, 0:256], 12582912.0, None, ALU.subtract))
            c1 = 6.28125
            c2 = math.floor((2 * math.pi - c1) * 2 ** 21) / 2 ** 21
            for c in (c1, c2, 2 * math.pi - c1 - c2):
                step(STT(sinT[R, :], tmpA[R, 0:256], -c, sinT[R, :], ALU.mult, ALU.add))
            step(TS(sinT[R, :], sinT[R, :], -3.1415925, 3.1415925, ALU.max, ALU.min))
            STT(cosT[R, :], sinT[R, :], -1.0, sinT[R, :], ALU.mult, ALU.max).then_inc(rope_arg, 1)
            for b in (1, 3):
                dve.wait_ge(x_turned, b + 1)
                dve.tensor_copy(xT[:, 2 * b:2 * b + 2, :].rearrange("p k s -> p (k s)"), ps[b][:]).then_inc(x_kept, 1)
            dve.wait_ge(x_kept, 4)
            dve.sem_inc(x_fed, 4)
            dve.sem_clear(vec_order)
            step_no[0] = 0

            with dve.Fori(0, L) as l:
                split_to = [0]

                def advance(c):
                    want = min(SPLITS.index(c) + 2, NMIX)
                    while split_to[0] < want:
                        split_low(dve, SPLITS[split_to[0]], l)
                        split_to[0] += 1

                def normed(norm, shift, scale, gain, low, scaled=False):
                    step(STT(hscale[:], adav[:, scale:scale + KB], 1.0, pv[:, gain:gain + KB], ALU.add, ALU.mult))
                    for i in range(5):
                        if i < 4:
                            ks = slice(2 * i, 2 * i + 2)
                            if not scaled:
                                step(TT(htmp[:, ks, :], xT[:, ks, :],
                                        rstd[:].unsqueeze(1).broadcast_to([P, 2, SEQ]), ALU.mult))
                            for m in (2 * i, 2 * i + 1):
                                ins = TS(htmp[:, m, :], htmp[:, m, :], hscale[:, m:m + 1],
                                         adav[:, shift + m:shift + m + 1], ALU.mult, ALU.add)
                            ins.then_inc(h_ready, 1)
                        if low and i >= 1:
                            ks = slice(2 * i - 2, 2 * i)
                            dve.wait_ge(h_high, 8 * l + 4 * norm + i)
                            TT(hl[:, ks, :], htmp[:, ks, :], hh[:, ks, :].bitcast(f32), ALU.subtract).then_inc(h_split, 1)

                def drain(name):
                    acc = ps[bank_of(name)[0]]
                    if name[:4] == "adar":
                        i = 16 + 8 * int(name[4:])
                        wait_unit(dve, name, l)
                        read_out(TT(adav[:, i:i + 8], acc[:, 0:8], pv[:, i:i + 8], ALU.add), name)
                        if name == "adar0":
                            wait_drained(dve, name, l)
                            TS(adav[:, i:i + 8], adav[:, i:i + 8], 0.5, None, ALU.mult)
                    elif name in ("rot01", "rot23"):
                        h = int(name[3])
                        q = mqT[R, h:h + 2, :]
                        cosb = cosT[R, :].unsqueeze(1).broadcast_to([32, 2, SEQ])
                        sinb = sinT[R, :].unsqueeze(1).broadcast_to([32, 2, SEQ])
                        wait_unit(dve, name, l)
                        if name == "rot23":
                            dve.wait_ge(q_roped, 2 * l + 1)
                        read_out(TT(tmpA[R, :].rearrange("p (h s) -> p h s", h=2),
                                    acc[R, :].rearrange("p (h s) -> p h s", h=2), sinb, ALU.mult), name)
                        step(TT(q, q, cosb, ALU.mult))
                        wait_drained(dve, name, l)
                        TT(q, q, tmpA[R, :].rearrange("p (h s) -> p h s", h=2), ALU.add).then_inc(q_roped, 1)
                    elif name == "rotk":
                        wait_unit(dve, name, l)
                        dve.wait_ge(q_roped, 2 * (l + 1))
                        read_out(TT(tmpA[R, 0:256], acc[R, 0:256], sinT[R, :], ALU.mult), name)
                        step(TT(krr[R, :], krr[R, :], cosT[R, :], ALU.mult))
                        wait_drained(dve, name, l)
                        TT(mkT[R, :, :], krr[R, :].unsqueeze(1).broadcast_to([32, HEADS, SEQ]),
                           tmpA[R, 0:256].unsqueeze(1).broadcast_to([32, HEADS, SEQ]), ALU.add).then_inc(k_roped, 1)

                def unit(name):
                    for c in chunks_of(name):
                        advance(c)
                    drain(name)
                    if name[:2] == "wb":
                        gated(name)

                def gated(name):
                    q, n = int(name[4]), BRANCH_ORDER.index(name[2])
                    part = (part0, part1)[q % 2]
                    m = htmp[:, 2 * q:2 * q + 2, :]
                    g = gates[:, 8 * BRANCH_N[name[2]] + 2 * q:8 * BRANCH_N[name[2]] + 2 * q + 2, :]
                    acc = ps[bank_of(name)[0]][:].rearrange("p (m s) -> p m s", m=2)
                    if q == 0:
                        wait_all_drained(dve, GATES[4 * n:4 * n + 4], l)
                        carry(dve)
                    wait_unit(dve, name, l)
                    if n == 0:
                        read_out(STT(m, g, 1.0, acc, ALU.add, ALU.mult), name)
                        return
                    if n == 3 and q >= 2:
                        dve.wait_ge(merged, 4 * l + q - 1)
                    elif n > 1 or q >= 2:
                        dve.wait_ge(part_used, 8 * l + 4 * (n - 1) + q - 1)
                    read_out(STT(part[:], g, 1.0, acc, ALU.add, ALU.mult), name)
                    if n == 3:
                        wait_drained(dve, name, l)
                        dve.wait_ge(part_used, 8 * l + 4 + q + 1)
                        TT(m, m, part[:], ALU.add).then_inc(merged, 1)

                def low_of_merged(q):
                    dve.wait_ge(m_high, 4 * l + q + 1)
                    TT(hl[:, 2 * q:2 * q + 2, :], htmp[:, 2 * q:2 * q + 2, :],
                       hh[:, 2 * q:2 * q + 2, :].bitcast(f32), ALU.subtract).then_inc(m_split, 1)

                def index(i):
                    wait_sc_drained(dve, f"I{i}", l)
                    if i == 2:
                        dve.wait_ge(relu_used, 3 * l + 2)
                    t, keys, heads = (0, 128, (0, 2, 1, 3)) if i == 0 else (1, 256, (i - 1, i + 1))
                    dst = score[:, 0:128] if i == 0 else score[:, 128:384]
                    for n, h in enumerate(heads):
                        before = C["causal"][:, 256 - keys:256] if h == 0 else dst
                        ins = STT(dst, prob[:, i % 2, n * keys:(n + 1) * keys], iw[:, t, h:h + 1], before,
                                  ALU.mult, ALU.add)
                        if n < len(heads) - 1:
                            step(ins)
                    ins.then_inc(relu_used, 1)

                def topk_round(r):
                    if r == 0:
                        dve.wait_ge(relu_used, 3 * (l + 1))
                        carry(dve)
                    for t, cols in enumerate((slice(0, 128), slice(128, 384))):
                        src = (score if r == 0 else work)[:, cols]
                        step(dve.max(small[:, 32 + 8 * t:40 + 8 * t], src))
                        step(dve.match_replace(work[:, cols], small[:, 32 + 8 * t:40 + 8 * t], src, TAKEN))
                    if r == TOPK // 8 - 1:
                        step(TS(work[:], work[:], TAKEN / 2, NEG, ALU.is_gt, ALU.mult))

                def stage1a(t):
                    br, i = ATT[t]
                    if br == "C":
                        return
                    name = f"{br}{i}"
                    sc = ps[SCB + sc_place(name)[0]]
                    pr = prob[:, t % 2, :]
                    wait_scores(dve, name, l)
                    if t >= 2:
                        if ATT[t - 2][0] == "C":
                            dve.wait_ge(z_summed, 4 * l + t - 1)
                        else:
                            dve.wait_ge(turned, l * NSM + t - 2 - 4 + 1)
                    _, keys, maps = head_cols(ATT[t])
                    n = len(maps)
                    p3 = pr.rearrange("p (n k) -> p n k", n=n)
                    s3 = sc[:].rearrange("p (n k) -> p n k", n=n)
                    if br == "B":
                        ins = TT(p3, s3, C["causal"][:, 256 - keys:256].unsqueeze(1).broadcast_to([P, n, keys]), ALU.add)
                    else:
                        dist = C["dist"][:, 256 - keys:256]
                        per = 2 if br == "D" else 1
                        for j in range(0, n, per):
                            head = maps[j] // per
                            slope = 2.0 ** -(2 * head + (2 if br == "D" else 1))
                            ins = STT(p3[:, j:j + per, :], dist.unsqueeze(1).broadcast_to([P, per, keys]), slope,
                                      s3[:, j:j + per, :], ALU.mult, ALU.add)
                    scores_read(ins, name)
                    wait_sc_drained(dve, name, l)
                    if br == "A":
                        bias = work[:, 0:128] if keys == 128 else work[:, 128:384]
                        step(TT(p3, p3, bias.unsqueeze(1).broadcast_to([P, n, keys]), ALU.add))
                    dve.tensor_reduce(small[:, 8 + 4 * (t % 2):8 + 4 * (t % 2) + n], p3, AX.X, ALU.max, negate=True) \
                        .then_inc(max_ready, 1)

                def strictly_causal(buf):
                    diagonal = buf[:, 0:512].rearrange("p (b q) -> p b q", b=2)[:, :, 0:128]
                    return STT(diagonal, diagonal, 3e38, C["strict"].unsqueeze(1).broadcast_to([P, 2, P]),
                               ALU.min, ALU.mult)

                def stage1b(t):
                    br, i = ATT[t]
                    pr = prob[:, t % 2, :]
                    if br == "C":
                        sc = ps[SCB + sc_place(f"C{i}")[0]]
                        dve.wait_ge(z_log, 4 * l + i + 1)
                        step(STT(pr[:, 0:384], sc[:, 0:384], 0.0, pr[:, 0:384], ALU.max, ALU.add))
                        strictly_causal(pr).then_inc(z_masked, 1)
                        return
                    v = t - 4
                    n = len(head_cols(ATT[t])[2])
                    dve.wait_ge(exp_ready, l * NSM + v + 1)
                    rec = small[:, 24 + 4 * (t % 2):24 + 4 * (t % 2) + n]
                    step(dve.reciprocal(rec, small[:, 16 + 4 * (t % 2):16 + 4 * (t % 2) + n]))
                    if br == "D":
                        odd = rec.rearrange("p (a two) -> p a two", two=2)[:, :, 1]
                        step(TS(odd, odd, small[:, 5:6], None, ALU.mult))
                    TT(diag[:, t % 2, 0:n * 128].rearrange("p (n k) -> p n k", n=n),
                       C["ident"].unsqueeze(1).broadcast_to([P, n, 128]), rec.unsqueeze(2).broadcast_to([P, n, 128]),
                       ALU.mult).then_inc(diag_ready, 1)

                def low_of_branch(br):
                    n = BRANCH_ORDER.index(br)
                    dve.wait_ge(y_high, 4 * l + n + 1)
                    y = tmpA[:] if br == "D" else ps[YB + n % 2][:]
                    TT(yl[:, n, :], y, yh[:, n, :].bitcast(f32), ALU.subtract).then_inc(y_split, 1)

                wait_unit(dve, "params", l)
                read_out(dve.tensor_copy(pv[:], ps[bank_of("params")[0]][:, 0:NROW]), "params")
                wait_drained(dve, "params", l)
                TT(small[0:32, 0:2], pv[0:32, ROW["lq1"]:ROW["lq1"] + 4:2], pv[0:32, ROW["lk1"]:ROW["lk1"] + 4:2],
                   ALU.mult).then_inc(lamprod_ready, 1)
                TT(small[:, 6:7], pv[:, ROW["diff"]:ROW["diff"] + 1],
                   pv[:, ROW["one_minus_lam"]:ROW["one_minus_lam"] + 1], ALU.mult).then_inc(params_ready, 1)
                def scaled_x():
                    wait_drained(dve, "stats1", l)
                    step(dve.reciprocal(rstd[:], rstd[:]))
                    for i in range(4):
                        ks = slice(2 * i, 2 * i + 2)
                        step(TT(htmp[:, ks, :], xT[:, ks, :], rstd[:].unsqueeze(1).broadcast_to([P, 2, SEQ]), ALU.mult))

                before_scaled = step_no[0]
                with dve.If(l > 0):
                    scaled_x()
                step_no[0] = before_scaled
                with dve.If(l < 1):
                    dve.wait_ge(cond_ready, 1)
                    added = 0
                    for i in FIRST_DVE:
                        if i == FIRST_DVE[2]:
                            scaled_x()
                        dve.wait_ge(first_full[i], 16)
                        w = first_at(i)
                        for k in range(KB):
                            if k == 0:
                                ins = TS(ada_first[:, i, :], w[:, 0, :], cond[:, 0:1], None, ALU.mult)
                            else:
                                dve.wait_ge(first_order, added)
                                ins = STT(ada_first[:, i, :], w[:, k, :], cond[:, k:k + 1], ada_first[:, i, :],
                                          ALU.mult, ALU.add)
                            if k < KB - 1:
                                ins.then_inc(first_order, 1)
                                added += 1
                        ins.then_inc(first_summed, 1)
                split_low(dve, SPLITS[0], l)
                split_to[0] = 1
                wait_unit(dve, "ada_a", l)
                read_out(TT(adav[:, 0:16], ps[bank_of("ada_a")[0]][:, 0:16], pv[:, 0:16], ALU.add), "ada_a")
                wait_drained(dve, "ada_a", l)
                normed(0, 0, 8, ROW["norm1"], True, True)
                wait_drained(dve, "lam", l)
                step(TT(small[:, 4:5], small[:, 3:4], small[:, 2:3], ALU.subtract))
                step(TT(small[:, 5:6], small[:, 4:5], pv[:, ROW["lam_init"]:ROW["lam_init"] + 1], ALU.subtract))
                advance("iq")
                for name in PRE[PRE.index("ada_a") + 1:]:
                    if name[0] == "@":
                        index(int(name[2]))
                    elif name == "mla_stats":
                        wait_drained(dve, name, l)
                        step(dve.reciprocal(pT[:, 0, :], pT[:, 0, :]))
                        for k in range(2):
                            step(STT(cqT[:, k, :], cqT[:, k, :], pv[:, ROW["qn"] + k:ROW["qn"] + k + 1], pT[:, 0, 0:256],
                                     ALU.mult, ALU.mult))
                        STT(ckvT[:], ckvT[:], pv[:, ROW["kvn"]:ROW["kvn"] + 1], pT[:, 0, 256:512],
                            ALU.mult, ALU.mult).then_inc(lat_normed, 1)
                    else:
                        unit(name)
                for t in range(NATT + 2):
                    if t == NATT + 1:
                        wait_drained(dve, "dstats", l)
                        step(dve.reciprocal(tmpA[:], tmpA[:]))
                        STT(tmpA[:], ps[YB][:], small[:, 6:7], tmpA[:], ALU.mult, ALU.mult).then_inc(y_float, 1)
                        low_of_branch("D")
                    if t < NATT:
                        stage1a(t)
                    if FILL[t] and chunks_of(FILL[t][0]):
                        advance(FILL[t][0])
                    if t < NATT:
                        stage1b(t)
                    for name in FILL[t]:
                        unit(name)
                    if 2 <= t < 2 + TOPK // 8:
                        topk_round(t - 2)
                    if 1 <= t <= 4:
                        wait_sc_drained(dve, f"C{t - 1}", l)
                        strictly_causal(pT[:, (t - 1) % 2, :]).then_inc(w_masked, 1)
                    if t >= 3 and ATT[t - 3][0] != (ATT + [("", 0)])[t - 2][0] and ATT[t - 3][0] in "CB":
                        low_of_branch(ATT[t - 3][0])
                low_of_branch("A")
                for name in POST:
                    unit(name)
                    if name[:3] == "wbA":
                        q = int(name[4])
                        if q >= 1:
                            low_of_merged(q - 1)
                        if q == 3:
                            low_of_merged(3)
                    if name[:2] == "wo":
                        acc = ps[bank_of(name)[0]]
                        i = int(name[2])
                        if name == "wo3":
                            with dve.If(l < 1):
                                split_low(dve, SPLITS[NMIX], 0)
                        wait_unit(dve, name, l)
                        for j in range(2):
                            m = 2 * i + j
                            ins = STT(xT[:, m, :], acc[:, j * 256:(j + 1) * 256], adav[:, 16 + m:17 + m], xT[:, m, :],
                                      ALU.mult, ALU.add)
                        read_out(ins, name)
                wait_drained(dve, "stats2", l)
                step(dve.reciprocal(rstd[:], rstd[:]))
                before_norm = step_no[0]
                with dve.If(l > 0):
                    normed(1, 24, 32, ROW["norm2"], False)
                step_no[0] = before_norm
                with dve.If(l < 1):
                    normed(1, 24, 32, ROW["norm2"], True)
                    to = [NMIX + 1]

                    def ahead(c):
                        while to[0] < min(SPLITS.index(c) + 2, len(SPLITS)):
                            split_low(dve, SPLITS[to[0]], 0)
                            to[0] += 1

                    for g in range(FG + 1):
                        if g < FG:
                            ahead(f"w1_{g}")
                            ahead(f"w3_{g}")
                            b = (2 * g) % 4
                            dve.wait_ge(up_free[b], g // 2 + 1)
                            u, before, _ = half_place(f"w3_{g}", 1)
                            dve.wait_ge(split_used[u], before + 1 + BEGUN)
                            TT(diag[:, g % 2, :], prob[:, g % 2, :], ps[b + 1][:], ALU.mult).then_inc(up_free[b + 1], 1)
                        if g >= 1:
                            ahead(f"w2_{g - 1}")
                        if g < FG:
                            dve.wait_ge(glu_high, g + 1)
                            TT(gl[:, g % 2, :], diag[:, g % 2, :], gh[:, g % 2, :].bitcast(f32), ALU.subtract) \
                                .then_inc(glu_split, 1)
                    for m in range(KB):
                        if m == KB - 2:
                            u, before, _ = half_place(f"w2_{FG - 1}", 1)
                            dve.wait_ge(split_used[u], before + 1 + BEGUN)
                        elif m % 2 == 0:
                            dve.wait_ge(down_done, m // 2 + 1)
                        ins = STT(xT[:, m, :], ps[4 + m // 2][:, (m % 2) * 256:(m % 2) * 256 + 256],
                                  adav[:, 40 + m:41 + m], xT[:, m, :], ALU.mult, ALU.add)
                        if m % 2 == 1:
                            ins.then_inc(x_fed, 1)
                dve.sem_clear(vec_order)
                step_no[0] = 0
            dve.nop().then_inc(mixer_over, 1)

            lg = rt[:, 16:32].rearrange("p (t e) -> p t e", t=TB)
            top = rt[:, 32:48].rearrange("p (t e) -> p t e", t=TB)
            idx = rt[:, 48:64].rearrange("p (t e) -> p t e", t=TB)
            mask = rt[:, 0:16].rearrange("p (t e) -> p t e", t=TB)
            comb = rt[:, 64:80].rearrange("p (t e) -> p t e", t=TB)
            second = rt[:, 80:96].rearrange("p (t e) -> p t e", t=TB)
            gapexp, gap, w1, w2 = (rt[:, c:c + 2] for c in (96, 98, 100, 102))
            slot = rt[:, 104:104 + 18].rearrange("p (t e) -> p t e", t=TB)
            N3 = NEU // 3

            def split(it, j):
                g, part = EUNITS[j]
                r = g % 3
                dve.wait_ge(e_hi, it * NEU + j + 1)
                if part == 2:
                    o, i = elo[:, j % 3, :], w2_at(r)
                    h = ehi[:, j % 3, :].bitcast(f32)
                else:
                    o = elo[:, j % 3, :].rearrange("p (w n) -> p w n", w=2)
                    h = ehi[:, j % 3, :].bitcast(f32).rearrange("p (w n) -> p w n", w=2)
                    i = pair_at(r)[:, :, part * 1024:(part + 1) * 1024]
                TT(o, i, h, ALU.subtract).then_inc(e_full[j % 3], 1)

            dve.wait_ge(mixer_over, 3)
            dve.wait_ge(logits_done, 1)
            dve.tensor_copy(rt[:, 16:24], ps[4][:, 0:8])
            step(dve.tensor_copy(rt[:, 24:32], ps[5][:, 0:8]))
            for t in range(TB):
                step(dve.max(top[:, t, :], lg[:, t, :]))
                step(dve.max_index(rtu[:, t, :], top[:, t, :], lg[:, t, :]))
            step(dve.tensor_copy(rt[:, 48:64], rtu[:].rearrange("p t e -> p (t e)")))
            TT(gap, top[:, :, 1], top[:, :, 0], ALU.subtract).then_inc(gap_ready, 1)
            dve.wait_ge(gapexp_ready, 1)
            step(TS(w1, gapexp, 1.0, None, ALU.add))
            step(dve.reciprocal(w1, w1))
            step(TT(w2, w1, gapexp, ALU.mult))
            for t in range(TB):
                step(TS(mask[:, t, :], C["iota"][:, 0:8], idx[:, t, 0:1], None, ALU.is_equal))
                step(TS(second[:, t, :], C["iota"][:, 0:8], idx[:, t, 1:2], None, ALU.is_equal))
                step(TS(comb[:, t, :], second[:, t, :], w2[:, t:t + 1], None, ALU.mult))
                step(STT(comb[:, t, :], mask[:, t, :], w1[:, t:t + 1], comb[:, t, :], ALU.mult, ALU.add))
            TT(mask, mask, second, ALU.add).then_inc(mask_ready, 1)
            split(0, 0)
            dve.wait_ge(rank_done, 1)
            step(dve.memset(rt[:, 104:122], -1.0))
            step(STT(slot[:, :, 0:8], ps[7][:, 0:16].rearrange("p (t e) -> p t e", t=TB), 1.0, mask, ALU.add, ALU.mult))
            step(TS(slot[:, :, 0:8], slot[:, :, 0:8], 1.0, None, ALU.subtract))
            step(dve.tensor_reduce(rt[:, 124:125], ps[7][:, 16:24], AX.X, ALU.max))
            step(TS(rt[:, 125:126], rt[:, 124:125], 128.5, 1.0, ALU.is_gt, ALU.add))
            dve.tensor_copy(npass_i[:], rt[0:1, 125:126]).then_inc(npass_ready, 1)
            dve.wait_ge(npass_ready, 1)
            npass = dve.value_load(npass_i[0:1, 0:1], min_val=1, max_val=2)
            dve.sem_clear(vec_order)
            step_no[0] = 0
            with dve.Fori(0, npass) as p:
                def select(first, n):
                    for t in range(TB):
                        ins = TT(sel[:, t, first:first + n, :], C["iota"].unsqueeze(1).broadcast_to([P, n, P]),
                                 slot[:, t, first:first + n].unsqueeze(2).broadcast_to([P, n, P]), ALU.is_equal)
                    return ins

                select(0, 1).then_inc(sel_ready, 1)
                step(select(1, EXPERTS))
                dve.wait_ge(sel_ready, p + 1)
                flat = htmp[:].rearrange("p k s -> p (k s)").rearrange("p (t e c) -> p t e c", t=TB, e=EXPERTS)
                for t in range(TB):
                    ins = TT(flat[:, t, :, :], sel[:, t, 0:EXPERTS, :],
                             comb[:, t, :].unsqueeze(2).broadcast_to([P, EXPERTS, P]), ALU.mult)
                    if t == 0:
                        step(ins)
                ins.then_inc(selw_ready, 1)
                step(TS(rt[:, 104:122], rt[:, 104:122], 128.0, None, ALU.subtract))

                def low_of_tokens(nth):
                    for b in range(2):
                        dve.wait_ge(xg_high, 2 * nth + b + 1)
                        TT(xgl[:, b * 512:(b + 1) * 512], ps[6 + b][:],
                           xgh[:, b * 512:(b + 1) * 512].bitcast(f32), ALU.subtract).then_inc(xg_ready, 1)

                low_of_tokens(p * 9)
                def add_output(nth):
                    for q in range(4):
                        dve.wait_ge(scattered, 4 * nth + q + 1 + BEGUN)
                        for j in range(2):
                            m = 2 * q + j
                            ins = STT(xT[:, m, :], ps[6 + q % 2][:, j * 256:(j + 1) * 256], adav[:, 40 + m:41 + m],
                                      xT[:, m, :], ALU.mult, ALU.add)
                        ins.then_inc(x_added, 1)

                with dve.If(p > 0):
                    split(p * EXPERTS, 0)
                split(p * EXPERTS, 1)
                with dve.Fori(0, EXPERTS) as e:
                    it = p * EXPERTS + e
                    for j, (g, part) in enumerate(EUNITS):
                        if j + 2 < NEU:
                            split(it, j + 2)
                        if part == 1:
                            dve.wait_ge(e_silu, it * EG + g + 1)
                            dve.wait_ge(e_turned, (it * EG + g - 1 if g >= 2 else it * EG) + BEGUN)
                            TT(glu[:, g % 2, :], sil[:, g % 2, :], ps[g % 2][:, 256:512], ALU.mult).then_inc(e_glu, 1)
                        if g >= 1 and part == 0 or j == NEU - 1:
                            h = g - 1 if part == 0 else g
                            dve.wait_ge(e_gth, it * EG + h + 1)
                            TT(gtl[:, h % 2, :], ps[2 + h % 2][:, 0:256], gth[:, h % 2, :].bitcast(f32),
                               ALU.subtract).then_inc(e_gtl, 1)
                        if part == 1 and g == 0:
                            with dve.If(e > 0):
                                add_output(it - 1)
                        if part == 1 and g == EG - 1:
                            low_of_tokens(it + p + 1)
                    with dve.If(e < EXPERTS - 1):
                        split(it + 1, 0)
                        split(it + 1, 1)
                    u, before = e_unit(EG - 1, 2)
                    dve.wait_ge(e_used[u], it * N3 + before + 1 + BEGUN)
                    dve.wait_ge(scattered, 4 * it + BEGUN)
                    dve.tensor_copy(ysb[:, 512:1024], ps[5][:]).then_inc(y_kept, 1)
                add_output(p * EXPERTS + EXPERTS - 1)
                dve.sem_clear(vec_order)
                step_no[0] = 0

            dve.wait_ge(f_std, 1)
            step(dve.reciprocal(rstd[:], rstd[:]))
            for m in range(KB):
                STT(htmp[:, m, :], xT[:, m, :], pv[:, ROW["final"] + m:ROW["final"] + m + 1], rstd[:],
                    ALU.mult, ALU.mult).then_inc(f_scaled, 1)

            for b in range(2):
                dve.wait_ge(f_turned, b + 1)
                dve.tensor_copy(htok[:, 1, b * 512:b * 512 + 512], ps[2 + 2 * b][:]).then_inc(f_kept[1], 1)

        @block.gpsimd
        def _(pool):
            step_no = [0]
            for s in (*acc_free, *sc_free, *split_used, *e_used, e_glu, e_gtl, e_turned, y_kept, scattered, x_added):
                pool.sem_inc(s, BEGUN)
            pool.memset(rows[:], 0.0).then_inc(rows_cleared, 1)
            with pool.Fori(0, L) as l:
                def step(ins):
                    step_no[0] += 1
                    ins.then_inc(pool_order, 1)
                    pool.wait_ge(pool_order, step_no[0])

                def load_ada(h, base, of_layer):
                    i, half = ADA_ORDER[h // 2], h % 2
                    if h >= 2:
                        pool.wait_ge(ada_summed, base * ADA_HALVES + h - 1)
                        carry(pool)
                    pool.dma_start(ada_raw[:, h % 2],
                                   ada_w[of_layer, :, 4 * half:4 * half + 4, i * COLS:(i + 1) * COLS]) \
                        .then_inc(ada_full[h % 2], 16)

                def sum_ada(i, half, acc, base):
                    h = ada_place(i, half)
                    w = ada_raw[:, h % 2]
                    pool.wait_ge(ada_full[h % 2], 16 * (base * (ADA_HALVES // 2) + h // 2 + 1))
                    carry(pool)
                    step(pool.tensor_tensor(w, w, cond[:, 4 * half:4 * half + 4].unsqueeze(2)
                                            .broadcast_to([P, 4, COLS]), ALU.mult))
                    step(pool.tensor_tensor(w[:, 0:2, :], w[:, 0:2, :], w[:, 2:4, :], ALU.add))
                    if half == 0:
                        ins = pool.tensor_tensor(acc, w[:, 0, :], w[:, 1, :], ALU.add)
                    else:
                        step(pool.tensor_tensor(w[:, 0, :], w[:, 0, :], w[:, 1, :], ALU.add))
                        pool.wait_ge(ada_summed, base * ADA_HALVES + h)
                        carry(pool)
                        ins = pool.tensor_tensor(acc, acc, w[:, 0, :], ALU.add)
                    ins.then_inc(ada_summed, 1)

                def mixer_ada(i):
                    if i in (8, 16, 20):
                        if i == 8:
                            pool.wait_ge(h_split, 8 * l + 4)
                        elif i >= 16:
                            wait_unit(pool, f"adar{i // 4 - 4}", l)
                        carry(pool)
                    for half in range(2):
                        sum_ada(i, half, ada_sum[:, i % 8, :], l)
                        if ada_place(i, half) + 2 < 32:
                            load_ada(ada_place(i, half) + 2, l, l)

                with pool.If(l > 0):
                    pool.wait_ge(ada_summed, ADA_HALVES)
                load_ada(0, l, l)
                load_ada(1, l, l)
                pool.wait_ge(cond_ready, 1)
                carry(pool)
                for i in range(8, 24):
                    mixer_ada(i)
                for n in range(1, 3):
                    for q in range(4):
                        wait_drained(pool, f"wb{BRANCH_ORDER[n]}_{q}", l)
                        m = htmp[:, 2 * q:2 * q + 2, :]
                        pool.tensor_tensor(m, m, (part0, part1)[q % 2][:], ALU.add).then_inc(part_used, 1)
                with pool.If(l < 1):
                    pool.wait_ge(merged, 4)
                    load_ada(32, 0, 1)
                    load_ada(33, 0, 1)
                    for i in range(8):
                        for half in range(2):
                            sum_ada(i, half, ada_first[:, i, :], 0)
                            if ada_place(i, half) + 2 < ADA_HALVES:
                                load_ada(ada_place(i, half) + 2, 0, 1)
                pool.sem_clear(pool_order)
                step_no[0] = 0
            pool.nop().then_inc(mixer_over, 1)


def table():
    import numpy as np

    t = np.zeros((P, NCONST), np.float32)
    i, j = np.arange(P)[:, None], np.arange(P)[None, :]

    def put(name, v):
        lo, hi = CONST[name]
        t[:, lo:hi] = v

    put("ident", i == j)
    put("ntri", -1.0 * (i >= j))
    put("nones", -1.0)
    put("ones", 1.0)
    put("blk", i // 64 == j // 64)
    put("strict", i < j)
    put("iota", j)
    put("dist", np.concatenate([-(128.0 + i - j), np.where(j <= i, -(i - j), NEG)], 1))
    put("causal", np.concatenate([np.zeros((P, P)), np.where(j <= i, 0.0, NEG)], 1))
    rot = np.zeros((P, 32), np.float32)
    for d in range(16):
        rot[64 + 16 + d, d] = -1.0
        rot[64 + d, 16 + d] = 1.0
    put("rot", rot)
    inv = np.zeros((P, 1), np.float32)
    inv[64:96, 0] = 10000.0 ** (-(np.arange(32) % 16) / 16.0)
    put("inv", inv)
    put("eps", EPS)
    put("half_pi", math.pi / 2)
    lam = [0.8 - 0.6 * math.exp(-0.3 * l) for l in range(L)]
    rows = np.array([[[1.0 - v] * P, [v] * P] for v in lam], np.float32)
    return t, rows


_INS = ["x", "c", "positions", "ada_w", "ada_b", "norm1_g", "norm2_g", "w_in", "mla_q_norm_g", "mla_kv_norm_g",
        "mla_w_uq", "mla_w_ukv", "diff_lq1", "diff_lk1", "diff_lq2", "diff_lk2", "diff_norm_g", "w_branch", "w_out",
        "ffn_w1", "ffn_w3", "ffn_w2", "router_w", "router_b", "moe_w1", "moe_w3", "moe_w2", "final_norm_g"]


def kernel(**inputs):
    import numpy as np
    import concourse.bacc as bacc
    from concourse.bass_utils import run_bass_kernel_spmd

    nc = bacc.Bacc("TRN2", target_bir_lowering=False, num_devices=1)
    arrays = {n: np.ascontiguousarray(inputs[n]) for n in _INS}
    arrays["consts"], arrays["lam_rows"] = table()
    args = {}
    for n, v in arrays.items():
        args[n] = nc.dram_tensor(f"in_{n}", v.shape, mybir.dt.from_np(v.dtype), kind="ExternalInput").ap()
    out = nc.dram_tensor("out_x", (1, SEQ, D), mybir.dt.float32, kind="ExternalOutput").ap()
    trunk(nc, args, out)
    r = run_bass_kernel_spmd(nc, [{f"in_{n}": v for n, v in arrays.items()}], core_ids=[0])
    return r.results[0]["out_x"]
```
